# Optimizing a Trainium2 kernel written in Bass

```python
import math
import jax, jax.numpy as jnp
from jax import lax
import numpy as np

D_MODEL = 1024
BATCH = 1
SEQ = 256
DEPTH = 2

GRID_W = 64
CTX_LEN = 256
Q_BLOCK = 128
ROPE_THETA = 10000.0
NORM_EPS = 1e-6
MLA_HEADS = 8
MLA_Q_LORA = 384
MLA_KV_LORA = 256
MLA_NOPE = 64
MLA_ROPE = 32
MLA_V = 64
MLA_SCALE = (MLA_NOPE + MLA_ROPE) ** -0.5
GQA_HEADS = 8
GQA_KV_HEADS = 2
GQA_GROUP = GQA_HEADS // GQA_KV_HEADS
GQA_HEAD_DIM = 64
GQA_SCALE = GQA_HEAD_DIM ** -0.5
FFN_DENSE = 2816
N_EXPERTS = 8
TOP_K = 2
FFN_EXPERT = 3584
N_DENSE = (DEPTH + 1) // 2
N_MOE = DEPTH // 2
IN_SIZES = (MLA_Q_LORA, MLA_KV_LORA, MLA_ROPE,
            GQA_HEADS * GQA_HEAD_DIM, GQA_KV_HEADS * GQA_HEAD_DIM, GQA_KV_HEADS * GQA_HEAD_DIM,
            D_MODEL, D_MODEL)
D_IN = sum(IN_SIZES)

kernel_name = 'hybrid_mla_gqa_moe_prefix_ctx_trunk'

def rms_norm(x, g):
    xf = x.astype(jnp.float32)
    y = xf * lax.rsqrt(jnp.mean(xf * xf, axis=-1, keepdims=True) + NORM_EPS)
    return (y * g.astype(jnp.float32)).astype(x.dtype)

def modulate(h, shift, scale):
    return h * (1 + scale) + shift

def split_cols(y, sizes):
    offs, s = [], 0
    for n in sizes[:-1]:
        s += n
        offs.append(s)
    return jnp.split(y, offs, axis=-1)

def axial_rope_tables(n_ctx, n_lat, dim):
    half = dim // 2
    inv = ROPE_THETA ** (-(jnp.arange(half // 2, dtype=jnp.float32) * 2.0) / half)
    rows = n_lat // GRID_W
    t = jnp.arange(rows * GRID_W)
    row = (t // GRID_W).astype(jnp.float32)
    col = (t % GRID_W).astype(jnp.float32)
    zeros = jnp.zeros((n_ctx, half // 2), jnp.float32)
    ang_r = jnp.concatenate([zeros, row[:, None] * inv], axis=0)[:, None, :]
    ang_c = jnp.concatenate([zeros, col[:, None] * inv], axis=0)[:, None, :]
    return (jnp.cos(ang_r), jnp.sin(ang_r), jnp.cos(ang_c), jnp.sin(ang_c))

def _rotate(xa, cos, sin):
    x1, x2 = jnp.split(xa, 2, axis=-1)
    cos = cos.astype(xa.dtype)
    sin = sin.astype(xa.dtype)
    return jnp.concatenate([x1 * cos - x2 * sin, x1 * sin + x2 * cos], axis=-1)

def rope_2d(x, tabs):
    cos_r, sin_r, cos_c, sin_c = tabs
    half = x.shape[-1] // 2
    return jnp.concatenate([_rotate(x[..., :half], cos_r, sin_r),
                            _rotate(x[..., half:], cos_c, sin_c)], axis=-1)

def attn_blocks(q, k, v, scale):
    b, s, kh, g, dk = q.shape
    nb = s // Q_BLOCK
    qb = jnp.moveaxis(q.reshape(b, nb, Q_BLOCK, kh, g, dk), 1, 0)

    def one_block(q_blk):
        logits = jnp.einsum('bqhgd,bkhd->bhgqk', q_blk, k,
                            preferred_element_type=jnp.float32) * scale
        p = jax.nn.softmax(logits, axis=-1).astype(v.dtype)
        return jnp.einsum('bhgqk,bkhe->bqhge', p, v)

    out = lax.map(one_block, qb)
    return jnp.moveaxis(out, 0, 1).reshape(b, s, kh * g, v.shape[-1])

def attend(q, k, v, n_ctx, latent_only, scale):
    lat = attn_blocks(q[:, n_ctx:], k, v, scale)
    if latent_only:
        return lat
    ctx_out = attn_blocks(q[:, :n_ctx], k[:, :n_ctx], v[:, :n_ctx], scale)
    return jnp.concatenate([ctx_out, lat], axis=1)

def token_mixer(h, n_ctx, latent_only, w_in, q_norm_g, w_qb, kv_norm_g, w_kvb,
                gqa_q_g, gqa_k_g, w_o_mla, w_o_gqa, w_out, tabs_mla, tabs_gqa):
    b, t, _ = h.shape
    q_c, kv_c, k_pe, q_g, k_g, v_g, gate_mla, gate_gqa = split_cols(h @ w_in, IN_SIZES)

    q = (rms_norm(q_c, q_norm_g) @ w_qb).reshape(b, t, MLA_HEADS, MLA_NOPE + MLA_ROPE)
    q = jnp.concatenate([q[..., :MLA_NOPE], rope_2d(q[..., MLA_NOPE:], tabs_mla)], axis=-1)
    kv = (rms_norm(kv_c, kv_norm_g) @ w_kvb).reshape(b, t, MLA_HEADS, MLA_NOPE + MLA_V)
    k_pe = rope_2d(k_pe[:, :, None, :], tabs_mla)
    k = jnp.concatenate([kv[..., :MLA_NOPE],
                         jnp.broadcast_to(k_pe, (b, t, MLA_HEADS, MLA_ROPE))], axis=-1)
    v = kv[..., MLA_NOPE:]

    qg = rope_2d(rms_norm(q_g.reshape(b, t, GQA_HEADS, GQA_HEAD_DIM), gqa_q_g), tabs_gqa)
    qg = qg.reshape(b, t, GQA_KV_HEADS, GQA_GROUP, GQA_HEAD_DIM)
    kg = rope_2d(rms_norm(k_g.reshape(b, t, GQA_KV_HEADS, GQA_HEAD_DIM), gqa_k_g), tabs_gqa)
    vg = v_g.reshape(b, t, GQA_KV_HEADS, GQA_HEAD_DIM)

    start = n_ctx if latent_only else 0
    t_out = t - start
    o_mla = attend(q[:, :, :, None, :], k, v, n_ctx, latent_only, MLA_SCALE)
    o_mla = o_mla.reshape(b, t_out, MLA_HEADS * MLA_V) @ w_o_mla
    o_gqa = attend(qg, kg, vg, n_ctx, latent_only, GQA_SCALE)
    o_gqa = o_gqa.reshape(b, t_out, GQA_HEADS * GQA_HEAD_DIM) @ w_o_gqa

    merged = (jax.nn.sigmoid(gate_mla[:, start:]) * o_mla
              + jax.nn.sigmoid(gate_gqa[:, start:]) * o_gqa)
    return merged @ w_out

def swiglu(h, w1, w3, w2):
    return (jax.nn.silu(h @ w1) * (h @ w3)) @ w2

def moe_swiglu(h, router, w1, w3, w2):
    logits = (h @ router).astype(jnp.float32)
    top_val, top_idx = lax.top_k(logits, TOP_K)
    top_w = jax.nn.softmax(top_val, axis=-1)
    combine = jnp.sum(jax.nn.one_hot(top_idx, N_EXPERTS, dtype=jnp.float32) * top_w[..., None],
                      axis=-2).astype(h.dtype)
    y = jnp.zeros_like(h)
    for e in range(N_EXPERTS):
        y = y + combine[..., e:e + 1] * swiglu(h, w1[e], w3[e], w2[e])
    return y

def setup_inputs(seed: int = 0) -> dict:
    key = jax.random.key(seed)
    k = jax.random.split(key, 32)
    f32 = jnp.float32

    def w(i, shape, fan_in, s=1.0):
        return jax.random.normal(k[i], shape, f32) * (s * fan_in ** -0.5)

    def gain(i, shape):
        return 1.0 + 0.1 * jax.random.normal(k[i], shape, f32)

    D = D_MODEL
    return {
        'x': jax.random.normal(k[0], (BATCH, SEQ, D), f32),
        'c': jax.random.normal(k[1], (BATCH, D), f32),
        'ctx': jax.random.normal(k[2], (BATCH, CTX_LEN, D), f32),
        'c_ctx': jax.random.normal(k[3], (D,), f32),
        'w_ada': w(4, (DEPTH, D, 6 * D), D, 0.5),
        'b_ada': 0.1 * jax.random.normal(k[5], (DEPTH, 6 * D), f32),
        'norm1_g': gain(6, (DEPTH, D)),
        'norm2_g': gain(7, (DEPTH, D)),
        'w_in': w(8, (DEPTH, D, D_IN), D),
        'mla_q_norm_g': gain(9, (DEPTH, MLA_Q_LORA)),
        'mla_w_qb': w(10, (DEPTH, MLA_Q_LORA, MLA_HEADS * (MLA_NOPE + MLA_ROPE)), MLA_Q_LORA),
        'mla_kv_norm_g': gain(11, (DEPTH, MLA_KV_LORA)),
        'mla_w_kvb': w(12, (DEPTH, MLA_KV_LORA, MLA_HEADS * (MLA_NOPE + MLA_V)), MLA_KV_LORA),
        'gqa_q_norm_g': gain(13, (DEPTH, GQA_HEAD_DIM)),
        'gqa_k_norm_g': gain(14, (DEPTH, GQA_HEAD_DIM)),
        'w_o_mla': w(15, (DEPTH, MLA_HEADS * MLA_V, D), MLA_HEADS * MLA_V),
        'w_o_gqa': w(16, (DEPTH, GQA_HEADS * GQA_HEAD_DIM, D), GQA_HEADS * GQA_HEAD_DIM),
        'w_out': w(17, (DEPTH, D, D), D),
        'dense_w1': w(18, (N_DENSE, D, FFN_DENSE), D),
        'dense_w3': w(19, (N_DENSE, D, FFN_DENSE), D),
        'dense_w2': w(20, (N_DENSE, FFN_DENSE, D), FFN_DENSE),
        'moe_router': w(21, (N_MOE, D, N_EXPERTS), D),
        'moe_w1': w(22, (N_MOE, N_EXPERTS, D, FFN_EXPERT), D),
        'moe_w3': w(23, (N_MOE, N_EXPERTS, D, FFN_EXPERT), D),
        'moe_w2': w(24, (N_MOE, N_EXPERTS, FFN_EXPERT, D), FFN_EXPERT),
        'final_norm_g': gain(25, (D,)),
    }

def reference(x, c, ctx, c_ctx, w_ada, b_ada, norm1_g, norm2_g, w_in,
              mla_q_norm_g, mla_w_qb, mla_kv_norm_g, mla_w_kvb,
              gqa_q_norm_g, gqa_k_norm_g, w_o_mla, w_o_gqa, w_out,
              dense_w1, dense_w3, dense_w2, moe_router, moe_w1, moe_w3, moe_w2,
              final_norm_g):
    b, n_lat, d = x.shape
    n_ctx = ctx.shape[1]
    tabs_mla = axial_rope_tables(n_ctx, n_lat, MLA_ROPE)
    tabs_gqa = axial_rope_tables(n_ctx, n_lat, GQA_HEAD_DIM)
    silu_c = jax.nn.silu(c)
    silu_cc = jax.nn.silu(c_ctx)

    for l in range(DEPTH):
        last = l == DEPTH - 1
        mod_lat = (silu_c @ w_ada[l] + b_ada[l]).reshape(b, 1, 6, d)
        mod_ctx = (silu_cc @ w_ada[l] + b_ada[l]).reshape(1, 1, 6, d)
        sh1_l, sc1_l, g1_l, sh2_l, sc2_l, g2_l = [mod_lat[:, :, i] for i in range(6)]
        sh1_c, sc1_c, g1_c, sh2_c, sc2_c, g2_c = [mod_ctx[:, :, i] for i in range(6)]

        h = jnp.concatenate([modulate(rms_norm(ctx, norm1_g[l]), sh1_c, sc1_c),
                             modulate(rms_norm(x, norm1_g[l]), sh1_l, sc1_l)], axis=1)
        mix = token_mixer(h, n_ctx, last, w_in[l], mla_q_norm_g[l], mla_w_qb[l],
                          mla_kv_norm_g[l], mla_w_kvb[l], gqa_q_norm_g[l], gqa_k_norm_g[l],
                          w_o_mla[l], w_o_gqa[l], w_out[l], tabs_mla, tabs_gqa)
        x = x + g1_l * mix[:, -n_lat:]
        if not last:
            ctx = ctx + g1_c * mix[:, :n_ctx]

        h2_lat = modulate(rms_norm(x, norm2_g[l]), sh2_l, sc2_l)
        if last:
            h2 = h2_lat
        else:
            h2 = jnp.concatenate([modulate(rms_norm(ctx, norm2_g[l]), sh2_c, sc2_c), h2_lat], axis=1)
        if l % 2 == 0:
            f = swiglu(h2, dense_w1[l // 2], dense_w3[l // 2], dense_w2[l // 2])
        else:
            f = moe_swiglu(h2, moe_router[l // 2], moe_w1[l // 2], moe_w3[l // 2], moe_w2[l // 2])
        x = x + g2_l * f[:, -n_lat:]
        if not last:
            ctx = ctx + g2_c * f[:, :n_ctx]

    return rms_norm(x, final_norm_g)


_drawn_inputs = setup_inputs


def setup_inputs(seed=0):
    import zlib

    import numpy as np

    out = dict(_drawn_inputs(seed))
    spreads = {}
    factors = {'norm1_g': 5.36,
     'mla_q_norm_g': 8.0,
     'mla_kv_norm_g': 4.551,
     'gqa_q_norm_g': 8.0,
     'gqa_k_norm_g': 7.912}
    for name, (base, spread) in spreads.items():
        noise = np.random.default_rng([zlib.crc32(name.encode()), seed]).standard_normal(out[name].shape)
        drawn = base * np.exp(spread * noise) if base else spread * noise
        out[name] = __import__('jax').numpy.asarray(drawn.astype(out[name].dtype))
    for name, factor in factors.items():
        out[name] = (out[name] * factor).astype(out[name].dtype)
    return out
```

```python
from contextlib import ExitStack

import numpy as np

import concourse.bass as bass
from concourse import mybir

F32 = mybir.dt.float32
I32 = mybir.dt.int32
ALU = mybir.AluOpType
ACT = mybir.ActivationFunctionType
AX = mybir.AxisListType

P = 128
D = 1024
KD = D // P
LAT = 256
CTX = 256
TOK = CTX + LAT
NT = TOK // P
DEPTH = 2
EPS = 1e-6
QL, KVL, ROPE, NOPE, VD = 384, 256, 32, 64, 64
HM, HG, HKV, HD = 8, 8, 2, 64
DK = NOPE + ROPE
MLA_SCALE = DK ** -0.5
GQA_SCALE = HD ** -0.5
FFN = 2816
FT = FFN // P
NE = 8
FE = 3584
FET = FE // P
GRID_W = 64
THETA = 10000.0
C_Q, C_KV, C_PE, C_QG, C_KG, C_VG = 0, QL, QL + KVL, QL + KVL + ROPE, QL + KVL + ROPE + HG * HD, QL + KVL + ROPE + HG * HD + HKV * HD
C_GA = C_VG + HKV * HD
C_GB = C_GA + D
IN_SLABS = [(0, 192, True), (192, 192, True), (C_KV, KVL + ROPE, False), (C_KG, 2 * HKV * HD, False),
            (C_QG, 256, True), (C_QG + 256, 256, True)]
SLAB_KG = 3
ADA_A, ADA_B = range(0, 16), range(16, 48)
RING = 6
SLOT = 2304
CHUNK = 256
STEPS = FE // CHUNK // 2
WIDTHS = (96, 144, LAT)
V_L = 64
V_CC, V_C, V_FIN, V_QN, V_KVN, V_GQ, V_GK = 128, 136, 144, 152, 158, 162, 164
V_ROWS = 166


def tiles_q(l):
    return [0, 1, 2, 3] if l < DEPTH - 1 else [2, 3]


def in_tiles(l):
    return [(s, t) for s, (_, _, q) in enumerate(IN_SLABS) for t in (tiles_q(l) if q else range(NT))]


_UNITS = NT * (HM + HG)
LAYER_COUNTS = dict(
    in_psum=len(in_tiles(0)), z_ready=len(in_tiles(0)), ssc_ready=2 * NT, msc_ready=1, rmsc_ready=1, msg_ready=1,
    rmsg_ready=1, c_ready=1, cT_psum=5, cT_ready=5, up_psum=4 * NT, up_taken=4 * NT, g_ready=1, gT_psum=HG + HKV,
    gT_taken=HG + HKV, qk_ready=1, qkT_psum=2 * HM, qT_taken=HM, kT_taken=HM, s_psum=_UNITS, max_ready=_UNITS,
    p_ready=_UNITS, pT_psum=_UNITS, pT_ready=_UNITS, rinv_ready=_UNITS, o_psum=_UNITS, o_ready=_UNITS, oT_psum=2 * NT,
    oT_ready=2 * NT, mg_psum=KD, sig_ready=KD, mT_ready=KD, out_psum=4 * NT, x1_added=4 * NT,
    **{f"{n}{w}": c for w in (1, 2) for n, c in (("xn_ready", NT), ("ss_ready", NT), ("ms_ready", 1), ("rms_ready", 1),
                                                 ("ht_psum", KD))},
    **{f"ht_taken{w}_{par}": KD // 2 for w in (1, 2) for par in (0, 1)},
    **{f"g{w}_{n}": 4 for w in (1, 2) for n in ("psum", "ready")})


def slab_list(a):
    out = []
    cols = lambda w, c, n: w.rearrange("(k p) n -> p k n", p=P)[:, :, c:c + n]

    def add(name, *parts):
        out.append((name, parts))

    def ada(l, tiles):
        for c in range(tiles[0], tiles[-1] + 1, 2):
            add("ada", cols(a["w_ada"][l], c * P, 2 * P))

    ada(0, ADA_A)
    for l in range(DEPTH):
        for c, n, _ in IN_SLABS:
            add("in", cols(a["w_in"][l], c, n))
        if l == 0:
            ada(0, ADA_B)
        add("qb", cols(a["mla_w_qb"][l], 0, HM * DK))
        add("kvb", cols(a["mla_w_kvb"][l], 0, HM * (NOPE + VD)))
        for jj in range(KD // 2):
            add("wo", cols(a["w_o_mla"][l], jj * 256, 256), cols(a["w_o_gqa"][l], jj * 256, 256))
            add("ga", cols(a["w_in"][l], C_GA + jj * 256, 256))
            add("gb", cols(a["w_in"][l], C_GB + jj * 256, 256))
        for s in range(4):
            add("out", cols(a["w_out"][l], s * 256, 256))
        if l == 0:
            ada(1, ADA_A)
            for s in range(FT // 2):
                add("w1", cols(a["dense_w1"][0], s * 256, 256))
                add("w3", cols(a["dense_w3"][0], s * 256, 256))
            for h in range(2):
                for f in range(0, FT, 4):
                    n = min(4, FT - f)
                    add("w2", a["dense_w2"][0].rearrange("(f p) n -> p f n", p=P)[:, f:f + n, h * 512:h * 512 + 512])
            ada(1, ADA_B)
    return out


def build(nc, a, out_dram):
    slabs = slab_list(a)
    n_slabs = len(slabs)

    with ExitStack() as ctx:
        def sb(name, shape, dt=F32):
            return ctx.enter_context(nc.sbuf_tensor(name, shape, dt))

        sems = {}

        def sem(name):
            if name not in sems:
                sems[name] = ctx.enter_context(nc.semaphore(name))
            return sems[name]

        def before_layer(name, l):
            return LAYER_COUNTS[name] if l else 0

        ring = [sb(f"ring{i}", [P, SLOT]) for i in range(RING)]
        x_res = sb("x_res", [P, NT, D])
        hT = sb("hT", [P, KD, TOK])
        z_mem = sb("z_mem", [P, NT * C_VG])
        q_mem = sb("q_mem", [P, NT * HM * DK])
        k_mem = sb("k_mem", [P, NT * HM * DK])
        v_mla = sb("v_mla", [P, NT, HM * VD])
        v_gqa = sb("v_gqa", [P, NT, HKV * HD])
        R_mem = sb("R_mem", [P, 13312])
        view = lambda mem, off, **dims: mem[:, off:off + int(np.prod(list(dims.values())))].rearrange(
            "p (" + " ".join(dims) + ") -> p " + " ".join(dims), **dims)

        z = view(z_mem, 0, t=NT, c=C_VG)
        xn = view(z_mem, 0, t=NT, c=D)
        oT = view(z_mem, 0, j=KD, t=TOK)
        q_tm = view(q_mem, 0, t=NT, c=HM * DK)
        o_tm = view(q_mem, 0, b=2, c=2 * HM * VD)
        sig = view(q_mem, 0, b=4, c=TOK)
        mg_t = view(q_mem, 4 * TOK, b=2, c=TOK)
        k_tm = view(k_mem, 0, t=NT, c=HM * DK)
        probs = view(k_mem, 0, b=2, c=TOK)
        probsT = view(k_mem, 2 * TOK, b=2, c=TOK)
        add_t = view(k_mem, 0, c=512)
        silu_t = view(k_mem, 512, b=2, c=TOK)
        qT = view(R_mem, 0, h=HM, t=TOK)
        kT = view(R_mem, 4096, h=HM, t=TOK)
        qgT = view(R_mem, 8192, h=HG, t=TOK)
        kgT = view(R_mem, 12288, h=HKV, t=TOK)
        cT = view(R_mem, 8192, j=5, t=TOK)
        junk_act = view(R_mem, 4096, c=QL)
        rope_a = view(R_mem, 0, c=(HG + HKV) * HD)
        rope_b = view(R_mem, 1024, c=(HG + HKV) * HD)
        mT = view(R_mem, 0, j=KD, t=TOK)
        gT = view(R_mem, 0, f=FT, t=TOK)
        gate_row = view(R_mem, 11264, b=2, c=D)
        hTe = view(R_mem, 0, k=KD, s=LAT)
        gTe = view(R_mem, 2048, b=4, s=LAT)
        silu_e = view(R_mem, 3072, b=2, s=LAT)
        S_oh = view(R_mem, 3584, t=2, s=LAT)
        C_oh = view(R_mem, 4096, t=2, s=LAT)
        CT = view(R_mem, 4608, s=2, t=LAT)
        yT = view(R_mem, 5120, k=KD, s=LAT)
        y = view(R_mem, 7168, s=2, c=D)
        acc = view(R_mem, 9216, t=2, c=D)
        fin_row = view(q_mem, 0, c=D)
        out_t = view(k_mem, 0, t=2, c=D)

        ident = sb("ident", [P, P])
        ones = sb("ones", [P, P])
        before = sb("before", [P, P])
        iota = sb("iota", [P, LAT])
        lower = sb("lower", [P, NE, NE])
        zeros = sb("zeros", [P, 512])
        vec_rows = sb("vec_rows", [P, 2, P])
        vec = sb("vec", [P, 256])
        sc = sb("sc", [P, 16])
        mod = sb("mod", [P, DEPTH, 48, 2])
        A1 = sb("A1", [P, DEPTH, KD, 2])
        A2 = sb("A2", [P, DEPTH, KD, 2])
        rope = sb("rope", [P, 2, 192])
        gq_row = sb("gq_row", [P, DEPTH, 2, HD])
        ss = sb("ss", [P, 8])
        rs = sb("rs", [P, 8])
        ssg = sb("ssg", [P, NT, HG + HKV])
        nmax = sb("nmax", [P, 4])
        rsum = sb("rsum", [P, 4])
        rinv = sb("rinv", [P, 4])
        router = sb("router", [P, KD, NE])
        lg = sb("lg", [P, 2, NE])
        v1 = sb("v1", [P, 2])
        cmp_a = sb("cmp_a", [P, 2, NE * NE])
        cmp_b = sb("cmp_b", [P, 2, NE * NE])
        rank = sb("rank", [P, 2, NE])
        ex = sb("ex", [P, 2, NE])
        den = sb("den", [P, 2])
        dinv = sb("dinv", [P, 2])
        sel = sb("sel", [P, 2, NE + 1])
        wgt = sb("wgt", [P, 2, NE + 1])
        pos = sb("pos", [P, 2, NE + 1])
        cnt = sb("cnt", [P, NE + 1], I32)
        ps = ctx.enter_context(nc.psum_tensor("ps", [P, 8, 512], F32))

        colv = lambda c, n=1: vec[:, c:c + n]
        tk = lambda t: slice(t * P, (t + 1) * P)
        loaded = [sem(f"slab_loaded_{i}") for i in range(RING)]
        slab_used = sem("slab_used")
        load_count = []
        tally = [0] * RING
        for i, (_, parts) in enumerate(slabs):
            tally[i % RING] += 16 * len(parts)
            load_count.append(tally[i % RING])

        block = ctx.enter_context(nc.Block())

        @block.sync
        def _(sp):
            for i, (name, parts) in enumerate(slabs):
                if i >= RING:
                    sp.wait_ge(slab_used, i - RING + 1)
                off = 0
                for src in parts:
                    _, k, n = src.shape
                    dst = ring[i % RING][:, off:off + k * n].rearrange("p (k n) -> p k n", k=k)
                    sp.dma_start(dst, src).then_inc(loaded[i % RING], 16)
                    off += k * n
            w1 = a["moe_w1"][0].rearrange("e (k p) n -> p e k n", p=P)
            w3 = a["moe_w3"][0].rearrange("e (k p) n -> p e k n", p=P)
            w2 = a["moe_w2"][0].rearrange("e (f p) n -> p (e f) n", p=P)
            with sp.Fori(0, NE) as e:
                with sp.Fori(0, STEPS) as s:
                    for c in range(2):
                        for m in range(3):
                            j = 3 * c + m
                            slot = (n_slabs + j) % RING
                            sp.wait_ge(slab_used, (e * STEPS + s) * RING + (n_slabs + j - RING + 1))
                            if m < 2:
                                src = (w1, w3)[m][:, bass.ds(e, 1), :, bass.ds(s * (2 * CHUNK) + c * CHUNK, CHUNK)]
                                src = src.rearrange("p e k n -> p (e k) n")
                                dst = ring[slot][:, 0:KD * CHUNK].rearrange("p (k n) -> p k n", k=KD)
                            else:
                                src = w2[:, bass.ds(e * FET + s * 4 + 2 * c, 2), :]
                                dst = ring[slot][:, 0:2 * D].rearrange("p (f n) -> p f n", f=2)
                            sp.dma_start(dst, src).then_inc(loaded[slot], 16)
            for t in range(2):
                sp.wait_ge(sem("out_ready"), t + 1)
                sp.dma_start(out_dram[0, t * P:(t + 1) * P, :], out_t[:, t, :]).then_inc(sem("out_stored"), 16)
            sp.wait_ge(sem("out_stored"), 32)

        @block.gpsimd
        def _(pool):
            pool.memset(ident[:, :], 0.0).then_inc(sem("const_step"), 1)
            pool.memset(ones[:, :], 1.0).then_inc(sem("const_step"), 1)
            pool.memset(before[:, :], 0.0).then_inc(sem("const_step"), 1)
            pool.memset(lower[:, :, :], 0.0).then_inc(sem("const_step"), 1)
            pool.memset(zeros[:, :], 0.0).then_inc(sem("const_ready"), 1)
            pool.wait_ge(sem("const_step"), 4)
            pool.affine_select(out=ident[:, :], in_=ident[:, :], compare_op=ALU.not_equal, fill=1.0, base=0,
                               pattern=[[-1, P]], channel_multiplier=1).then_inc(sem("const_ready"), 1)
            pool.affine_select(out=before[:, :], in_=before[:, :], compare_op=ALU.is_ge, fill=1.0, base=0,
                               pattern=[[-1, P]], channel_multiplier=1).then_inc(sem("const_ready"), 1)
            pool.affine_select(out=lower[:, :, :], in_=lower[:, :, :], compare_op=ALU.is_ge, fill=1.0, base=0,
                               pattern=[[-1, NE], [1, NE]], channel_multiplier=0).then_inc(sem("const_ready"), 1)
            pool.iota(iota[:, :], pattern=[[1, LAT]], base=0, channel_multiplier=0,
                      allow_small_or_imprecise_dtypes=True).then_inc(sem("const_ready"), 1)
            pool.memset(sel[:, :, NE:NE + 1], 0.0).then_inc(sem("const_ready"), 1)
            pool.memset(wgt[:, :, NE:NE + 1], 0.0).then_inc(sem("const_ready"), 1)
            pool.memset(pos[:, :, NE:NE + 1], 0.0).then_inc(sem("const_ready"), 1)
            pool.memset(cnt[:, NE:NE + 1], 0).then_inc(sem("const_ready"), 1)
        CONSTS = 9

        @block.tensor
        def _(pe):
            at = [0]

            spent = [0]

            def release(mm):
                if spent[0]:
                    mm.then_inc(slab_used, spent[0])
                    spent[0] = 0

            def slab():
                i = at[0]
                at[0] += 1
                pe.wait_ge(loaded[i % RING], load_count[i])
                views, o = [], 0
                for src in slabs[i][1]:
                    _, k, n = src.shape
                    views.append(ring[i % RING][:, o:o + k * n].rearrange("p (k n) -> p k n", k=k))
                    o += k * n
                return views if len(views) > 1 else views[0]

            def ada(l, tiles):
                for c in tiles[::2]:
                    w = slab()
                    for j in range(2):
                        for k in range(KD):
                            mm = pe.matmul(ps[:, 7, 2 * (c + j - tiles[0]):2 * (c + j - tiles[0]) + 2],
                                           w[:, k, j * P:(j + 1) * P],
                                           sc[:, :].rearrange("p (c k) -> p k c", c=2)[:, k, :],
                                           start=(k == 0), stop=(k == KD - 1))
                            if k == 0:
                                release(mm)
                    spent[0] += 1
                mm.then_inc(sem("ada_psum"), 1)

            def h_transpose(l, which, tiles):
                pe.wait_ge(sem(f"xn_ready{which}"), before_layer(f"xn_ready{which}", l) + len(tiles))
                for k in range(KD):
                    if k >= 4:
                        pe.wait_ge(sem(f"ht_taken{which}_{k % 2}"), before_layer(f"ht_taken{which}_{k % 2}", l) + (k - 4) // 2 + 1)
                    for t in tiles:
                        mm = pe.transpose(ps[:, k % 4, tk(t)], xn[:, t, tk(k)], ident[:, :])
                        if t != tiles[-1]:
                            release(mm)
                    mm.then_inc(sem(f"ht_psum{which}"), 1)
                for par in range(2):
                    pe.wait_ge(sem(f"ht_taken{which}_{par}"), before_layer(f"ht_taken{which}_{par}", l) + KD // 2)

            def rows(l, col, banks, name):
                for b, (c, kk) in zip(banks, [(c, kk) for c in col for kk in range(2)]):
                    for k in range(4):
                        mm = pe.matmul(ps[:, b, tk(k)], c(4 * kk + k).to_broadcast([P, P]), ident[:, :],
                                       start=True, stop=True)
                        if k == 0:
                            release(mm)
                    mm.then_inc(sem(f"{name}_psum"), 1)

            pe.wait_ge(sem("const_ready"), CONSTS)
            pe.wait_ge(sem("vec_loaded_a"), 16)
            pe.wait_ge(sem("vec_loaded_b"), 16)
            pe.transpose(ps[:, 0, 0:P], vec_rows[:, 0, :], ident[:, :])
            pe.transpose(ps[:, 0, P:V_ROWS], vec_rows[0:V_ROWS - P, 1, :], ident[0:V_ROWS - P, 0:V_ROWS - P])\
              .then_inc(sem("vec_psum"), 1)
            pe.wait_ge(sem("vec_ready"), 1)
            for l in range(DEPTH):
                for m, c in enumerate((V_GQ + l, V_GK + l)):
                    mm = pe.matmul(ps[:, 1, (2 * l + m) * HD:(2 * l + m + 1) * HD], colv(c).to_broadcast([P, P])[0:HD, :],
                                   ident[0:HD, 0:HD], start=True, stop=True)
            mm.then_inc(sem("gq_psum"), 1)
            pe.wait_ge(sem("gq_ready"), 1)

            ada(0, ADA_A)
            for l in range(DEPTH):
                tq = tiles_q(l)
                q0 = tq[0] * P
                nq = len(tq) * P
                h_transpose(l, 1, range(NT))

                n = -1
                for s, (c, cols, q) in enumerate(IN_SLABS):
                    w = slab()
                    for t in (tq if q else range(NT)):
                        n += 1
                        if n >= 3:
                            pe.wait_ge(sem("z_ready"), before_layer("z_ready", l) + n - 2)
                        for k in range(KD):
                            mm = pe.matmul(ps[:, 4 + n % 3, 0:cols], hT[:, k, tk(t)], w[:, k, :],
                                           start=(k == 0), stop=(k == KD - 1))
                            if k == 0:
                                release(mm)
                        mm.then_inc(sem("in_psum"), 1)
                    spent[0] += 1
                if l == 0:
                    ada(0, ADA_B)

                pe.wait_ge(sem("c_ready"), before_layer("c_ready", l) + 1)
                for j in range(5):
                    if j == 4:
                        pe.wait_ge(sem("cT_ready"), before_layer("cT_ready", l) + 1)
                    for t in (tq if j < 3 else range(NT)):
                        mm = pe.transpose(ps[:, j % 4, tk(t)], z[:, t, tk(j)], ident[:, :])
                        if t != NT - 1:
                            release(mm)
                    mm.then_inc(sem("cT_psum"), 1)
                pe.wait_ge(sem("cT_ready"), before_layer("cT_ready", l) + 5)
                pe.wait_ge(sem("z_ready"), before_layer("z_ready", l) + len(in_tiles(l)))
                pe.wait_ge(sem("mod_ready"), 2 if l == 0 else 4)
                n = -1
                w = slab()
                for t in tq:
                    for h in range(2):
                        n += 1
                        if n >= 4:
                            pe.wait_ge(sem("up_taken"), before_layer("up_taken", l) + n - 3)
                        for k in range(3):
                            mm = pe.matmul(ps[:, 4 + n % 4, 0:384], cT[:, k, tk(t)], w[:, k, h * 384:h * 384 + 384],
                                           start=(k == 0), stop=(k == 2))
                        mm.then_inc(sem("up_psum"), 1)
                spent[0] += 1
                w = slab()
                for t in range(NT):
                    for h in range(2):
                        n += 1
                        pe.wait_ge(sem("up_taken"), before_layer("up_taken", l) + n - 3)
                        for k in range(2):
                            mm = pe.matmul(ps[:, 4 + n % 4, :], cT[:, 3 + k, tk(t)], w[:, k, h * 512:h * 512 + 512],
                                           start=(k == 0), stop=(k == 1))
                            if k == 0:
                                release(mm)
                        mm.then_inc(sem("up_psum"), 1)
                spent[0] += 1

                pe.wait_ge(sem("g_ready"), before_layer("g_ready", l) + 1)
                for m in range(HG + HKV):
                    if m >= 4:
                        pe.wait_ge(sem("gT_taken"), before_layer("gT_taken", l) + m - 3)
                    for t in (tq if m < HG else range(NT)):
                        mm = pe.transpose(ps[0:HD, m % 4, tk(t)], z[:, t, C_QG + m * HD:C_QG + (m + 1) * HD], ident[:, :])
                        if t != NT - 1:
                            release(mm)
                    mm.then_inc(sem("gT_psum"), 1)
                pe.wait_ge(sem("gT_taken"), before_layer("gT_taken", l) + HG + HKV)
                pe.wait_ge(sem("qk_ready"), before_layer("qk_ready", l) + 1)
                pe.wait_ge(sem("up_taken"), before_layer("up_taken", l) + 2 * (len(tq) + NT))
                for m in range(2 * HM):
                    if m >= 4:
                        pe.wait_ge(sem(("qT_taken", "kT_taken")[m % 2]), before_layer(("qT_taken", "kT_taken")[m % 2], l) + (m - 4) // 2 + 1)
                    src = (q_tm, k_tm)[m % 2]
                    for t in (tq if m % 2 == 0 else range(NT)):
                        mm = pe.transpose(ps[0:DK, m % 4, tk(t)], src[:, t, (m // 2) * DK:(m // 2 + 1) * DK], ident[:, :])
                    mm.then_inc(sem("qkT_psum"), 1)
                pe.wait_ge(sem("qT_taken"), before_layer("qT_taken", l) + HM)
                pe.wait_ge(sem("kT_taken"), before_layer("kT_taken", l) + HM)

                units = [(qi, h) for qi in range(len(tq)) for h in range(HM + HG)]
                keys = lambda qi: CTX if tq[qi] < CTX // P else TOK
                for i in range(len(units) + 4):
                    if i < len(units):
                        qi, h = units[i]
                        nk = keys(qi)
                        if i >= 3:
                            pe.wait_ge(sem("p_ready"), before_layer("p_ready", l) + i - 2)
                        if h < HM:
                            pe.matmul(ps[:, i % 3, 0:nk], qT[0:DK, h, tk(tq[qi])], kT[0:DK, h, 0:nk],
                                      start=True, stop=True).then_inc(sem("s_psum"), 1)
                        else:
                            pe.matmul(ps[:, i % 3, 0:nk], qgT[0:HD, h - HM, tk(tq[qi])],
                                      kgT[0:HD, (h - HM) // (HG // HKV), 0:nk],
                                      start=True, stop=True).then_inc(sem("s_psum"), 1)
                    j = i - 2
                    if 0 <= j < len(units):
                        pe.wait_ge(sem("p_ready"), before_layer("p_ready", l) + j + 1)
                        if j >= 2:
                            pe.wait_ge(sem("pT_ready"), before_layer("pT_ready", l) + j - 1)
                        for kt in range(keys(units[j][0]) // P):
                            mm = pe.transpose(ps[:, 3 + j % 2, tk(kt)], probs[:, j % 2, tk(kt)], ident[:, :])
                        mm.then_inc(sem("pT_psum"), 1)
                    j = i - 3
                    if 0 <= j < len(units):
                        qi, h = units[j]
                        pe.wait_ge(sem("pT_ready"), before_layer("pT_ready", l) + j + 1)
                        if j >= 2:
                            pe.wait_ge(sem("o_ready"), before_layer("o_ready", l) + j - 1)
                        nkt = keys(qi) // P
                        for kt in range(nkt):
                            v = (v_mla[:, kt, h * VD:(h + 1) * VD] if h < HM else
                                 v_gqa[:, kt, (h - HM) // (HG // HKV) * HD:((h - HM) // (HG // HKV) + 1) * HD])
                            mm = pe.matmul(ps[:, 5 + j % 2, 0:VD], probsT[:, j % 2, tk(kt)], v,
                                           start=(kt == 0), stop=(kt == nkt - 1))
                        mm.then_inc(sem("o_psum"), 1)
                    j = i - 4
                    if 0 <= j < len(units) and units[j][1] == HM + HG - 1:
                        qi = units[j][0]
                        pe.wait_ge(sem("o_ready"), before_layer("o_ready", l) + j + 1)
                        for half in range(2):
                            r = 2 * qi + half
                            if r >= 1:
                                pe.wait_ge(sem("oT_ready"), before_layer("oT_ready", l) + r)
                            for k in range(4):
                                mm = pe.transpose(ps[:, 7, tk(k)], o_tm[:, qi % 2, tk(4 * half + k)], ident[:, :])
                            mm.then_inc(sem("oT_psum"), 1)
                pe.wait_ge(sem("oT_ready"), before_layer("oT_ready", l) + 2 * len(tq))

                for jj in range(KD // 2):
                    wa, wb = slab()
                    wga, wgb = slab(), slab()
                    for j in (2 * jj, 2 * jj + 1):
                        b = 4 * (j % 2)
                        c = (j % 2) * P
                        if j >= 2:
                            pe.wait_ge(sem("mT_ready"), before_layer("mT_ready", l) + j - 1)
                        for m, w in enumerate((wa, wb)):
                            for k in range(4):
                                mm = pe.matmul(ps[:, b + m, 0:nq], w[:, k, c:c + P], oT[:, 4 * m + k, q0:TOK],
                                               start=(k == 0), stop=(k == 3))
                                if k == 0:
                                    release(mm)
                        for m, w in enumerate((wga, wgb)):
                            for k in range(KD):
                                mm = pe.matmul(ps[:, b + 2 + m, 0:nq], w[:, k, c:c + P], hT[:, k, q0:TOK],
                                               start=(k == 0), stop=(k == KD - 1))
                        mm.then_inc(sem("mg_psum"), 1)
                    spent[0] += 3
                pe.wait_ge(sem("mT_ready"), before_layer("mT_ready", l) + KD - 1)
                rows(l, [lambda k, c=c: mod[:, l, 16 + k, c:c + 1] for c in range(2)], range(4), "g1")
                pe.wait_ge(sem("mT_ready"), before_layer("mT_ready", l) + KD)
                n = -1
                for s in range(4):
                    w = slab()
                    for t in tq:
                        n += 1
                        if n >= 4:
                            pe.wait_ge(sem("x1_added"), before_layer("x1_added", l) + n - 3)
                        for k in range(KD):
                            mm = pe.matmul(ps[:, 4 + n % 4, 0:256], mT[:, k, tk(t)], w[:, k, :],
                                           start=(k == 0), stop=(k == KD - 1))
                            if k == 0:
                                release(mm)
                        mm.then_inc(sem("out_psum"), 1)
                    spent[0] += 1
                pe.wait_ge(sem("x1_added"), before_layer("x1_added", l) + n + 1)
                if l == 0:
                    ada(1, ADA_A)
                h_transpose(l, 2, tq)
                if l == 0:
                    pe.wait_ge(sem("mod_ready"), 3)
                rows(l, [lambda k, c=c: mod[:, l, 40 + k, c:c + 1] for c in range(2)], range(4, 8), "g2")

                if l == 0:
                    for s in range(FT // 2):
                        w1, w3 = slab(), slab()
                        for j in range(2):
                            f = 2 * s + j
                            b = 2 * (f % 2)
                            if f >= 2:
                                pe.wait_ge(sem("gT_ready"), f - 1)
                            for m, w in enumerate((w1, w3)):
                                for k in range(KD):
                                    mm = pe.matmul(ps[:, b + m, :], w[:, k, tk(j)], hT[:, k, :],
                                                   start=(k == 0), stop=(k == KD - 1))
                                    if k == 0:
                                        release(mm)
                            mm.then_inc(sem("ff_psum"), 1)
                        spent[0] += 2
                    pe.wait_ge(sem("gT_ready"), FT)
                    pe.wait_ge(sem("g2_ready"), 4)
                    for h in range(2):
                        b = 4 if h == 0 else 0
                        for f0 in range(0, FT, 4):
                            w = slab()
                            for f in range(f0, min(f0 + 4, FT)):
                                for t in range(NT):
                                    mm = pe.matmul(ps[:, b + t, :], gT[:, f, tk(t)], w[:, f - f0, :],
                                                   start=(f == 0), stop=(f == FT - 1))
                                    if t == 0:
                                        release(mm)
                            spent[0] += 1
                        mm.then_inc(sem("dn_psum"), 1)
                    pe.wait_ge(sem("dn_added"), 1)
                    ada(1, ADA_B)

            pe.wait_ge(sem("router_loaded"), 16)
            for t in range(2):
                for k in range(KD):
                    mm = pe.matmul(ps[:, 0, t * NE:(t + 1) * NE], hT[:, k, tk(2 + t)], router[:, k, :],
                                   start=(k == 0), stop=(k == KD - 1))
                    release(mm) if k == 0 else None
            mm.then_inc(sem("lg_psum"), 1)
            rows(0, [lambda k: colv(V_FIN + k)], range(1, 3), "fin")
            pe.wait_ge(sem("sel_ready"), 1)
            pe.matmul(ps[:, 3, 0:NE], before[:, :], sel[:, 0, 0:NE], start=True, stop=True)
            pe.matmul(ps[:, 3, NE:2 * NE], ones[:, :], sel[:, 0, 0:NE], start=True, stop=False)
            pe.matmul(ps[:, 3, NE:2 * NE], before[:, :], sel[:, 1, 0:NE], start=False, stop=True)
            pe.matmul(ps[:, 3, 2 * NE:3 * NE], ones[:, :], sel[:, 0, 0:NE], start=True, stop=False)
            pe.matmul(ps[:, 3, 2 * NE:3 * NE], ones[:, :], sel[:, 1, 0:NE], start=False, stop=True)\
              .then_inc(sem("pos_psum"), 1)
            pe.wait_ge(sem("g2_ready"), 8)
            pe.wait_ge(sem("fin_ready"), 2)
            pe.wait_ge(sem("pos_ready"), 1)
            for b in (0, 1, 6, 7):
                pe.matmul(ps[:, b, :], zeros[:, 0:P], zeros[:, :], start=True, stop=True)

            def gather(e_next, W, first=None):
                for k in range(KD):
                    if k >= 2:
                        pe.wait_ge(sem(f"hTe_ready_{k % 2}"), e_next * (KD // 2) + k // 2)
                    for t in range(2):
                        mm = pe.matmul(ps[:, 6 + k % 2, 0:W], xn[:, 2 + t, tk(k)], S_oh[:, t, 0:W],
                                       start=(t == 0), stop=(t == 1))
                        if first and k == 0 and t == 0:
                            mm.then_inc(first, 1)
                    mm.then_inc(sem("hTe_psum"), 1)

            pe.wait_ge(sem("S_ready"), 1)
            gather(0, LAT)

            def expert_products(e, W):
                with pe.Fori(0, STEPS) as s:
                    it = pe.snap(e * STEPS + s)

                    def up(i, w1, w3):
                        pe.wait_ge(sem("gTe_ready"), it * 4 + i + 1)
                        for m, w in enumerate((w1, w3)):
                            for k in range(KD):
                                mm = pe.matmul(ps[:, i % 2, m * LAT:m * LAT + W], w[:, k, tk(i % 2)], hTe[:, k, 0:W],
                                               start=(k == 0), stop=(k == KD - 1))
                        mm.then_inc(sem("upe_psum"), 1)

                    def down(i, w2, free_first=0, free_last=0):
                        pe.wait_ge(sem("gTe_ready"), it * 4 + i + 3)
                        for k in range(KD):
                            mm = pe.matmul(ps[:, 2 + k // 2, (k % 2) * LAT:(k % 2) * LAT + W],
                                           w2[:, i % 2, tk(k)], gTe[:, i, 0:W], start=False, stop=False,
                                           skip_group_check=True)
                            if k == 0 and free_first:
                                mm.then_inc(slab_used, free_first)
                        if free_last:
                            mm.then_inc(slab_used, free_last)

                    def slabs_in(c):
                        v = []
                        for m in range(2):
                            slot = (n_slabs + 3 * c + m) % RING
                            pe.wait_ge(loaded[slot], it * 16 + (tally[slot] + 16))
                            v.append(ring[slot][:, 0:KD * CHUNK].rearrange("p (k n) -> p k n", k=KD))
                        return v

                    def slab_w2(c):
                        slot = (n_slabs + 3 * c + 2) % RING
                        pe.wait_ge(loaded[slot], it * 16 + (tally[slot] + 16))
                        return ring[slot][:, 0:2 * D].rearrange("p (f n) -> p f n", f=2)

                    w1, w3 = slabs_in(0)
                    up(0, w1, w3)
                    up(1, w1, w3)
                    w2 = slab_w2(0)
                    down(0, w2, free_first=2)
                    w1, w3 = slabs_in(1)
                    up(2, w1, w3)
                    down(1, w2, free_last=1)
                    up(3, w1, w3)
                    w2 = slab_w2(1)
                    down(2, w2, free_first=2)
                    down(3, w2, free_last=1)

            with pe.Fori(0, NE) as e:
                count = pe.value_load(cnt[0:1, bass.ds(e, 1)], min_val=0, max_val=LAT)
                for par in range(2):
                    pe.wait_ge(sem(f"hTe_ready_{par}"), e * (KD // 2) + KD // 2)
                for b in range(2, 6):
                    pe.matmul(ps[:, b, :], zeros[:, 0:P], zeros[:, :], start=True, stop=True, skip_group_check=True)
                with pe.If(count < WIDTHS[0] + 1):
                    expert_products(e, WIDTHS[0])
                with pe.Else():
                    with pe.If(count < WIDTHS[1] + 1):
                        expert_products(e, WIDTHS[1])
                    with pe.Else():
                        expert_products(e, WIDTHS[2])
                pe.wait_ge(sem("S_ready"), e + 2)
                gather(e + 1, LAT, first=sem("y_psum"))
                pe.wait_ge(sem("C_ready"), e + 1)
                for t in range(2):
                    for s in range(2):
                        mm = pe.transpose(ps[:, 0, s * LAT + t * P:s * LAT + (t + 1) * P], C_oh[:, t, tk(s)], ident[:, :])
                mm.then_inc(sem("CT_psum"), 1)
                pe.wait_ge(sem("yT_ready_a"), e * 2 + 2)
                pe.wait_ge(sem("yT_ready_v"), e * 2 + 2)
                for r, b in enumerate((1, 6, 7, 0)):
                    s, half = divmod(r, 2)
                    if b == 0:
                        pe.wait_ge(sem("y_taken_a"), e * 3 + 1)
                    if b in (6, 7):
                        pe.wait_ge(sem(f"hTe_ready_{b - 6}"), (e + 2) * (KD // 2))
                    for k in range(4):
                        mm = pe.transpose(ps[:, b, tk(k)], yT[:, 4 * half + k, tk(s)], ident[:, :])
                    mm.then_inc(sem("yt_psum"), 1)
                for r, b in enumerate((1, 6, 7, 0)):
                    t, half = divmod(r, 2)
                    if r == 0:
                        pe.wait_ge(sem("y_taken_a"), e * 3 + 3)
                        pe.wait_ge(sem("y_taken_v"), e * 2 + 2)
                    for s in range(2):
                        mm = pe.matmul(ps[:, b, :], CT[:, s, tk(t)], y[:, s, half * 512:half * 512 + 512],
                                       start=(s == 0), stop=(s == 1))
                    mm.then_inc(sem("sc_psum"), 1)
                pe.wait_ge(sem("acc_added"), e * 4 + 4)

        @block.scalar
        def _(act):
            act.dma_start(vec_rows[:, 0, :], a["vecs"][0:P, :]).then_inc(sem("vec_loaded_a"), 16)
            act.dma_start(vec_rows[0:V_ROWS - P, 1, :], a["vecs"][P:V_ROWS, :]).then_inc(sem("vec_loaded_b"), 16)
            act.dma_start(x_res[:, 0:2, :], a["ctx"][0].rearrange("(t p) d -> p t d", p=P)).then_inc(sem("ctx_loaded"), 16)
            act.dma_start(x_res[:, 2:4, :], a["x"][0].rearrange("(t p) d -> p t d", p=P)).then_inc(sem("x_loaded"), 16)
            act.dma_start(rope[:, :, :], a["rope"].rearrange("(t p) d -> p t d", p=P)).then_inc(sem("rope_loaded"), 16)
            act.dma_start(router[:, :, :], a["moe_router"][0].rearrange("(k p) n -> p k n", p=P))\
               .then_inc(sem("router_loaded"), 16)

            def squares(l, which, tiles):
                for i, t in enumerate(tiles):
                    act.activation(xn[:, t, :], x_res[:, t, :], ACT.Square, accum_out=ss[:, i:i + 1])\
                       .then_inc(sem(f"ss_ready{which}"), 1)
                act.wait_ge(sem(f"ms_ready{which}"), before_layer(f"ms_ready{which}", l) + 1)
                act.activation(rs[:, 0:len(tiles)], ss[:, 0:len(tiles)], ACT.Sqrt).then_inc(sem(f"rms_ready{which}"), 1)

            def modulate(l, which, tiles, A, sh):
                for k in range(0, KD, 2):
                    act.wait_ge(sem(f"ht_psum{which}"), before_layer(f"ht_psum{which}", l) + k + 1)
                    for c in ((0, 1) if 0 in tiles else (1,)):
                        ins = act.activation(hT[:, k, c * CTX:(c + 1) * CTX], ps[:, k % 4, c * CTX:(c + 1) * CTX],
                                             ACT.Identity, scale=A[:, l, k, c:c + 1], bias=mod[:, l, sh + k, c:c + 1])
                    ins.then_inc(sem(f"ht_taken{which}_0"), 1)

            def rows(l, n, bank0, name, dst):
                for b in range(n):
                    act.wait_ge(sem(f"{name}_psum"), 4 * l + b + 1)
                    act.activation(dst(b), ps[:, bank0 + b, :], ACT.Copy).then_inc(sem(f"{name}_ready"), 1)

            n_sq = [0]
            act.wait_ge(sem("vec_done"), 1)
            act.activation(sc[:, :], vec[:, V_CC:V_CC + 16], ACT.Silu).then_inc(sem("vec_ready"), 1)
            act.wait_ge(sem("ctx_loaded"), 16)
            act.wait_ge(sem("x_loaded"), 16)
            for l in range(DEPTH):
                tq = tiles_q(l)
                nq = len(tq) * P
                if l > 0:
                    act.wait_ge(sem("dn_added"), 2)
                squares(l, 1, range(NT))
                act.wait_ge(sem("mod_ready"), 2 * l + 1)
                modulate(l, 1, range(NT), A1, 0)
                n = -1
                for s, (c, cols, q) in enumerate(IN_SLABS):
                    for t in (tq if q else range(NT)):
                        n += 1
                        act.wait_ge(sem("in_psum"), before_layer("in_psum", l) + n + 1)
                        if s == SLAB_KG:
                            act.activation(v_gqa[:, t, :], ps[:, 4 + n % 3, P:2 * P], ACT.Copy)
                            cols = P
                        act.activation(z[:, t, c:c + cols], ps[:, 4 + n % 3, 0:cols], ACT.Copy)\
                           .then_inc(sem("z_ready"), 1)
                    if s == 2:
                        act.wait_ge(sem("z_ready"), before_layer("z_ready", l) + n + 1)
                        for t in tq:
                            act.activation(junk_act[:, 0:QL], z[:, t, C_Q:C_Q + QL], ACT.Square,
                                           accum_out=ss[:, t:t + 1]).then_inc(sem("ssc_ready"), 1)
                            n_sq[0] += 1
                            act.wait_ge(sem("ssc_ready"), n_sq[0])
                        for t in range(NT):
                            act.activation(junk_act[:, 0:KVL], z[:, t, C_KV:C_KV + KVL], ACT.Square,
                                           accum_out=ss[:, 4 + t:5 + t]).then_inc(sem("ssc_ready"), 1)
                            n_sq[0] += 1
                            act.wait_ge(sem("ssc_ready"), n_sq[0])
                act.wait_ge(sem("msc_ready"), before_layer("msc_ready", l) + 1)
                act.activation(rs[:, tq[0]:8], ss[:, tq[0]:8], ACT.Sqrt).then_inc(sem("rmsc_ready"), 1)
                act.wait_ge(sem("msg_ready"), before_layer("msg_ready", l) + 1)
                act.activation(ssg[:, :, :], ssg[:, :, :], ACT.Sqrt).then_inc(sem("rmsg_ready"), 1)
                n = -1
                for t in tq:
                    for h in range(2):
                        n += 1
                        act.wait_ge(sem("up_psum"), before_layer("up_psum", l) + n + 1)
                        act.activation(q_tm[:, t, h * 384:h * 384 + 384], ps[:, 4 + n % 4, 0:384], ACT.Copy)\
                           .then_inc(sem("up_taken"), 1)
                for t in range(NT):
                    for h in range(2):
                        n += 1
                        act.wait_ge(sem("up_psum"), before_layer("up_psum", l) + n + 1)
                        src = ps[:, 4 + n % 4, :].rearrange("p (h c) -> p h c", h=4)
                        act.activation(k_tm[:, t, :].rearrange("p (h c) -> p h c", h=HM)[:, 4 * h:4 * h + 4, 0:NOPE],
                                       src[:, :, 0:NOPE], ACT.Copy)
                        act.activation(v_mla[:, t, h * 256:h * 256 + 256].rearrange("p (h c) -> p h c", h=4),
                                       src[:, :, NOPE:NOPE + VD], ACT.Copy).then_inc(sem("up_taken"), 1)
                for m in range(HG + HKV):
                    act.wait_ge(sem("gT_psum"), before_layer("gT_psum", l) + m + 1)
                    if m < HG:
                        act.activation(qgT[0:HD, m, tq[0] * P:TOK], ps[0:HD, m % 4, tq[0] * P:TOK], ACT.Copy,
                                       scale=GQA_SCALE).then_inc(sem("gT_taken"), 1)
                    else:
                        act.activation(kgT[0:HD, m - HG, :], ps[0:HD, m % 4, :], ACT.Copy).then_inc(sem("gT_taken"), 1)
                for h in range(HM):
                    act.wait_ge(sem("qkT_psum"), before_layer("qkT_psum", l) + 2 * h + 1)
                    act.activation(qT[0:DK, h, tq[0] * P:TOK], ps[0:DK, (2 * h) % 4, tq[0] * P:TOK], ACT.Copy,
                                   scale=MLA_SCALE).then_inc(sem("qT_taken"), 1)
                n_units = len(tq) * (HM + HG)
                for i in range(n_units):
                    qi = i // (HM + HG)
                    nk = CTX if tq[qi] < CTX // P else TOK
                    act.wait_ge(sem("max_ready"), before_layer("max_ready", l) + i + 1)
                    if i >= 2:
                        act.wait_ge(sem("pT_psum"), before_layer("pT_psum", l) + i - 1)
                    act.activation(probs[:, i % 2, 0:nk], ps[:, i % 3, 0:nk], ACT.Exp, bias=nmax[:, i % 4:i % 4 + 1],
                                   accum_out=rsum[:, i % 4:i % 4 + 1]).then_inc(sem("p_ready"), 1)
                    for qi in range(len(tq)):
                        if i == min((qi + 1) * (HM + HG) + 3, n_units - 1 if qi == len(tq) - 1 else n_units):
                            for half in range(2):
                                act.wait_ge(sem("oT_psum"), before_layer("oT_psum", l) + 2 * qi + half + 1)
                                act.activation(oT[:, 4 * half:4 * half + 4, tk(tq[qi])],
                                               ps[:, 7, :].rearrange("p (k t) -> p k t", k=4), ACT.Copy)\
                                   .then_inc(sem("oT_ready"), 1)
                for j in range(KD):
                    act.wait_ge(sem("mg_psum"), before_layer("mg_psum", l) + j + 1)
                    if j >= 2:
                        act.wait_ge(sem("mT_ready"), before_layer("mT_ready", l) + j - 1)
                    for m in range(2):
                        ins = act.activation(sig[:, 2 * (j % 2) + m, 0:nq], ps[:, 4 * (j % 2) + 2 + m, 0:nq], ACT.Sigmoid)
                    ins.then_inc(sem("sig_ready"), 1)
                rows(l, 4, 0, "g1", lambda b: gate_row[:, b // 2, (b % 2) * 512:(b % 2) * 512 + 512])
                act.wait_ge(sem("x1_added"), before_layer("x1_added", l) + 4 * len(tq))
                squares(l, 2, tq)
                act.wait_ge(sem("mod_ready"), 2 * l + 2)
                modulate(l, 2, tq, A2, 24)
                rows(l, 4, 4, "g2", lambda b: gate_row[:, b // 2, (b % 2) * 512:(b % 2) * 512 + 512])
                if l == 0:
                    for f in range(FT):
                        act.wait_ge(sem("ff_psum"), f + 1)
                        if f >= 2:
                            act.wait_ge(sem("gT_ready"), f - 1)
                        act.activation(silu_t[:, f % 2, :], ps[:, 2 * (f % 2), :], ACT.Silu).then_inc(sem("silu_ready"), 1)

            rows(0, 2, 1, "fin", lambda b: fin_row[:, b * 512:b * 512 + 512])
            act.wait_ge(sem("lgm_ready"), 1)
            act.activation(ex[:, :, :], ex[:, :, :], ACT.Exp).then_inc(sem("ex_ready"), 1)

            def slots_in(e_at, k):
                act.wait_ge(sem("hTe_psum"), e_at * KD + k + 1)
                act.activation(hTe[:, k, :], ps[:, 6, 0:LAT], ACT.Identity, scale=A2[:, 1, k, 1:2],
                               bias=mod[:, 1, 24 + k, 1:2]).then_inc(sem("hTe_ready_0"), 1)

            for k in range(0, KD, 2):
                slots_in(0, k)
            with act.Fori(0, NE) as e:
                with act.Fori(0, STEPS) as s:
                    for i in range(4):
                        act.wait_ge(sem("upe_psum"), (e * STEPS + s) * 4 + i + 1)
                        act.activation(silu_e[:, i % 2, :], ps[:, i % 2, 0:LAT], ACT.Silu).then_inc(sem("silu_e_ready"), 1)
                act.wait_ge(sem("y_psum"), e + 1)
                for b in (2, 3):
                    act.activation(yT[:, 2 * (b - 2):2 * (b - 2) + 2, :], ps[:, b, :].rearrange("p (k s) -> p k s", k=2),
                                   ACT.Copy).then_inc(sem("yT_ready_a"), 1)
                for k in range(0, KD, 2):
                    slots_in(e + 1, k)
                act.wait_ge(sem("CT_psum"), e + 1)
                act.activation(CT[:, :, :], ps[:, 0, :].rearrange("p (s t) -> p s t", s=2), ACT.Copy)\
                   .then_inc(sem("y_taken_a"), 1)
                for r, b in ((0, 1), (2, 7)):
                    act.wait_ge(sem("yt_psum"), e * 4 + r + 1)
                    act.activation(y[:, r // 2, (r % 2) * 512:(r % 2) * 512 + 512], ps[:, b, :], ACT.Copy)\
                       .then_inc(sem("y_taken_a"), 1)
            for t in range(2):
                act.wait_ge(sem("xf_ready"), t + 1)
                act.activation(hT[:, 2 * t:2 * t + 2, :], x_res[:, 2 + t, :].rearrange("p (a b) -> p a b", a=2),
                               ACT.Square, accum_out=ss[:, t:t + 1]).then_inc(sem("ssf_ready"), 1)
            act.wait_ge(sem("msf_ready"), 1)
            act.activation(rs[:, 0:2], ss[:, 0:2], ACT.Sqrt).then_inc(sem("rmsf_ready"), 1)

        @block.vector
        def _(dve):
            steps = [0]

            def then(ins):
                steps[0] += 1
                ins.then_inc(sem("dve_step"), 1)
                dve.wait_ge(sem("dve_step"), steps[0])

            def bc(ap, shape):
                return ap.to_broadcast(shape)

            def norm(l, which, tiles):
                n = len(tiles)
                dve.wait_ge(sem(f"ss_ready{which}"), before_layer(f"ss_ready{which}", l) + n)
                dve.tensor_scalar(ss[:, 0:n], ss[:, 0:n], 1.0 / D, EPS, ALU.mult, ALU.add)\
                   .then_inc(sem(f"ms_ready{which}"), 1)
                dve.wait_ge(sem(f"rms_ready{which}"), before_layer(f"rms_ready{which}", l) + 1)
                then(dve.reciprocal(rs[:, 0:n], rs[:, 0:n]))
                for i, t in enumerate(tiles):
                    dve.tensor_scalar(xn[:, t, :], x_res[:, t, :], rs[:, i:i + 1], None, ALU.mult)\
                       .then_inc(sem(f"xn_ready{which}"), 1)

            def ada(l, tiles):
                n = len(tiles)
                dve.wait_ge(sem("ada_psum"), 2 * l + (1 if tiles is ADA_A else 2))
                then(dve.tensor_tensor(mod[:, l, tiles[0]:tiles[0] + n, :],
                                       ps[:, 7, 0:2 * n].rearrange("p (t c) -> p t c", c=2),
                                       bc(vec[:, l * V_L + tiles[0]:l * V_L + tiles[0] + n].unsqueeze(2), [P, n, 2]), ALU.add))
                A, src, g = (A1, 8, 48) if tiles is ADA_A else (A2, 32, 56)
                dve.scalar_tensor_tensor(A[:, l, :, :], mod[:, l, src:src + KD, :], 1.0,
                                         bc(vec[:, l * V_L + g:l * V_L + g + KD].unsqueeze(2), [P, KD, 2]),
                                         ALU.add, ALU.mult).then_inc(sem("mod_ready"), 1)

            def modulate(l, which, tiles, A, sh):
                dve.wait_ge(sem("mod_ready"), 2 * l + which)
                for k in range(1, KD, 2):
                    dve.wait_ge(sem(f"ht_psum{which}"), before_layer(f"ht_psum{which}", l) + k + 1)
                    for c in ((0, 1) if 0 in tiles else (1,)):
                        ins = dve.tensor_scalar(hT[:, k, c * CTX:(c + 1) * CTX], ps[:, k % 4, c * CTX:(c + 1) * CTX],
                                                A[:, l, k, c:c + 1], mod[:, l, sh + k, c:c + 1], ALU.mult, ALU.add)
                    ins.then_inc(sem(f"ht_taken{which}_1"), 1)

            def rotate(xs, t, heads, dim, stride, tab, ta, tb):
                f = dim // 4
                flat = lambda m: m[:, 0:heads * dim].rearrange("p (h d) -> p h d", h=heads)
                halves = lambda m: m.rearrange("p h (a b f) -> p h a b f", a=2, b=2)
                cos = rope[:, t, tab:tab + dim]
                sin = rope[:, t, tab + dim:tab + 2 * dim].rearrange("p (a b f) -> p a b f", a=2, b=2)
                dve.tensor_tensor(flat(ta), xs, bc(cos.unsqueeze(1), [P, heads, dim]), ALU.mult)
                for b in range(2):
                    for ax in range(2):
                        ins = dve.tensor_tensor(halves(flat(tb))[:, :, ax, b, :], halves(xs)[:, :, ax, 1 - b, :],
                                                bc(sin[:, ax, b, :].unsqueeze(1), [P, heads, f]), ALU.mult)
                then(ins)
                return dve.tensor_tensor(xs, flat(ta), flat(tb), ALU.add)

            dve.wait_ge(sem("vec_psum"), 1)
            dve.tensor_copy(vec[:, 0:V_ROWS], ps[:, 0, 0:V_ROWS]).then_inc(sem("vec_done"), 1)
            dve.wait_ge(sem("gq_psum"), 1)
            dve.tensor_copy(gq_row[:, :, :, :], ps[:, 1, 0:4 * HD].rearrange("p (l m d) -> p l m d", l=DEPTH, m=2))\
               .then_inc(sem("gq_ready"), 1)
            dve.wait_ge(sem("ctx_loaded"), 16)
            dve.wait_ge(sem("x_loaded"), 16)
            dve.wait_ge(sem("rope_loaded"), 16)

            for l in range(DEPTH):
                tq = tiles_q(l)
                nq = len(tq) * P
                qt = slice(tq[0], NT)
                norm(l, 1, range(NT))
                ada(l, ADA_A if l == 0 else ADA_B)
                modulate(l, 1, range(NT), A1, 0)

                dve.wait_ge(sem("ssc_ready"), before_layer("ssc_ready", l) + len(tq) + NT)
                then(dve.tensor_scalar(ss[:, tq[0]:4], ss[:, tq[0]:4], 1.0 / QL, EPS, ALU.mult, ALU.add))
                dve.tensor_scalar(ss[:, 4:8], ss[:, 4:8], 1.0 / KVL, EPS, ALU.mult, ALU.add).then_inc(sem("msc_ready"), 1)
                z_g = lambda t, m0, m1: z[:, t, C_QG + m0 * HD:C_QG + m1 * HD]
                dve.wait_ge(sem("z_ready"), before_layer("z_ready", l) + len(in_tiles(l)))
                heads = lambda t: (0 if t in tq else HG, HG + HKV)
                if l > 0:
                    then(dve.memset(ssg[:, 0:2, 0:HG], HD))
                for t in range(NT):
                    m0, m1 = heads(t)
                    n = (m1 - m0) * HD
                    then(dve.tensor_tensor(rope_a[:, 0:n], z_g(t, m0, m1), z_g(t, m0, m1), ALU.mult))
                    then(dve.tensor_reduce(ssg[:, t, m0:m1], rope_a[:, 0:n].rearrange("p (h d) -> p h d", d=HD), AX.X, ALU.add))
                dve.tensor_scalar(ssg[:, :, :], ssg[:, :, :], 1.0 / HD, EPS, ALU.mult, ALU.add)\
                   .then_inc(sem("msg_ready"), 1)
                dve.wait_ge(sem("rmsc_ready"), before_layer("rmsc_ready", l) + 1)
                then(dve.reciprocal(rs[:, tq[0]:8], rs[:, tq[0]:8]))
                for t in tq:
                    dve.tensor_scalar(z[:, t, C_Q:C_Q + QL], z[:, t, C_Q:C_Q + QL], rs[:, t:t + 1], None, ALU.mult)
                for t in range(NT):
                    ins = dve.tensor_scalar(z[:, t, C_KV:C_KV + KVL], z[:, t, C_KV:C_KV + KVL], rs[:, 4 + t:5 + t], None, ALU.mult)
                ins.then_inc(sem("c_ready"), 1)
                if l == 0:
                    ada(0, ADA_B)
                for j in range(5):
                    g = (V_QN + 3 * l + j) if j < 3 else (V_KVN + 2 * l + j - 3)
                    lo = tq[0] * P if j < 3 else 0
                    dve.wait_ge(sem("cT_psum"), before_layer("cT_psum", l) + j + 1)
                    dve.tensor_scalar(cT[:, j, lo:TOK], ps[:, j % 4, lo:TOK], colv(g), None, ALU.mult)\
                       .then_inc(sem("cT_ready"), 1)
                dve.wait_ge(sem("rmsg_ready"), before_layer("rmsg_ready", l) + 1)
                then(dve.reciprocal(ssg[:, :, :], ssg[:, :, :]))
                for t in range(NT):
                    m0, m1 = heads(t)
                    xs = z_g(t, m0, m1).rearrange("p (h d) -> p h d", d=HD)
                    then(dve.tensor_tensor(xs, xs, bc(ssg[:, t, m0:m1].unsqueeze(2), [P, m1 - m0, HD]), ALU.mult))
                    if m0 == 0:
                        xq = z_g(t, 0, HG).rearrange("p (h d) -> p h d", d=HD)
                        dve.tensor_tensor(xq, xq, bc(gq_row[:, l, 0, :].unsqueeze(1), [P, HG, HD]), ALU.mult)
                    xk = z_g(t, HG, HG + HKV).rearrange("p (h d) -> p h d", d=HD)
                    ins = dve.tensor_tensor(xk, xk, bc(gq_row[:, l, 1, :].unsqueeze(1), [P, HKV, HD]), ALU.mult)
                    if t >= 2:
                        then(ins)
                        ins = rotate(xs, t - 2, m1 - m0, HD, HD, 0, rope_a, rope_b)
                        if t < NT - 1:
                            then(ins)
                ins.then_inc(sem("g_ready"), 1)
                dve.wait_ge(sem("g_ready"), before_layer("g_ready", l) + 1)
                for t in range(NT):
                    xk = z[:, t, C_PE:C_PE + ROPE].rearrange("p (h d) -> p h d", h=1)
                    if t >= 2:
                        then(rotate(xk, t - 2, 1, ROPE, ROPE, 128, rope_a, rope_b))
                    dve.tensor_copy(k_tm[:, t, :].rearrange("p (h c) -> p h c", h=HM)[:, :, NOPE:DK],
                                    bc(z[:, t, C_PE:C_PE + ROPE].unsqueeze(1), [P, HM, ROPE]))
                for t in (2, 3):
                    dve.wait_ge(sem("up_taken"), before_layer("up_taken", l) + 2 * (t - tq[0] + 1))
                    xq = q_tm[:, t, :].rearrange("p (h c) -> p h c", h=HM)[:, :, NOPE:DK]
                    ins = rotate(xq, t - 2, HM, ROPE, DK, 128, rope_a, rope_b)
                    if t == 2:
                        then(ins)
                ins.then_inc(sem("qk_ready"), 1)
                for h in range(HM):
                    dve.wait_ge(sem("qkT_psum"), before_layer("qkT_psum", l) + 2 * h + 2)
                    dve.tensor_copy(kT[0:DK, h, :], ps[0:DK, (2 * h + 1) % 4, :]).then_inc(sem("kT_taken"), 1)

                n_units = len(tq) * (HM + HG)
                keys = lambda i: CTX if tq[i // (HM + HG)] < CTX // P else TOK
                for i in range(n_units + 3):
                    if i < n_units:
                        dve.wait_ge(sem("s_psum"), before_layer("s_psum", l) + i + 1)
                        dve.tensor_reduce(nmax[:, i % 4:i % 4 + 1], ps[:, i % 3, 0:keys(i)], AX.X, ALU.max, negate=True)\
                           .then_inc(sem("max_ready"), 1)
                    j = i - 2
                    if 0 <= j < n_units:
                        dve.wait_ge(sem("pT_psum"), before_layer("pT_psum", l) + j + 1)
                        if j >= 2:
                            dve.wait_ge(sem("o_psum"), before_layer("o_psum", l) + j - 1)
                        dve.tensor_copy(probsT[:, j % 2, 0:keys(j)], ps[:, 3 + j % 2, 0:keys(j)]).then_inc(sem("pT_ready"), 1)
                        dve.reciprocal(rinv[:, j % 4:j % 4 + 1], rsum[:, j % 4:j % 4 + 1]).then_inc(sem("rinv_ready"), 1)
                    j = i - 3
                    if 0 <= j < n_units:
                        qi, h = divmod(j, HM + HG)
                        dve.wait_ge(sem("o_psum"), before_layer("o_psum", l) + j + 1)
                        dve.wait_ge(sem("rinv_ready"), before_layer("rinv_ready", l) + j + 1)
                        if h == 0 and qi >= 2:
                            dve.wait_ge(sem("oT_psum"), before_layer("oT_psum", l) + 2 * (qi - 1))
                        dve.tensor_scalar(o_tm[:, qi % 2, h * VD:(h + 1) * VD], ps[:, 5 + j % 2, 0:VD],
                                          rinv[:, j % 4:j % 4 + 1], None, ALU.mult).then_inc(sem("o_ready"), 1)
                for j in range(KD):
                    dve.wait_ge(sem("sig_ready"), before_layer("sig_ready", l) + j + 1)
                    dve.wait_ge(sem("mT_ready"), before_layer("mT_ready", l) + j)
                    for m in range(2):
                        ins = dve.tensor_tensor(mg_t[:, m, 0:nq], sig[:, 2 * (j % 2) + m, 0:nq], ps[:, 4 * (j % 2) + m, 0:nq], ALU.mult)
                    then(ins)
                    dve.tensor_tensor(mT[:, j, tq[0] * P:TOK], mg_t[:, 0, 0:nq], mg_t[:, 1, 0:nq], ALU.add)\
                       .then_inc(sem("mT_ready"), 1)
                dve.wait_ge(sem("g1_ready"), before_layer("g1_ready", l) + 4)
                n = -1
                for s in range(4):
                    for t in tq:
                        n += 1
                        dve.wait_ge(sem("out_psum"), before_layer("out_psum", l) + n + 1)
                        then(dve.tensor_tensor(add_t[:, 0:256], gate_row[:, t // 2, s * 256:s * 256 + 256],
                                               ps[:, 4 + n % 4, 0:256], ALU.mult))
                        dve.tensor_tensor(x_res[:, t, s * 256:s * 256 + 256], x_res[:, t, s * 256:s * 256 + 256],
                                          add_t[:, 0:256], ALU.add).then_inc(sem("x1_added"), 1)
                        dve.wait_ge(sem("x1_added"), before_layer("x1_added", l) + n + 1)
                norm(l, 2, tq)
                if l == 0:
                    ada(1, ADA_A)
                modulate(l, 2, tq, A2, 24)
                if l == 0:
                    for f in range(FT):
                        dve.wait_ge(sem("silu_ready"), f + 1)
                        dve.tensor_tensor(gT[:, f, :], silu_t[:, f % 2, :], ps[:, 2 * (f % 2) + 1, :], ALU.mult)\
                           .then_inc(sem("gT_ready"), 1)
                    for h in range(2):
                        dve.wait_ge(sem("dn_psum"), h + 1)
                        for t in range(NT):
                            then(dve.tensor_tensor(add_t[:, :], gate_row[:, t // 2, h * 512:h * 512 + 512],
                                                   ps[:, (4 if h == 0 else 0) + t, :], ALU.mult))
                            ins = dve.tensor_tensor(x_res[:, t, h * 512:h * 512 + 512], x_res[:, t, h * 512:h * 512 + 512],
                                                    add_t[:, :], ALU.add)
                            if t < NT - 1:
                                then(ins)
                        ins.then_inc(sem("dn_added"), 1)
                        dve.wait_ge(sem("dn_added"), h + 1)

            dve.wait_ge(sem("lg_psum"), 1)
            then(dve.tensor_copy(lg[:, :, :], ps[:, 0, 0:2 * NE].rearrange("p (t e) -> p t e", t=2)))
            then(dve.tensor_reduce(v1[:, :], lg[:, :, :], AX.X, ALU.max))
            dve.tensor_tensor(ex[:, :, :], lg[:, :, :], bc(v1[:, :].unsqueeze(2), [P, 2, NE]), ALU.subtract)\
               .then_inc(sem("lgm_ready"), 1)
            for t in range(2):
                a3 = cmp_a[:, t, :].rearrange("p (e j) -> p e j", e=NE)
                b3 = cmp_b[:, t, :].rearrange("p (e j) -> p e j", e=NE)
                other = bc(lg[:, t, :].unsqueeze(1), [P, NE, NE])
                own = bc(lg[:, t, :].unsqueeze(2), [P, NE, NE])
                dve.tensor_tensor(a3, other, own, ALU.is_gt)
                then(dve.tensor_tensor(b3, other, own, ALU.is_equal))
                then(dve.tensor_tensor(b3, b3, lower[:, :, :], ALU.mult))
                then(dve.tensor_tensor(a3, a3, b3, ALU.add))
                then(dve.tensor_reduce(rank[:, t, :], a3, AX.X, ALU.add))
            dve.tensor_scalar(sel[:, :, 0:NE], rank[:, :, :], 1.5, None, ALU.is_lt).then_inc(sem("sel_ready"), 1)
            dve.wait_ge(sem("sel_ready"), 1)
            dve.wait_ge(sem("ex_ready"), 1)
            then(dve.tensor_tensor(ex[:, :, :], ex[:, :, :], sel[:, :, 0:NE], ALU.mult))
            then(dve.tensor_reduce(den[:, :], ex[:, :, :], AX.X, ALU.add))
            then(dve.reciprocal(dinv[:, :], den[:, :]))
            then(dve.tensor_tensor(wgt[:, :, 0:NE], ex[:, :, :], bc(dinv[:, :].unsqueeze(2), [P, 2, NE]), ALU.mult))
            dve.wait_ge(sem("pos_psum"), 1)
            dve.tensor_copy(cnt[:, 0:NE], ps[:, 3, 2 * NE:3 * NE])
            then(dve.tensor_copy(pos[:, :, 0:NE], ps[:, 3, 0:2 * NE].rearrange("p (t e) -> p t e", t=2)))
            dve.memset(acc[:, :, :], 0.0).then_inc(sem("pos_ready"), 1)
            dve.wait_ge(sem("pos_ready"), 1)

            def one_hot(dst, e_at, weight):
                for t in range(2):
                    ins = dve.tensor_scalar(dst[:, t, :], iota[:, :], pos[:, t, bass.ds(e_at, 1)],
                                            weight[:, t, bass.ds(e_at, 1)], ALU.is_equal, ALU.mult)
                return ins

            def slots_in(e_at, k):
                dve.wait_ge(sem("hTe_psum"), e_at * KD + k + 1)
                dve.tensor_scalar(hTe[:, k, :], ps[:, 7, 0:LAT], A2[:, 1, k, 1:2], mod[:, 1, 24 + k, 1:2],
                                  ALU.mult, ALU.add).then_inc(sem("hTe_ready_1"), 1)

            one_hot(S_oh, 0, sel).then_inc(sem("S_ready"), 1)
            dve.tensor_copy(rinv[:, 1:2], den[:, 0:1]).then_inc(sem("gTe_ready"), 2)
            for k in range(1, KD, 2):
                slots_in(0, k)
            with dve.Fori(0, NE) as e:
                one_hot(C_oh, e, wgt).then_inc(sem("C_ready"), 1)
                dve.wait_ge(sem("hTe_psum"), e * KD + KD)
                one_hot(S_oh, e + 1, sel).then_inc(sem("S_ready"), 1)
                with dve.Fori(0, STEPS) as s:
                    for i in range(4):
                        dve.wait_ge(sem("silu_e_ready"), (e * STEPS + s) * 4 + i + 1)
                        dve.tensor_tensor(gTe[:, i, :], silu_e[:, i % 2, :], ps[:, i % 2, LAT:2 * LAT], ALU.mult)\
                           .then_inc(sem("gTe_ready"), 1)
                dve.wait_ge(sem("y_psum"), e + 1)
                for b in (4, 5):
                    dve.tensor_copy(yT[:, 2 * (b - 2):2 * (b - 2) + 2, :], ps[:, b, :].rearrange("p (k s) -> p k s", k=2))\
                       .then_inc(sem("yT_ready_v"), 1)
                for k in range(1, KD, 2):
                    slots_in(e + 1, k)
                for r, b in ((1, 6), (3, 0)):
                    dve.wait_ge(sem("yt_psum"), e * 4 + r + 1)
                    dve.tensor_copy(y[:, r // 2, (r % 2) * 512:(r % 2) * 512 + 512], ps[:, b, :])\
                       .then_inc(sem("y_taken_v"), 1)
                for r, b in enumerate((1, 6, 7, 0)):
                    dve.wait_ge(sem("sc_psum"), e * 4 + r + 1)
                    part = acc[:, r // 2, (r % 2) * 512:(r % 2) * 512 + 512]
                    dve.tensor_tensor(part, part, ps[:, b, :], ALU.add).then_inc(sem("acc_added"), 1)
                dve.wait_ge(sem("acc_added"), e * 4 + 4)
                dve.wait_ge(sem("CT_psum"), e + 1)
            dve.wait_ge(sem("acc_added"), 4 * NE)
            then(dve.tensor_tensor(acc[:, :, :], acc[:, :, :], bc(gate_row[:, 1, :].unsqueeze(1), [P, 2, D]), ALU.mult))
            for t in range(2):
                dve.tensor_tensor(x_res[:, 2 + t, :], x_res[:, 2 + t, :], acc[:, t, :], ALU.add).then_inc(sem("xf_ready"), 1)
            dve.wait_ge(sem("ssf_ready"), 2)
            dve.tensor_scalar(ss[:, 0:2], ss[:, 0:2], 1.0 / D, EPS, ALU.mult, ALU.add).then_inc(sem("msf_ready"), 1)
            dve.wait_ge(sem("rmsf_ready"), 1)
            then(dve.reciprocal(rs[:, 0:2], rs[:, 0:2]))
            dve.wait_ge(sem("fin_ready"), 2)
            dve.wait_ge(sem("xf_ready"), 2)
            for t in range(2):
                dve.scalar_tensor_tensor(out_t[:, t, :], x_res[:, 2 + t, :], rs[:, t:t + 1], fin_row[:, :],
                                         ALU.mult, ALU.mult).then_inc(sem("out_ready"), 1)


_WEIGHTS = ["w_ada", "w_in", "mla_w_qb", "mla_w_kvb", "w_o_mla", "w_o_gqa", "w_out", "dense_w1", "dense_w3", "dense_w2",
            "moe_router", "moe_w1", "moe_w3", "moe_w2"]


def rope_rows():
    t = np.arange(LAT)
    out = []
    for dim in (HD, ROPE):
        half = dim // 2
        inv = (np.float32(THETA) ** (-(np.arange(half // 2, dtype=np.float32) * np.float32(2.0)) / np.float32(half))).astype(np.float32)
        ang = [(p.astype(np.float32)[:, None] * inv).astype(np.float32) for p in (t // GRID_W, t % GRID_W)]
        out += [np.concatenate([np.cos(g) for a in ang for g in (a, a)], axis=1),
                np.concatenate([s * np.sin(a) for a in ang for s in (-1.0, 1.0)], axis=1)]
    return np.concatenate(out, axis=1).astype(np.float32)


def pack_vectors(i):
    wide = lambda v: np.reshape(v, (-1, P))
    half = lambda v: np.concatenate([np.reshape(v, (1, HD)), np.zeros((1, P - HD), np.float32)], axis=1)
    rows = [wide(i[n][l]) for l in range(DEPTH) for n in ("b_ada", "norm1_g", "norm2_g")]
    rows += [wide(i["c_ctx"]), wide(i["c"]), wide(i["final_norm_g"])]
    rows += [wide(i["mla_q_norm_g"]), wide(i["mla_kv_norm_g"])]
    rows += [half(i[n][l]) for n in ("gqa_q_norm_g", "gqa_k_norm_g") for l in range(DEPTH)]
    return np.ascontiguousarray(np.concatenate(rows, axis=0))


def kernel(**inputs):
    import concourse.bacc as _bacc
    from concourse.bass_utils import run_bass_kernel_spmd as _run

    nc = _bacc.Bacc("TRN2", target_bir_lowering=False, num_devices=1)
    host = {n: np.ascontiguousarray(v) for n, v in inputs.items()}
    given = {n: host[n] for n in ["x", "ctx"] + _WEIGHTS}
    given["vecs"] = pack_vectors(host)
    given["rope"] = rope_rows()
    aps, arrays = {}, {}
    for n, v in given.items():
        arrays[f"in_{n}"] = v
        aps[n] = nc.dram_tensor(f"in_{n}", v.shape, mybir.dt.from_np(v.dtype), kind="ExternalInput").ap()
    out = nc.dram_tensor("out", (1, LAT, D), F32, kind="ExternalOutput").ap()
    build(nc, aps, out)
    r = _run(nc, [arrays], core_ids=[0])
    return r.results[0]["out"]
```

```python
from contextlib import ExitStack

import numpy as np

import concourse.bass as bass
from concourse import mybir

F32 = mybir.dt.float32
F32R = mybir.dt.float32r
I32 = mybir.dt.int32
ALU = mybir.AluOpType
ACT = mybir.ActivationFunctionType
AX = mybir.AxisListType

P = 128
D = 1024
KD = D // P
LAT = 256
CTX = 256
TOK = CTX + LAT
NT = TOK // P
DEPTH = 2
EPS = 1e-6
QL, KVL, ROPE, NOPE, VD = 384, 256, 32, 64, 64
HM, HG, HKV, HD = 8, 8, 2, 64
DK = NOPE + ROPE
MLA_SCALE = DK ** -0.5
GQA_SCALE = HD ** -0.5
FFN = 2816
FT = FFN // P
NE = 8
FE = 3584
FET = FE // P
GRID_W = 64
THETA = 10000.0
C_Q, C_KV, C_PE, C_QG, C_KG, C_VG = 0, QL, QL + KVL, QL + KVL + ROPE, QL + KVL + ROPE + HG * HD, QL + KVL + ROPE + HG * HD + HKV * HD
C_GA = C_VG + HKV * HD
C_GB = C_GA + D
IN_SLABS = [(0, 192, True), (192, 192, True), (C_KV, KVL + ROPE, False), (C_KG, 2 * HKV * HD, False),
            (C_QG, 256, True), (C_QG + 256, 256, True)]
SLAB_KG = 3
ADA_PARTS, ADA_COLS = 3, 2048
RING = 6
SLOT = 2304
STEP_F = 512
STEPS = FE // STEP_F
G = 64
H = G // 2
MAXG = LAT // G
COUNT = 12
V_L = 64
V_CC, V_C, V_FIN, V_QN, V_KVN, V_GQ, V_GK = 128, 136, 144, 152, 158, 162, 164
V_ROWS = 166


def tiles_q(l):
    return [0, 1, 2, 3] if l < DEPTH - 1 else [2, 3]


def in_tiles(l):
    return [(s, t) for s, (_, _, q) in enumerate(IN_SLABS) for t in (tiles_q(l) if q else range(NT))]


_UNITS = NT * (HM + HG)
LAYER_COUNTS = dict(
    in_psum=len(in_tiles(0)), z_ready=len(in_tiles(0)), ssc_ready=2 * NT, msc_ready=1, rmsc_ready=1, msg_ready=1,
    rmsg_ready=1, c_ready=1, cT_psum=5, cT_ready=5, up_psum=4 * NT, up_taken=4 * NT, g_ready=1, gT_psum=HG + HKV,
    gT_taken=HG + HKV, qk_ready=1, qkT_psum=2 * HM, qT_taken=HM, kT_taken=HM, s_psum=_UNITS, max_ready=_UNITS,
    p_ready=_UNITS, pT_psum=_UNITS, pT_ready=_UNITS, rinv_ready=_UNITS, o_psum=_UNITS, o_ready=_UNITS, oT_psum=2 * NT,
    oT_ready=2 * NT, mg_psum=KD, sig_ready=KD, mT_ready=KD, out_psum=4 * NT, x1_added=4 * NT,
    **{f"{n}{w}": c for w in (1, 2) for n, c in (("xn_ready", NT), ("ss_ready", NT), ("ms_ready", 1), ("rms_ready", 1),
                                                 ("ht_psum", KD))},
    **{f"ht_taken{w}_{par}": KD // 2 for w in (1, 2) for par in (0, 1)},
    **{f"g{w}_{n}": 4 for w in (1, 2) for n in ("psum", "ready")})


def ada_in(s):
    done = [(part, k) for part in (1, 2) for k in range(KD)]
    per = -(-len(done) // len(IN_SLABS))
    return done[s * per:(s + 1) * per]


def ada_ffn(s):
    done = [(part, k) for part in range(ADA_PARTS) for k in range(KD)]
    return done[0 if s == 0 else 2 * s + 2:2 * s + 4]


def slab_list(a):
    out = []
    cols = lambda w, c, n: w.rearrange("(k p) n -> p k n", p=P)[:, :, c:c + n]

    def add(name, *parts):
        out.append((name, parts))

    def ada(l, part, k):
        c = part * ADA_COLS
        add("ada", a["w_ada"][l][k * P:(k + 1) * P, c:c + ADA_COLS].rearrange("p (k n) -> p k n", k=1))

    for k in range(KD):
        ada(0, 0, k)
    for l in range(DEPTH):
        for s, (c, n, _) in enumerate(IN_SLABS):
            add("in", cols(a["w_in"][l], c, n))
            if l == 0:
                for part, k in ada_in(s):
                    ada(0, part, k)
        add("qb", cols(a["mla_w_qb"][l], 0, HM * DK))
        add("kvb", cols(a["mla_w_kvb"][l], 0, HM * (NOPE + VD)))
        for jj in range(KD // 2):
            add("wo", cols(a["w_o_mla"][l], jj * 256, 256), cols(a["w_o_gqa"][l], jj * 256, 256))
            add("ga", cols(a["w_in"][l], C_GA + jj * 256, 256))
            add("gb", cols(a["w_in"][l], C_GB + jj * 256, 256))
        for s in range(4):
            add("out", cols(a["w_out"][l], s * 256, 256))
        if l == 0:
            for s in range(FT // 2):
                add("w1", cols(a["dense_w1"][0], s * 256, 256))
                add("w3", cols(a["dense_w3"][0], s * 256, 256))
                for part, k in ada_ffn(s):
                    ada(1, part, k)
            for h in range(2):
                for f in range(0, FT, 4):
                    n = min(4, FT - f)
                    add("w2", a["dense_w2"][0].rearrange("(f p) n -> p f n", p=P)[:, f:f + n, h * 512:h * 512 + 512])
    return out


def build(nc, a, out_dram):
    slabs = slab_list(a)
    n_slabs = len(slabs)

    with ExitStack() as ctx:
        def sb(name, shape, dt=F32):
            return ctx.enter_context(nc.sbuf_tensor(name, shape, dt))

        sems = {}

        def sem(name):
            if name not in sems:
                sems[name] = ctx.enter_context(nc.semaphore(name))
            return sems[name]

        def before_layer(name, l):
            return LAYER_COUNTS[name] if l else 0

        ring = [sb(f"ring{i}", [P, SLOT]) for i in range(RING)]
        x_res = sb("x_res", [P, NT, D])
        k_mem = sb("k_mem", [P, NT * HM * DK])
        with ExitStack() as under:
            def sb_under(name, shape):
                return under.enter_context(nc.sbuf_tensor(name, shape, F32))

            hT_mem = sb_under("hT_mem", [P, KD * TOK])
            z_mem = sb_under("z_mem", [P, NT * C_VG])
            q_mem = sb_under("q_mem", [P, NT * HM * DK])
            v_mla = sb_under("v_mla", [P, NT, HM * VD])
        w_parts_12 = sb("w_parts_12", [P, 2, 2, KD, P], F32R)
        hT_hi = sb("hT_hi", [P, KD, TOK], F32R)
        hT_lo = sb("hT_lo", [P, KD, TOK], F32R)
        w_parts_0 = sb("w_parts_0", [P, 1, 2, KD, P], F32R)
        over_size = 2 * KD * P * 3 + 2 * KD * TOK
        under_size = KD * TOK + NT * C_VG + NT * HM * DK + NT * HM * VD
        sb("over_rest", [P, under_size - over_size])
        v_gqa = sb("v_gqa", [P, NT, HKV * HD])
        R_mem = sb("R_mem", [P, 13312])
        view = lambda mem, off, **dims: mem[:, off:off + int(np.prod(list(dims.values())))].rearrange(
            "p (" + " ".join(dims) + ") -> p " + " ".join(dims), **dims)

        hT = view(hT_mem, 0, k=KD, t=TOK)
        z = view(z_mem, 0, t=NT, c=C_VG)
        xn = view(z_mem, 0, t=NT, c=D)
        oT = view(z_mem, 0, j=KD, t=TOK)
        q_tm = view(q_mem, 0, t=NT, c=HM * DK)
        o_tm = view(q_mem, 0, b=2, c=2 * HM * VD)
        sig = view(q_mem, 0, b=4, c=TOK)
        mg_t = view(q_mem, 4 * TOK, b=2, c=TOK)
        k_tm = view(k_mem, 0, t=NT, c=HM * DK)
        probs = view(k_mem, 0, b=2, c=TOK)
        probsT = view(k_mem, 2 * TOK, b=2, c=TOK)
        add_t = view(k_mem, 0, c=512)
        silu_t = view(k_mem, 512, b=2, c=TOK)
        qT = view(R_mem, 0, h=HM, t=TOK)
        kT = view(R_mem, 4096, h=HM, t=TOK)
        qgT = view(R_mem, 8192, h=HG, t=TOK)
        kgT = view(R_mem, 12288, h=HKV, t=TOK)
        cT = view(R_mem, 8192, j=5, t=TOK)
        junk_act = view(R_mem, 4096, c=QL)
        rope_a = view(R_mem, 0, c=(HG + HKV) * HD)
        rope_b = view(R_mem, 1024, c=(HG + HKV) * HD)
        mT = view(R_mem, 0, j=KD, t=TOK)
        gT = view(R_mem, 0, f=FT, t=TOK)
        gate_row = view(R_mem, 11264, b=2, c=D)
        SPAN = 2 * LAT + LAT
        hAll = view(R_mem, 0, k=KD, s=SPAN)
        hTe = view(R_mem, 6144, k=KD, s=LAT)
        acc = view(R_mem, 8192, t=2, c=D)
        S_all = view(R_mem, 10240, t=2, s=2 * LAT)
        CT = view(hT_mem, 0, g=MAXG, t=LAT)
        C_oh = view(hT_mem, 1024, t=2, c=2 * LAT)
        y = view(hT_mem, 2048, g=MAXG, c=512)
        silu_e = view(k_mem, 2048, b=2, c=256)
        h_e = view(k_mem, 2560, b=2, c=256)
        cmp_a = view(k_mem, 1536, t=2, c=NE * NE)
        cmp_b = view(k_mem, 1664, t=2, c=NE * NE)
        gTe = view(q_mem, 1024, b=2, i=4, s=G)
        fin_row = view(q_mem, 0, c=D)
        out_t = view(k_mem, 0, t=2, c=D)

        ident = sb("ident", [P, P])
        ones = sb("ones", [P, P])
        before = sb("before", [P, P])
        iota = sb("iota", [P, 2 * LAT])
        iota_g = sb("iota_g", [P, 2 * LAT])
        zero_b = sb("zero_b", [P, 512], mybir.dt.bfloat16)
        lower = sb("lower", [P, NE, NE])
        vec_rows = view(z_mem, 4096, i=2, c=P)
        iota_h = sb("iota_h", [P, P])
        vec = sb("vec", [P, 256])
        sc32 = sb("sc32", [P, KD, 32])
        ada_rows = view(k_mem, 2048, c=512)
        mod = sb("mod", [P, DEPTH, 48, 2])
        A1 = sb("A1", [P, DEPTH, KD, 2])
        A2 = sb("A2", [P, DEPTH, KD, 2])
        rope = sb("rope", [P, 2, 192])
        gq_row = sb("gq_row", [P, DEPTH, 2, HD])
        ss = sb("ss", [P, 8])
        rs = sb("rs", [P, 8])
        ssg = sb("ssg", [P, NT, HG + HKV])
        nmax = sb("nmax", [P, 4])
        rsum = sb("rsum", [P, 4])
        rinv = sb("rinv", [P, 4])
        router = sb("router", [P, KD, NE])
        lg = sb("lg", [P, 2, NE])
        v1 = sb("v1", [P, 2])
        rank = sb("rank", [P, 2, NE])
        ex = sb("ex", [P, 2, NE])
        den = sb("den", [P, 2])
        dinv = sb("dinv", [P, 2])
        sel = sb("sel", [P, 2, NE])
        wgt = sb("wgt", [P, 2, NE])
        pos = sb("pos", [P, 2, NE])
        pos_g = sb("pos_g", [P, MAXG, 2, NE])
        cnt = sb("cnt", [P, NE], I32)
        first = sb("first", [P, NE], I32)
        cntf = sb("cntf", [P, NE])
        offf = sb("offf", [P, NE])
        slot12 = sb("slot12", [P, 2, 2])
        ps = ctx.enter_context(nc.psum_tensor("ps", [P, 8, 512], F32))

        colv = lambda c, n=1: vec[:, c:c + n]
        tk = lambda t: slice(t * P, (t + 1) * P)
        loaded = [sem(f"slab_loaded_{i}") for i in range(RING)]
        slab_used = sem("slab_used")
        load_count = []
        tally = [0] * RING
        for i, (_, parts) in enumerate(slabs):
            tally[i % RING] += 16 * len(parts)
            load_count.append(tally[i % RING])

        def by_halves(eng, count, body, lo=1, hi=LAT // H):
            if lo == hi or lo == 2 * MAXG - 1:
                body(hi)
                return
            mid = (lo + hi) // 2
            with eng.If(count < mid * H + 1):
                by_halves(eng, count, body, lo, mid)
            with eng.Else():
                by_halves(eng, count, body, mid + 1, hi)

        def group_widths(halves):
            return [G] * (halves // 2) + [H] * (halves % 2)

        ff_slab = {n: [i for i, (name, _) in enumerate(slabs) if name == n] for n in ("w1", "w3")}

        def ff_weights(n):
            f, m = divmod(n, 2)
            i = ff_slab[("w1", "w3")[m]][f // 2]
            w = ring[i % RING][:, 0:KD * 256].rearrange("p (k n) -> p k n", k=KD)[:, :, tk(f % 2)]
            parts = w_parts_0[:, 0] if n % 3 == 0 else w_parts_12[:, n % 3 - 1]
            return i, w, parts[:, 0], parts[:, 1]

        block = ctx.enter_context(nc.Block())

        @block.sync
        def _(sp):
            for i, (name, parts) in enumerate(slabs):
                if i >= RING:
                    sp.wait_ge(slab_used, i - RING + 1)
                off = 0
                for src in parts:
                    _, k, n = src.shape
                    dst = ring[i % RING][:, off:off + k * n].rearrange("p (k n) -> p k n", k=k)
                    sp.dma_start(dst, src).then_inc(loaded[i % RING], 16)
                    off += k * n
            w1 = a["moe_w1"][0].rearrange("e (k p) n -> p (e k) n", p=P)
            w3 = a["moe_w3"][0].rearrange("e (k p) n -> p (e k) n", p=P)
            w2 = a["moe_w2"][0].rearrange("e (f p) n -> p (e f) n", p=P)
            with sp.Fori(0, NE) as e:
                with sp.Fori(0, STEPS) as s:
                    for j in range(RING):
                        slot = (n_slabs + j) % RING
                        sp.wait_ge(slab_used, (e * STEPS + s) * RING + (n_slabs + j - RING + 1))
                        if j < 4:
                            src = (w1, w3)[j // 2][:, bass.ds(e * KD + 4 * (j % 2), 4), bass.ds(s * STEP_F, STEP_F)]
                        else:
                            src = w2[:, bass.ds(e * FET + s * 4 + 2 * (j - 4), 2), :]
                        k = src.shape[1]
                        dst = ring[slot][:, 0:2048].rearrange("p (k n) -> p k n", k=k)
                        sp.dma_start(dst, src).then_inc(loaded[slot], 16)
            for t in range(2):
                sp.wait_ge(sem("out_ready"), t + 1)
                sp.dma_start(out_dram[0, t * P:(t + 1) * P, :], out_t[:, t, :]).then_inc(sem("out_stored"), 16)
            sp.wait_ge(sem("out_stored"), 32)

        @block.gpsimd
        def _(pool):
            pool.memset(ident[:, :], 0.0).then_inc(sem("const_step"), 1)
            pool.memset(ones[:, :], 1.0).then_inc(sem("const_step"), 1)
            pool.memset(before[:, :], 0.0).then_inc(sem("const_step"), 1)
            pool.memset(lower[:, :, :], 0.0).then_inc(sem("const_step"), 1)
            pool.memset(zero_b[:, :], 0.0).then_inc(sem("const_ready"), 1)
            pool.memset(sc32[:, :, :], 0.0).then_inc(sem("const_ready"), 1)
            pool.wait_ge(sem("const_step"), 4)
            pool.affine_select(out=ident[:, :], in_=ident[:, :], compare_op=ALU.not_equal, fill=1.0, base=0,
                               pattern=[[-1, P]], channel_multiplier=1).then_inc(sem("const_ready"), 1)
            pool.affine_select(out=before[:, :], in_=before[:, :], compare_op=ALU.is_ge, fill=1.0, base=0,
                               pattern=[[-1, P]], channel_multiplier=1).then_inc(sem("const_ready"), 1)
            pool.affine_select(out=lower[:, :, :], in_=lower[:, :, :], compare_op=ALU.is_ge, fill=1.0, base=0,
                               pattern=[[-1, NE], [1, NE]], channel_multiplier=0).then_inc(sem("const_ready"), 1)
            pool.iota(iota[:, :], pattern=[[1, 2 * LAT]], base=0, channel_multiplier=0,
                      allow_small_or_imprecise_dtypes=True).then_inc(sem("const_ready"), 1)
            pool.iota(iota_g[:, :], pattern=[[G, MAXG], [0, 2], [1, G]], base=0, channel_multiplier=0,
                      allow_small_or_imprecise_dtypes=True).then_inc(sem("const_ready"), 1)
            pool.iota(iota_h[:, :], pattern=[[0, P // H], [1, H]], base=0, channel_multiplier=0,
                      allow_small_or_imprecise_dtypes=True).then_inc(sem("const_ready"), 1)
            pool.wait_ge(sem("hAll_a"), KD // 2)
            pool.wait_ge(sem("hAll_v"), KD // 2)
            pool.memset(hAll[:, :, 2 * LAT:SPAN], 0.0).then_inc(sem("pad_ready"), 1)
            pool.wait_ge(sem("pad_ready"), 1)
            pool.wait_ge(sem("first_ready"), 1)
            at = pool.value_load(first[0:1, 0:1], min_val=0, max_val=2 * LAT)
            pool.tensor_copy(hTe[:, :, :], hAll[:, :, bass.ds(at, LAT)]).then_inc(sem("hTe_ready"), 1)
            with pool.Fori(1, NE) as e:
                at = pool.value_load(first[0:1, bass.ds(e, 1)], min_val=0, max_val=2 * LAT)
                pool.wait_ge(sem("y_psum"), e)
                pool.tensor_copy(hTe[:, :, :], hAll[:, :, bass.ds(at, LAT)]).then_inc(sem("hTe_ready"), 1)
        CONSTS = 8

        @block.tensor
        def _(pe):
            at = [0]

            spent = [0]

            def release(mm):
                if spent[0]:
                    mm.then_inc(slab_used, spent[0])
                    spent[0] = 0

            def slab():
                i = at[0]
                at[0] += 1
                pe.wait_ge(loaded[i % RING], load_count[i])
                views, o = [], 0
                for src in slabs[i][1]:
                    _, k, n = src.shape
                    views.append(ring[i % RING][:, o:o + k * n].rearrange("p (k n) -> p k n", k=k))
                    o += k * n
                return views if len(views) > 1 else views[0]

            def ada(l, part, k, bank):
                n = ADA_PARTS * l + part
                w = slab()
                if k == 0 and n:
                    pe.wait_ge(sem("rows_ready"), n)
                for j in range(4):
                    mm = pe.matmul(ps[32 * j:32 * j + 32, 7, :], sc32[:, k, :], w[:, 0, j * 512:j * 512 + 512],
                                   start=(k == 0), stop=(k == KD - 1))
                    if j == 0:
                        release(mm)
                spent[0] += 1
                if k == KD - 1:
                    mm.then_inc(sem("ada_psum"), 1)
                    pe.wait_ge(sem("rows_ready"), n + 1)
                    for i in range(4):
                        mm = pe.transpose(ps[:, bank, tk(i)], ada_rows[:, tk(i)], ident[:, :])
                        if i == 0:
                            release(mm)
                    mm.then_inc(sem("adaT_psum"), 1)

            def h_transpose(l, which, tiles):
                pe.wait_ge(sem(f"xn_ready{which}"), before_layer(f"xn_ready{which}", l) + len(tiles))
                for k in range(KD):
                    if k >= 4:
                        pe.wait_ge(sem(f"ht_taken{which}_{k % 2}"), before_layer(f"ht_taken{which}_{k % 2}", l) + (k - 4) // 2 + 1)
                    for t in tiles:
                        mm = pe.transpose(ps[:, k % 4, tk(t)], xn[:, t, tk(k)], ident[:, :])
                        if t != tiles[-1]:
                            release(mm)
                    mm.then_inc(sem(f"ht_psum{which}"), 1)
                for par in range(2):
                    pe.wait_ge(sem(f"ht_taken{which}_{par}"), before_layer(f"ht_taken{which}_{par}", l) + KD // 2)

            def rows(l, col, banks, name):
                for b, (c, kk) in zip(banks, [(c, kk) for c in col for kk in range(2)]):
                    for k in range(4):
                        mm = pe.matmul(ps[:, b, tk(k)], c(4 * kk + k).to_broadcast([P, P]), ident[:, :],
                                       start=True, stop=True)
                        if k == 0:
                            release(mm)
                    mm.then_inc(sem(f"{name}_psum"), 1)

            pe.wait_ge(sem("const_ready"), CONSTS)
            pe.wait_ge(sem("vec_loaded_a"), 16)
            pe.wait_ge(sem("vec_loaded_b"), 16)
            pe.transpose(ps[:, 0, 0:P], vec_rows[:, 0, :], ident[:, :])
            pe.transpose(ps[:, 0, P:V_ROWS], vec_rows[0:V_ROWS - P, 1, :], ident[0:V_ROWS - P, 0:V_ROWS - P])\
              .then_inc(sem("vec_psum"), 1)
            pe.wait_ge(sem("vec_ready"), 1)
            for l in range(DEPTH):
                for m, c in enumerate((V_GQ + l, V_GK + l)):
                    mm = pe.matmul(ps[:, 1, (2 * l + m) * HD:(2 * l + m + 1) * HD], colv(c).to_broadcast([P, P])[0:HD, :],
                                   ident[0:HD, 0:HD], start=True, stop=True)
            mm.then_inc(sem("gq_psum"), 1)
            pe.wait_ge(sem("gq_ready"), 1)

            for k in range(KD):
                ada(0, 0, k, 3)
            pe.wait_ge(sem("mod_ready"), 1)
            for l in range(DEPTH):
                tq = tiles_q(l)
                q0 = tq[0] * P
                nq = len(tq) * P
                h_transpose(l, 1, range(NT))

                n = -1
                for s, (c, cols, q) in enumerate(IN_SLABS):
                    w = slab()
                    for t in (tq if q else range(NT)):
                        n += 1
                        if n >= 3:
                            pe.wait_ge(sem("z_ready"), before_layer("z_ready", l) + n - 2)
                        for k in range(KD):
                            mm = pe.matmul(ps[:, 4 + n % 3, 0:cols], hT[:, k, tk(t)], w[:, k, :],
                                           start=(k == 0), stop=(k == KD - 1))
                            if k == 0:
                                release(mm)
                        mm.then_inc(sem("in_psum"), 1)
                    spent[0] += 1
                    if l == 0:
                        for part, k in ada_in(s):
                            ada(0, part, k, 3)
                if l == 0:
                    pe.wait_ge(sem("mod_ready"), ADA_PARTS)

                pe.wait_ge(sem("c_ready"), before_layer("c_ready", l) + 1)
                for j in range(5):
                    if j == 4:
                        pe.wait_ge(sem("cT_ready"), before_layer("cT_ready", l) + 1)
                    for t in (tq if j < 3 else range(NT)):
                        mm = pe.transpose(ps[:, j % 4, tk(t)], z[:, t, tk(j)], ident[:, :])
                        if t != NT - 1:
                            release(mm)
                    mm.then_inc(sem("cT_psum"), 1)
                pe.wait_ge(sem("cT_ready"), before_layer("cT_ready", l) + 5)
                pe.wait_ge(sem("z_ready"), before_layer("z_ready", l) + len(in_tiles(l)))
                n = -1
                w = slab()
                for t in tq:
                    for h in range(2):
                        n += 1
                        if n >= 4:
                            pe.wait_ge(sem("up_taken"), before_layer("up_taken", l) + n - 3)
                        for k in range(3):
                            mm = pe.matmul(ps[:, 4 + n % 4, 0:384], cT[:, k, tk(t)], w[:, k, h * 384:h * 384 + 384],
                                           start=(k == 0), stop=(k == 2))
                        mm.then_inc(sem("up_psum"), 1)
                spent[0] += 1
                w = slab()
                for t in range(NT):
                    for h in range(2):
                        n += 1
                        pe.wait_ge(sem("up_taken"), before_layer("up_taken", l) + n - 3)
                        for k in range(2):
                            mm = pe.matmul(ps[:, 4 + n % 4, :], cT[:, 3 + k, tk(t)], w[:, k, h * 512:h * 512 + 512],
                                           start=(k == 0), stop=(k == 1))
                            if k == 0:
                                release(mm)
                        mm.then_inc(sem("up_psum"), 1)
                spent[0] += 1

                pe.wait_ge(sem("g_ready"), before_layer("g_ready", l) + 1)
                for m in range(HG + HKV):
                    if m >= 4:
                        pe.wait_ge(sem("gT_taken"), before_layer("gT_taken", l) + m - 3)
                    for t in (tq if m < HG else range(NT)):
                        mm = pe.transpose(ps[0:HD, m % 4, tk(t)], z[:, t, C_QG + m * HD:C_QG + (m + 1) * HD], ident[:, :])
                        if t != NT - 1:
                            release(mm)
                    mm.then_inc(sem("gT_psum"), 1)
                pe.wait_ge(sem("gT_taken"), before_layer("gT_taken", l) + HG + HKV)
                pe.wait_ge(sem("qk_ready"), before_layer("qk_ready", l) + 1)
                pe.wait_ge(sem("up_taken"), before_layer("up_taken", l) + 2 * (len(tq) + NT))
                for m in range(2 * HM):
                    if m >= 4:
                        pe.wait_ge(sem(("qT_taken", "kT_taken")[m % 2]), before_layer(("qT_taken", "kT_taken")[m % 2], l) + (m - 4) // 2 + 1)
                    src = (q_tm, k_tm)[m % 2]
                    for t in (tq if m % 2 == 0 else range(NT)):
                        mm = pe.transpose(ps[0:DK, m % 4, tk(t)], src[:, t, (m // 2) * DK:(m // 2 + 1) * DK], ident[:, :])
                    mm.then_inc(sem("qkT_psum"), 1)
                pe.wait_ge(sem("qT_taken"), before_layer("qT_taken", l) + HM)
                pe.wait_ge(sem("kT_taken"), before_layer("kT_taken", l) + HM)

                units = [(qi, h) for qi in range(len(tq)) for h in range(HM + HG)]
                keys = lambda qi: CTX if tq[qi] < CTX // P else TOK
                for i in range(len(units) + 4):
                    if i < len(units):
                        qi, h = units[i]
                        nk = keys(qi)
                        if i >= 3:
                            pe.wait_ge(sem("p_ready"), before_layer("p_ready", l) + i - 2)
                        if h < HM:
                            pe.matmul(ps[:, i % 3, 0:nk], qT[0:DK, h, tk(tq[qi])], kT[0:DK, h, 0:nk],
                                      start=True, stop=True).then_inc(sem("s_psum"), 1)
                        else:
                            pe.matmul(ps[:, i % 3, 0:nk], qgT[0:HD, h - HM, tk(tq[qi])],
                                      kgT[0:HD, (h - HM) // (HG // HKV), 0:nk],
                                      start=True, stop=True).then_inc(sem("s_psum"), 1)
                    j = i - 2
                    if 0 <= j < len(units):
                        pe.wait_ge(sem("p_ready"), before_layer("p_ready", l) + j + 1)
                        if j >= 2:
                            pe.wait_ge(sem("pT_ready"), before_layer("pT_ready", l) + j - 1)
                        for kt in range(keys(units[j][0]) // P):
                            mm = pe.transpose(ps[:, 3 + j % 2, tk(kt)], probs[:, j % 2, tk(kt)], ident[:, :])
                        mm.then_inc(sem("pT_psum"), 1)
                    j = i - 3
                    if 0 <= j < len(units):
                        qi, h = units[j]
                        pe.wait_ge(sem("pT_ready"), before_layer("pT_ready", l) + j + 1)
                        if j >= 2:
                            pe.wait_ge(sem("o_ready"), before_layer("o_ready", l) + j - 1)
                        nkt = keys(qi) // P
                        for kt in range(nkt):
                            v = (v_mla[:, kt, h * VD:(h + 1) * VD] if h < HM else
                                 v_gqa[:, kt, (h - HM) // (HG // HKV) * HD:((h - HM) // (HG // HKV) + 1) * HD])
                            mm = pe.matmul(ps[:, 5 + j % 2, 0:VD], probsT[:, j % 2, tk(kt)], v,
                                           start=(kt == 0), stop=(kt == nkt - 1))
                        mm.then_inc(sem("o_psum"), 1)
                    j = i - 4
                    if 0 <= j < len(units) and units[j][1] == HM + HG - 1:
                        qi = units[j][0]
                        pe.wait_ge(sem("o_ready"), before_layer("o_ready", l) + j + 1)
                        for half in range(2):
                            r = 2 * qi + half
                            if r >= 1:
                                pe.wait_ge(sem("oT_ready"), before_layer("oT_ready", l) + r)
                            for k in range(4):
                                mm = pe.transpose(ps[:, 7, tk(k)], o_tm[:, qi % 2, tk(4 * half + k)], ident[:, :])
                            mm.then_inc(sem("oT_psum"), 1)
                pe.wait_ge(sem("oT_ready"), before_layer("oT_ready", l) + 2 * len(tq))

                for jj in range(KD // 2):
                    wa, wb = slab()
                    wga, wgb = slab(), slab()
                    for j in (2 * jj, 2 * jj + 1):
                        b = 4 * (j % 2)
                        c = (j % 2) * P
                        if j >= 2:
                            pe.wait_ge(sem("mT_ready"), before_layer("mT_ready", l) + j - 1)
                        for m, w in enumerate((wa, wb)):
                            for k in range(4):
                                mm = pe.matmul(ps[:, b + m, 0:nq], w[:, k, c:c + P], oT[:, 4 * m + k, q0:TOK],
                                               start=(k == 0), stop=(k == 3))
                                if k == 0:
                                    release(mm)
                        for m, w in enumerate((wga, wgb)):
                            for k in range(KD):
                                mm = pe.matmul(ps[:, b + 2 + m, 0:nq], w[:, k, c:c + P], hT[:, k, q0:TOK],
                                               start=(k == 0), stop=(k == KD - 1))
                        mm.then_inc(sem("mg_psum"), 1)
                    spent[0] += 3
                pe.wait_ge(sem("mT_ready"), before_layer("mT_ready", l) + KD - 1)
                rows(l, [lambda k, c=c: mod[:, l, 16 + k, c:c + 1] for c in range(2)], range(4), "g1")
                pe.wait_ge(sem("mT_ready"), before_layer("mT_ready", l) + KD)
                n = -1
                for s in range(4):
                    w = slab()
                    for t in tq:
                        n += 1
                        if n >= 4:
                            pe.wait_ge(sem("x1_added"), before_layer("x1_added", l) + n - 3)
                        for k in range(KD):
                            mm = pe.matmul(ps[:, 4 + n % 4, 0:256], mT[:, k, tk(t)], w[:, k, :],
                                           start=(k == 0), stop=(k == KD - 1))
                            if k == 0:
                                release(mm)
                        mm.then_inc(sem("out_psum"), 1)
                    spent[0] += 1
                pe.wait_ge(sem("x1_added"), before_layer("x1_added", l) + n + 1)
                h_transpose(l, 2, tq)
                rows(l, [lambda k, c=c: mod[:, l, 40 + k, c:c + 1] for c in range(2)], range(4, 8), "g2")

                if l == 0:
                    for s in range(FT // 2):
                        slab(), slab()
                        for j in range(2):
                            f = 2 * s + j
                            b = 2 * (f % 2)
                            if f >= 2:
                                pe.wait_ge(sem("gT_ready"), f - 1)
                            for m in range(2):
                                _, _, w_hi, w_lo = ff_weights(2 * f + m)
                                pe.wait_ge(sem("w_split"), 2 * f + m + 1)
                                for k in range(KD):
                                    if f == 0 and m == 0:
                                        pe.wait_ge(sem("h_split"), k + 1)
                                    mm = pe.matmul(ps[:, b + m, :], w_hi[:, k, :], hT_hi[:, k, :], start=(k == 0), stop=False)
                                    if k == 0:
                                        release(mm)
                                    pe.matmul(ps[:, b + m, :], w_hi[:, k, :], hT_lo[:, k, :], start=False, stop=False)
                                    mm = pe.matmul(ps[:, b + m, :], w_lo[:, k, :], hT_hi[:, k, :],
                                                   start=False, stop=(k == KD - 1))
                                mm.then_inc(sem("ff_psum"), 1)
                        spent[0] += 2
                        if s == 0:
                            pe.wait_ge(sem("g2_ready"), 4)
                        for part, k in ada_ffn(s):
                            ada(1, part, k, 6)
                    pe.wait_ge(sem("gT_ready"), FT)
                    pe.wait_ge(sem("mod_ready"), 2 * ADA_PARTS)
                    for h in range(2):
                        b = 4 if h == 0 else 0
                        for f0 in range(0, FT, 4):
                            w = slab()
                            for f in range(f0, min(f0 + 4, FT)):
                                for t in range(NT):
                                    mm = pe.matmul(ps[:, b + t, :], gT[:, f, tk(t)], w[:, f - f0, :],
                                                   start=(f == 0), stop=(f == FT - 1))
                                    if t == 0:
                                        release(mm)
                            spent[0] += 1
                        mm.then_inc(sem("dn_psum"), 1)

            pe.wait_ge(sem("router_loaded"), 16)
            for t in range(2):
                for k in range(KD):
                    mm = pe.matmul(ps[:, 0, t * NE:(t + 1) * NE], hT[:, k, tk(2 + t)], router[:, k, :],
                                   start=(k == 0), stop=(k == KD - 1))
                    release(mm) if k == 0 else None
            mm.then_inc(sem("lg_psum"), 1)
            rows(0, [lambda k: colv(V_FIN + k)], range(1, 3), "fin")
            pe.wait_ge(sem("sel_ready"), 1)
            pe.matmul(ps[:, 3, 0:NE], before[:, :], sel[:, 0, 0:NE], start=True, stop=True)
            pe.matmul(ps[:, 3, NE:2 * NE], ones[:, :], sel[:, 0, 0:NE], start=True, stop=False)
            pe.matmul(ps[:, 3, NE:2 * NE], before[:, :], sel[:, 1, 0:NE], start=False, stop=True)
            pe.matmul(ps[:, 3, 2 * NE:3 * NE], ones[:, :], sel[:, 0, 0:NE], start=True, stop=False)
            pe.matmul(ps[:, 3, 2 * NE:3 * NE], ones[:, :], sel[:, 1, 0:NE], start=False, stop=True)\
              .then_inc(sem("pos_psum"), 1)
            pe.wait_ge(sem("g2_ready"), 8)
            pe.wait_ge(sem("fin_ready"), 2)
            pe.wait_ge(sem("S_ready"), 1)
            for k in range(KD):
                if k >= 4:
                    pe.wait_ge(sem(("hAll_a", "hAll_v")[k % 2]), (k - 4) // 2 + 1)
                for t in range(2):
                    mm = pe.matmul(ps[:, 4 + k % 4, :], xn[:, 2 + t, tk(k)], S_all[:, t, :], start=(t == 0), stop=(t == 1))
                mm.then_inc(sem("hAll_psum"), 1)
            pe.wait_ge(sem("hAll_a"), KD // 2)
            pe.wait_ge(sem("hAll_v"), KD // 2)
            for b in range(2, 6):
                pe.matmul(ps[:, b, :], zero_b[:, 0:P], zero_b[:, :], start=True, stop=True)

            def expert(e, halves):
                widths = group_widths(halves)
                ng = len(widths)
                inc = COUNT // ng
                for g in range(ng + halves % 2):
                    pe.matmul(ps[:, 2 + g, :], zero_b[:, 0:P], zero_b[:, :], start=True, stop=True)
                with pe.Fori(0, STEPS) as s:
                    it = pe.snap(e * STEPS + s)

                    def arrived(j):
                        slot = (n_slabs + j) % RING
                        pe.wait_ge(loaded[slot], it * 16 + (tally[slot] + 16))
                        return ring[slot]

                    def up(g):
                        width = widths[g]
                        n = width * STEP_F // P
                        for m in range(2):
                            for k in range(KD):
                                if g == 0 and k % 4 == 0:
                                    arrived(2 * m + k // 4)
                                w = ring[(n_slabs + 2 * m + k // 4) % RING][:, 0:2048].rearrange("p (k n) -> p k n", k=4)
                                for c in range(P // width):
                                    mm = pe.matmul(ps[width * c:width * c + width, g % 2, m * n:m * n + n],
                                                   hTe[:, k, g * G:g * G + width], w[:, k % 4, c * n:c * n + n],
                                                   start=(k == 0), stop=(k == KD - 1))
                                    if m == 1 and k == 0 and c == 0 and g == ng - 1:
                                        mm.then_inc(slab_used, 2)
                        mm.then_inc(sem("upe_psum"), inc)

                    def turn(g):
                        pe.wait_ge(sem("he_ready"), it * COUNT + inc * (g + 1))
                        for i in range(widths[g] // H):
                            mm = pe.transpose(ps[:, 6 + g % 2, tk(i)], h_e[:, g % 2, tk(i)], ident[:, :])
                            if i == 0 and g == ng - 1 and widths[g] == G:
                                mm.then_inc(slab_used, 2)
                        mm.then_inc(sem("gTe_psum"), inc)

                    def down(g):
                        width = widths[g]
                        pe.wait_ge(sem("gTe_ready"), it * COUNT + inc * (g + 1))
                        wf = [ring[(n_slabs + 4 + f // 2) % RING][:, f % 2 * D:f % 2 * D + D] for f in range(4)]
                        if width == G:
                            for f in range(4):
                                if g == 0 and f % 2 == 0:
                                    arrived(4 + f // 2)
                                for half in range(2):
                                    mm = pe.matmul(ps[G * half:G * half + G, 2 + g, :], gTe[:, g % 2, 2 * (f % 2) + f // 2, :],
                                                   wf[f][:, half * 512:half * 512 + 512], start=False, stop=False,
                                                   skip_group_check=True)
                        else:
                            if g == 0:
                                arrived(4)
                                arrived(5)
                            for half in range(2):
                                for f in range(4):
                                    mm = pe.matmul(ps[H * f:H * f + H, 2 + g + half, :], gTe[:, g % 2, f, 0:H],
                                                   wf[f][:, half * 512:half * 512 + 512], start=False, stop=False,
                                                   skip_group_check=True)
                                    if f == 0 and half == 0:
                                        mm.then_inc(slab_used, 2)
                        if g == ng - 1:
                            mm.then_inc(slab_used, 2)

                    up(0)
                    for g in range(ng):
                        if g + 1 < ng:
                            up(g + 1)
                        turn(g)
                        down(g)
                pe.wait_ge(sem("C_ready"), e + 1)
                for g in range(MAXG):
                    for t in range(2):
                        mm = pe.transpose(ps[:, g // 2, (g % 2) * LAT + t * P:(g % 2) * LAT + (t + 1) * P],
                                          C_oh[:, t, tk(g)], ident[:, :])
                        if g == 0 and t == 0:
                            mm.then_inc(sem("y_psum"), 1)
                    if g % 2 == 1:
                        mm.then_inc(sem("CT_psum"), 1)
                pe.wait_ge(sem("y_ready_a"), e * 3 + 3)
                pe.wait_ge(sem("y_ready_v"), e * 3 + 3)
                for t in range(2):
                    for half in range(2):
                        out = ps[:, (6, 0)[t] + half, :]
                        for g, width in enumerate(widths):
                            if width == G:
                                mm = pe.matmul(out, CT[G * half:G * half + G, g, tk(t)], y[G * half:G * half + G, g, :],
                                               start=(g == 0), stop=(g == ng - 1))
                            else:
                                mm = pe.matmul(out, CT[:, g, tk(t)], y[:, g + half, :], start=(g == 0), stop=True)
                    mm.then_inc(sem("sc_psum"), 1)
                pe.wait_ge(sem("acc_added"), e * 4 + 4)

            with pe.Fori(0, NE) as e:
                count = pe.value_load(cnt[0:1, bass.ds(e, 1)], min_val=0, max_val=LAT)
                pe.wait_ge(sem("hTe_ready"), e + 1)
                by_halves(pe, count, lambda halves: expert(e, halves))

        @block.scalar
        def _(act):
            act.dma_start(vec_rows[:, 0, :], a["vecs"][0:P, :]).then_inc(sem("vec_loaded_a"), 16)
            act.dma_start(vec_rows[0:V_ROWS - P, 1, :], a["vecs"][P:V_ROWS, :]).then_inc(sem("vec_loaded_b"), 16)
            act.dma_start(x_res[:, 0:2, :], a["ctx"][0].rearrange("(t p) d -> p t d", p=P)).then_inc(sem("ctx_loaded"), 16)
            act.dma_start(x_res[:, 2:4, :], a["x"][0].rearrange("(t p) d -> p t d", p=P)).then_inc(sem("x_loaded"), 16)
            act.dma_start(rope[:, :, :], a["rope"].rearrange("(t p) d -> p t d", p=P)).then_inc(sem("rope_loaded"), 16)
            act.dma_start(router[:, :, :], a["moe_router"][0].rearrange("(k p) n -> p k n", p=P))\
               .then_inc(sem("router_loaded"), 16)

            def squares(l, which, tiles):
                for i, t in enumerate(tiles):
                    act.activation(xn[:, t, :], x_res[:, t, :], ACT.Square, accum_out=ss[:, i:i + 1])\
                       .then_inc(sem(f"ss_ready{which}"), 1)
                act.wait_ge(sem(f"ms_ready{which}"), before_layer(f"ms_ready{which}", l) + 1)
                act.activation(rs[:, 0:len(tiles)], ss[:, 0:len(tiles)], ACT.Sqrt).then_inc(sem(f"rms_ready{which}"), 1)

            def modulate(l, which, tiles, A, sh):
                for k in range(0, KD, 2):
                    act.wait_ge(sem(f"ht_psum{which}"), before_layer(f"ht_psum{which}", l) + k + 1)
                    for c in ((0, 1) if 0 in tiles else (1,)):
                        ins = act.activation(hT[:, k, c * CTX:(c + 1) * CTX], ps[:, k % 4, c * CTX:(c + 1) * CTX],
                                             ACT.Identity, scale=A[:, l, k, c:c + 1], bias=mod[:, l, sh + k, c:c + 1])
                    ins.then_inc(sem(f"ht_taken{which}_0"), 1)

            def rows(l, n, bank0, name, dst):
                for b in range(n):
                    act.wait_ge(sem(f"{name}_psum"), 4 * l + b + 1)
                    act.activation(dst(b), ps[:, bank0 + b, :], ACT.Copy).then_inc(sem(f"{name}_ready"), 1)

            n_sq = [0]
            act.wait_ge(sem("vec_done"), 1)
            act.wait_ge(sem("const_ready"), CONSTS)
            act.activation(sc32[:, :, 0:2], vec[:, V_CC:V_CC + 16].rearrange("p (c k) -> p k c", c=2), ACT.Silu)\
               .then_inc(sem("vec_ready"), 1)
            act.wait_ge(sem("ctx_loaded"), 16)
            act.wait_ge(sem("x_loaded"), 16)
            for l in range(DEPTH):
                tq = tiles_q(l)
                nq = len(tq) * P
                if l > 0:
                    act.wait_ge(sem("dn_added"), 2)
                squares(l, 1, range(NT))
                act.wait_ge(sem("mod_ready"), ADA_PARTS * l + 1)
                modulate(l, 1, range(NT), A1, 0)
                n = -1
                for s, (c, cols, q) in enumerate(IN_SLABS):
                    for t in (tq if q else range(NT)):
                        n += 1
                        act.wait_ge(sem("in_psum"), before_layer("in_psum", l) + n + 1)
                        if s == SLAB_KG:
                            act.activation(v_gqa[:, t, :], ps[:, 4 + n % 3, P:2 * P], ACT.Copy)
                            cols = P
                        act.activation(z[:, t, c:c + cols], ps[:, 4 + n % 3, 0:cols], ACT.Copy)\
                           .then_inc(sem("z_ready"), 1)
                    if s == 2:
                        act.wait_ge(sem("z_ready"), before_layer("z_ready", l) + n + 1)
                        for t in tq:
                            act.activation(junk_act[:, 0:QL], z[:, t, C_Q:C_Q + QL], ACT.Square,
                                           accum_out=ss[:, t:t + 1]).then_inc(sem("ssc_ready"), 1)
                            n_sq[0] += 1
                            act.wait_ge(sem("ssc_ready"), n_sq[0])
                        for t in range(NT):
                            act.activation(junk_act[:, 0:KVL], z[:, t, C_KV:C_KV + KVL], ACT.Square,
                                           accum_out=ss[:, 4 + t:5 + t]).then_inc(sem("ssc_ready"), 1)
                            n_sq[0] += 1
                            act.wait_ge(sem("ssc_ready"), n_sq[0])
                act.wait_ge(sem("msc_ready"), before_layer("msc_ready", l) + 1)
                act.activation(rs[:, tq[0]:8], ss[:, tq[0]:8], ACT.Sqrt).then_inc(sem("rmsc_ready"), 1)
                act.wait_ge(sem("msg_ready"), before_layer("msg_ready", l) + 1)
                act.activation(ssg[:, :, :], ssg[:, :, :], ACT.Sqrt).then_inc(sem("rmsg_ready"), 1)
                n = -1
                for t in tq:
                    for h in range(2):
                        n += 1
                        act.wait_ge(sem("up_psum"), before_layer("up_psum", l) + n + 1)
                        act.activation(q_tm[:, t, h * 384:h * 384 + 384], ps[:, 4 + n % 4, 0:384], ACT.Copy)\
                           .then_inc(sem("up_taken"), 1)
                for t in range(NT):
                    for h in range(2):
                        n += 1
                        act.wait_ge(sem("up_psum"), before_layer("up_psum", l) + n + 1)
                        src = ps[:, 4 + n % 4, :].rearrange("p (h c) -> p h c", h=4)
                        act.activation(k_tm[:, t, :].rearrange("p (h c) -> p h c", h=HM)[:, 4 * h:4 * h + 4, 0:NOPE],
                                       src[:, :, 0:NOPE], ACT.Copy)
                        act.activation(v_mla[:, t, h * 256:h * 256 + 256].rearrange("p (h c) -> p h c", h=4),
                                       src[:, :, NOPE:NOPE + VD], ACT.Copy).then_inc(sem("up_taken"), 1)
                for m in range(HG + HKV):
                    act.wait_ge(sem("gT_psum"), before_layer("gT_psum", l) + m + 1)
                    if m < HG:
                        act.activation(qgT[0:HD, m, tq[0] * P:TOK], ps[0:HD, m % 4, tq[0] * P:TOK], ACT.Copy,
                                       scale=GQA_SCALE).then_inc(sem("gT_taken"), 1)
                    else:
                        act.activation(kgT[0:HD, m - HG, :], ps[0:HD, m % 4, :], ACT.Copy).then_inc(sem("gT_taken"), 1)
                for h in range(HM):
                    act.wait_ge(sem("qkT_psum"), before_layer("qkT_psum", l) + 2 * h + 1)
                    act.activation(qT[0:DK, h, tq[0] * P:TOK], ps[0:DK, (2 * h) % 4, tq[0] * P:TOK], ACT.Copy,
                                   scale=MLA_SCALE).then_inc(sem("qT_taken"), 1)
                n_units = len(tq) * (HM + HG)
                for i in range(n_units):
                    qi = i // (HM + HG)
                    nk = CTX if tq[qi] < CTX // P else TOK
                    act.wait_ge(sem("max_ready"), before_layer("max_ready", l) + i + 1)
                    if i >= 2:
                        act.wait_ge(sem("pT_psum"), before_layer("pT_psum", l) + i - 1)
                    act.activation(probs[:, i % 2, 0:nk], ps[:, i % 3, 0:nk], ACT.Exp, bias=nmax[:, i % 4:i % 4 + 1],
                                   accum_out=rsum[:, i % 4:i % 4 + 1]).then_inc(sem("p_ready"), 1)
                    for qi in range(len(tq)):
                        if i == min((qi + 1) * (HM + HG) + 3, n_units - 1 if qi == len(tq) - 1 else n_units):
                            for half in range(2):
                                act.wait_ge(sem("oT_psum"), before_layer("oT_psum", l) + 2 * qi + half + 1)
                                act.activation(oT[:, 4 * half:4 * half + 4, tk(tq[qi])],
                                               ps[:, 7, :].rearrange("p (k t) -> p k t", k=4), ACT.Copy)\
                                   .then_inc(sem("oT_ready"), 1)
                for j in range(KD):
                    act.wait_ge(sem("mg_psum"), before_layer("mg_psum", l) + j + 1)
                    if j >= 2:
                        act.wait_ge(sem("mT_ready"), before_layer("mT_ready", l) + j - 1)
                    for m in range(2):
                        ins = act.activation(sig[:, 2 * (j % 2) + m, 0:nq], ps[:, 4 * (j % 2) + 2 + m, 0:nq], ACT.Sigmoid)
                    ins.then_inc(sem("sig_ready"), 1)
                rows(l, 4, 0, "g1", lambda b: gate_row[:, b // 2, (b % 2) * 512:(b % 2) * 512 + 512])
                act.wait_ge(sem("x1_added"), before_layer("x1_added", l) + 4 * len(tq))
                squares(l, 2, tq)
                act.wait_ge(sem("mod_ready"), ADA_PARTS * l + 3)
                modulate(l, 2, tq, A2, 24)
                rows(l, 4, 4, "g2", lambda b: gate_row[:, b // 2, (b % 2) * 512:(b % 2) * 512 + 512])
                if l == 0:
                    def weights_hi(n):
                        i, w, w_hi, _ = ff_weights(n)
                        act.wait_ge(loaded[i % RING], load_count[i])
                        if n in (1, 2):
                            act.wait_ge(sem("h_split"), KD)
                        act.activation(w_hi, w, ACT.Copy).then_inc(sem("w_hi_ready"), 1)

                    act.wait_ge(sem("ht_psum2"), KD)
                    weights_hi(0)
                    for k in range(KD):
                        act.wait_ge(sem(f"ht_taken2_{k % 2}"), k // 2 + 1)
                        act.activation(hT_hi[:, k, :], hT[:, k, :], ACT.Copy).then_inc(sem("h_hi_ready"), 1)
                    weights_hi(1)
                    weights_hi(2)
                    for f in range(FT):
                        act.wait_ge(sem("ff_psum"), 2 * f + 1)
                        if f >= 2:
                            act.wait_ge(sem("gT_ready"), f - 1)
                        act.activation(silu_t[:, f % 2, :], ps[:, 2 * (f % 2), :], ACT.Silu).then_inc(sem("silu_ready"), 1)
                        for m in range(2):
                            if 2 * f + m + 3 < 2 * FT:
                                act.wait_ge(sem("ff_psum"), 2 * f + m + 1)
                                weights_hi(2 * f + m + 3)

            rows(0, 2, 1, "fin", lambda b: fin_row[:, b * 512:b * 512 + 512])
            act.wait_ge(sem("lgm_ready"), 1)
            act.activation(ex[:, :, :], ex[:, :, :], ACT.Exp).then_inc(sem("ex_ready"), 1)

            act.wait_ge(sem("mod_ready"), 2 * ADA_PARTS)
            for k in range(0, KD, 2):
                act.wait_ge(sem("hAll_psum"), k + 1)
                act.activation(hAll[:, k, 0:2 * LAT], ps[:, 4 + k % 4, :], ACT.Identity, scale=A2[:, 1, k, 1:2],
                               bias=mod[:, 1, 24 + k, 1:2]).then_inc(sem("hAll_a"), 1)

            def expert_groups(e, halves):
                widths = group_widths(halves)
                ng = len(widths)
                inc = COUNT // ng
                with act.Fori(0, STEPS) as s:
                    it = act.snap(e * STEPS + s)

                    def gate(g):
                        act.wait_ge(sem("upe_psum"), it * COUNT + inc * (g + 1))
                        n = widths[g] * STEP_F // P
                        act.activation(silu_e[:, g % 2, 0:n], ps[:, g % 2, 0:n], ACT.Silu).then_inc(sem("silu_e_ready"), inc)

                    gate(0)
                    for g in range(ng):
                        if g + 1 < ng:
                            gate(g + 1)
                        act.wait_ge(sem("gTe_psum"), it * COUNT + inc * (g + 1))
                        act.activation(gTe[:, g % 2, :, 0:widths[g]],
                                       ps[:, 6 + g % 2, 0:4 * widths[g]].rearrange("p (i s) -> p i s", i=4),
                                       ACT.Copy).then_inc(sem("gTe_ready"), inc)

            with act.Fori(0, NE) as e:
                count = act.value_load(cnt[0:1, bass.ds(e, 1)], min_val=0, max_val=LAT)
                by_halves(act, count, lambda halves: expert_groups(e, halves))
                act.wait_ge(sem("y_psum"), e + 1)
                for g in (0, 1):
                    act.activation(y[:, g, :], ps[:, 2 + g, :], ACT.Copy).then_inc(sem("y_ready_a"), 1)
                act.wait_ge(sem("CT_psum"), e * 2 + 1)
                act.activation(CT[:, 0:2, :], ps[:, 0, :].rearrange("p (g t) -> p g t", g=2), ACT.Copy)\
                   .then_inc(sem("y_ready_a"), 1)
            for t in range(2):
                act.wait_ge(sem("xf_ready"), t + 1)
                act.activation(xn[:, t, :].rearrange("p (a b) -> p a b", a=2), x_res[:, 2 + t, :].rearrange("p (a b) -> p a b", a=2),
                               ACT.Square, accum_out=ss[:, t:t + 1]).then_inc(sem("ssf_ready"), 1)
            act.wait_ge(sem("msf_ready"), 1)
            act.activation(rs[:, 0:2], ss[:, 0:2], ACT.Sqrt).then_inc(sem("rmsf_ready"), 1)

        @block.vector
        def _(dve):
            steps = [0]

            def then(ins):
                steps[0] += 1
                ins.then_inc(sem("dve_step"), 1)
                dve.wait_ge(sem("dve_step"), steps[0])

            def bc(ap, shape):
                return ap.to_broadcast(shape)

            def norm(l, which, tiles):
                n = len(tiles)
                dve.wait_ge(sem(f"ss_ready{which}"), before_layer(f"ss_ready{which}", l) + n)
                dve.tensor_scalar(ss[:, 0:n], ss[:, 0:n], 1.0 / D, EPS, ALU.mult, ALU.add)\
                   .then_inc(sem(f"ms_ready{which}"), 1)
                dve.wait_ge(sem(f"rms_ready{which}"), before_layer(f"rms_ready{which}", l) + 1)
                then(dve.reciprocal(rs[:, 0:n], rs[:, 0:n]))
                for i, t in enumerate(tiles):
                    dve.tensor_scalar(xn[:, t, :], x_res[:, t, :], rs[:, i:i + 1], None, ALU.mult)\
                       .then_inc(sem(f"xn_ready{which}"), 1)

            def ada(l, part, bank):
                n = ADA_PARTS * l + part
                dve.wait_ge(sem("ada_psum"), n + 1)
                if n:
                    dve.wait_ge(sem("adaT_psum"), n)
                dve.tensor_copy(ada_rows[:, :], ps[:, 7, :]).then_inc(sem("rows_ready"), 1)
                dve.wait_ge(sem("adaT_psum"), n + 1)
                t0 = 16 * part
                into = mod[:, l, t0:t0 + 16, :].rearrange("p (j i) c -> p i j c", j=4)
                src = ps[:, bank, :].rearrange("p (i j r) -> p i j r", i=4, j=4)[:, :, :, 0:2]
                bias = vec[:, l * V_L + t0:l * V_L + t0 + 16].rearrange("p (j i) -> p i j", j=4)
                last = dve.tensor_tensor(into, src, bc(bias.unsqueeze(3), [P, 4, 4, 2]), ALU.add)
                if part != 1:
                    then(last)
                    A, at, g = (A1, 8, 48) if part == 0 else (A2, 32, 56)
                    last = dve.scalar_tensor_tensor(A[:, l, :, :], mod[:, l, at:at + KD, :], 1.0,
                                                    bc(vec[:, l * V_L + g:l * V_L + g + KD].unsqueeze(2), [P, KD, 2]),
                                                    ALU.add, ALU.mult)
                last.then_inc(sem("mod_ready"), 1)

            def modulate(l, which, tiles, A, sh):
                dve.wait_ge(sem("mod_ready"), ADA_PARTS * l + (1 if which == 1 else 3))
                for k in range(1, KD, 2):
                    dve.wait_ge(sem(f"ht_psum{which}"), before_layer(f"ht_psum{which}", l) + k + 1)
                    for c in ((0, 1) if 0 in tiles else (1,)):
                        ins = dve.tensor_scalar(hT[:, k, c * CTX:(c + 1) * CTX], ps[:, k % 4, c * CTX:(c + 1) * CTX],
                                                A[:, l, k, c:c + 1], mod[:, l, sh + k, c:c + 1], ALU.mult, ALU.add)
                    ins.then_inc(sem(f"ht_taken{which}_1"), 1)

            def rotate(xs, t, heads, dim, stride, tab, ta, tb):
                f = dim // 4
                flat = lambda m: m[:, 0:heads * dim].rearrange("p (h d) -> p h d", h=heads)
                halves = lambda m: m.rearrange("p h (a b f) -> p h a b f", a=2, b=2)
                cos = rope[:, t, tab:tab + dim]
                sin = rope[:, t, tab + dim:tab + 2 * dim].rearrange("p (a b f) -> p a b f", a=2, b=2)
                dve.tensor_tensor(flat(ta), xs, bc(cos.unsqueeze(1), [P, heads, dim]), ALU.mult)
                for b in range(2):
                    for ax in range(2):
                        ins = dve.tensor_tensor(halves(flat(tb))[:, :, ax, b, :], halves(xs)[:, :, ax, 1 - b, :],
                                                bc(sin[:, ax, b, :].unsqueeze(1), [P, heads, f]), ALU.mult)
                then(ins)
                return dve.tensor_tensor(xs, flat(ta), flat(tb), ALU.add)

            dve.wait_ge(sem("vec_psum"), 1)
            dve.tensor_copy(vec[:, 0:V_ROWS], ps[:, 0, 0:V_ROWS]).then_inc(sem("vec_done"), 1)
            dve.wait_ge(sem("gq_psum"), 1)
            dve.tensor_copy(gq_row[:, :, :, :], ps[:, 1, 0:4 * HD].rearrange("p (l m d) -> p l m d", l=DEPTH, m=2))\
               .then_inc(sem("gq_ready"), 1)
            dve.wait_ge(sem("ctx_loaded"), 16)
            dve.wait_ge(sem("x_loaded"), 16)
            dve.wait_ge(sem("rope_loaded"), 16)

            for l in range(DEPTH):
                tq = tiles_q(l)
                nq = len(tq) * P
                qt = slice(tq[0], NT)
                norm(l, 1, range(NT))
                if l == 0:
                    ada(0, 0, 3)
                modulate(l, 1, range(NT), A1, 0)

                if l == 0:
                    ada(0, 1, 3)
                dve.wait_ge(sem("ssc_ready"), before_layer("ssc_ready", l) + len(tq) + NT)
                then(dve.tensor_scalar(ss[:, tq[0]:4], ss[:, tq[0]:4], 1.0 / QL, EPS, ALU.mult, ALU.add))
                dve.tensor_scalar(ss[:, 4:8], ss[:, 4:8], 1.0 / KVL, EPS, ALU.mult, ALU.add).then_inc(sem("msc_ready"), 1)
                z_g = lambda t, m0, m1: z[:, t, C_QG + m0 * HD:C_QG + m1 * HD]
                if l == 0:
                    ada(0, 2, 3)
                dve.wait_ge(sem("z_ready"), before_layer("z_ready", l) + len(in_tiles(l)))
                heads = lambda t: (0 if t in tq else HG, HG + HKV)
                if l > 0:
                    then(dve.memset(ssg[:, 0:2, 0:HG], HD))
                for t in range(NT):
                    m0, m1 = heads(t)
                    n = (m1 - m0) * HD
                    then(dve.tensor_tensor(rope_a[:, 0:n], z_g(t, m0, m1), z_g(t, m0, m1), ALU.mult))
                    then(dve.tensor_reduce(ssg[:, t, m0:m1], rope_a[:, 0:n].rearrange("p (h d) -> p h d", d=HD), AX.X, ALU.add))
                dve.tensor_scalar(ssg[:, :, :], ssg[:, :, :], 1.0 / HD, EPS, ALU.mult, ALU.add)\
                   .then_inc(sem("msg_ready"), 1)
                dve.wait_ge(sem("rmsc_ready"), before_layer("rmsc_ready", l) + 1)
                then(dve.reciprocal(rs[:, tq[0]:8], rs[:, tq[0]:8]))
                for t in tq:
                    dve.tensor_scalar(z[:, t, C_Q:C_Q + QL], z[:, t, C_Q:C_Q + QL], rs[:, t:t + 1], None, ALU.mult)
                for t in range(NT):
                    ins = dve.tensor_scalar(z[:, t, C_KV:C_KV + KVL], z[:, t, C_KV:C_KV + KVL], rs[:, 4 + t:5 + t], None, ALU.mult)
                ins.then_inc(sem("c_ready"), 1)
                for j in range(5):
                    g = (V_QN + 3 * l + j) if j < 3 else (V_KVN + 2 * l + j - 3)
                    lo = tq[0] * P if j < 3 else 0
                    dve.wait_ge(sem("cT_psum"), before_layer("cT_psum", l) + j + 1)
                    dve.tensor_scalar(cT[:, j, lo:TOK], ps[:, j % 4, lo:TOK], colv(g), None, ALU.mult)\
                       .then_inc(sem("cT_ready"), 1)
                dve.wait_ge(sem("rmsg_ready"), before_layer("rmsg_ready", l) + 1)
                then(dve.reciprocal(ssg[:, :, :], ssg[:, :, :]))
                for t in range(NT):
                    m0, m1 = heads(t)
                    xs = z_g(t, m0, m1).rearrange("p (h d) -> p h d", d=HD)
                    then(dve.tensor_tensor(xs, xs, bc(ssg[:, t, m0:m1].unsqueeze(2), [P, m1 - m0, HD]), ALU.mult))
                    if m0 == 0:
                        xq = z_g(t, 0, HG).rearrange("p (h d) -> p h d", d=HD)
                        dve.tensor_tensor(xq, xq, bc(gq_row[:, l, 0, :].unsqueeze(1), [P, HG, HD]), ALU.mult)
                    xk = z_g(t, HG, HG + HKV).rearrange("p (h d) -> p h d", d=HD)
                    ins = dve.tensor_tensor(xk, xk, bc(gq_row[:, l, 1, :].unsqueeze(1), [P, HKV, HD]), ALU.mult)
                    if t >= 2:
                        then(ins)
                        ins = rotate(xs, t - 2, m1 - m0, HD, HD, 0, rope_a, rope_b)
                        if t < NT - 1:
                            then(ins)
                ins.then_inc(sem("g_ready"), 1)
                dve.wait_ge(sem("g_ready"), before_layer("g_ready", l) + 1)
                for t in range(NT):
                    xk = z[:, t, C_PE:C_PE + ROPE].rearrange("p (h d) -> p h d", h=1)
                    if t >= 2:
                        then(rotate(xk, t - 2, 1, ROPE, ROPE, 128, rope_a, rope_b))
                    dve.tensor_copy(k_tm[:, t, :].rearrange("p (h c) -> p h c", h=HM)[:, :, NOPE:DK],
                                    bc(z[:, t, C_PE:C_PE + ROPE].unsqueeze(1), [P, HM, ROPE]))
                for t in (2, 3):
                    dve.wait_ge(sem("up_taken"), before_layer("up_taken", l) + 2 * (t - tq[0] + 1))
                    xq = q_tm[:, t, :].rearrange("p (h c) -> p h c", h=HM)[:, :, NOPE:DK]
                    ins = rotate(xq, t - 2, HM, ROPE, DK, 128, rope_a, rope_b)
                    if t == 2:
                        then(ins)
                ins.then_inc(sem("qk_ready"), 1)
                for h in range(HM):
                    dve.wait_ge(sem("qkT_psum"), before_layer("qkT_psum", l) + 2 * h + 2)
                    dve.tensor_copy(kT[0:DK, h, :], ps[0:DK, (2 * h + 1) % 4, :]).then_inc(sem("kT_taken"), 1)

                n_units = len(tq) * (HM + HG)
                keys = lambda i: CTX if tq[i // (HM + HG)] < CTX // P else TOK
                for i in range(n_units + 3):
                    if i < n_units:
                        dve.wait_ge(sem("s_psum"), before_layer("s_psum", l) + i + 1)
                        dve.tensor_reduce(nmax[:, i % 4:i % 4 + 1], ps[:, i % 3, 0:keys(i)], AX.X, ALU.max, negate=True)\
                           .then_inc(sem("max_ready"), 1)
                    j = i - 2
                    if 0 <= j < n_units:
                        dve.wait_ge(sem("pT_psum"), before_layer("pT_psum", l) + j + 1)
                        if j >= 2:
                            dve.wait_ge(sem("o_psum"), before_layer("o_psum", l) + j - 1)
                        dve.tensor_copy(probsT[:, j % 2, 0:keys(j)], ps[:, 3 + j % 2, 0:keys(j)]).then_inc(sem("pT_ready"), 1)
                        dve.reciprocal(rinv[:, j % 4:j % 4 + 1], rsum[:, j % 4:j % 4 + 1]).then_inc(sem("rinv_ready"), 1)
                    j = i - 3
                    if 0 <= j < n_units:
                        qi, h = divmod(j, HM + HG)
                        dve.wait_ge(sem("o_psum"), before_layer("o_psum", l) + j + 1)
                        dve.wait_ge(sem("rinv_ready"), before_layer("rinv_ready", l) + j + 1)
                        if h == 0 and qi >= 2:
                            dve.wait_ge(sem("oT_psum"), before_layer("oT_psum", l) + 2 * (qi - 1))
                        dve.tensor_scalar(o_tm[:, qi % 2, h * VD:(h + 1) * VD], ps[:, 5 + j % 2, 0:VD],
                                          rinv[:, j % 4:j % 4 + 1], None, ALU.mult).then_inc(sem("o_ready"), 1)
                for j in range(KD):
                    dve.wait_ge(sem("sig_ready"), before_layer("sig_ready", l) + j + 1)
                    dve.wait_ge(sem("mT_ready"), before_layer("mT_ready", l) + j)
                    for m in range(2):
                        ins = dve.tensor_tensor(mg_t[:, m, 0:nq], sig[:, 2 * (j % 2) + m, 0:nq], ps[:, 4 * (j % 2) + m, 0:nq], ALU.mult)
                    then(ins)
                    dve.tensor_tensor(mT[:, j, tq[0] * P:TOK], mg_t[:, 0, 0:nq], mg_t[:, 1, 0:nq], ALU.add)\
                       .then_inc(sem("mT_ready"), 1)
                dve.wait_ge(sem("g1_ready"), before_layer("g1_ready", l) + 4)
                n = -1
                for s in range(4):
                    for t in tq:
                        n += 1
                        dve.wait_ge(sem("out_psum"), before_layer("out_psum", l) + n + 1)
                        then(dve.tensor_tensor(add_t[:, 0:256], gate_row[:, t // 2, s * 256:s * 256 + 256],
                                               ps[:, 4 + n % 4, 0:256], ALU.mult))
                        dve.tensor_tensor(x_res[:, t, s * 256:s * 256 + 256], x_res[:, t, s * 256:s * 256 + 256],
                                          add_t[:, 0:256], ALU.add).then_inc(sem("x1_added"), 1)
                        dve.wait_ge(sem("x1_added"), before_layer("x1_added", l) + n + 1)
                norm(l, 2, tq)
                modulate(l, 2, tq, A2, 24)
                if l == 0:
                    def weights_lo(n):
                        _, w, w_hi, w_lo = ff_weights(n)
                        dve.wait_ge(sem("w_hi_ready"), n + 1)
                        dve.tensor_tensor(w_lo, w, w_hi, ALU.subtract).then_inc(sem("w_split"), 1)

                    weights_lo(0)
                    for k in range(KD):
                        dve.wait_ge(sem("h_hi_ready"), k + 1)
                        dve.tensor_tensor(hT_lo[:, k, :], hT[:, k, :], hT_hi[:, k, :], ALU.subtract)\
                           .then_inc(sem("h_split"), 1)
                    weights_lo(1)
                    weights_lo(2)
                    for f in range(FT):
                        if 2 * f + 3 < 2 * FT:
                            weights_lo(2 * f + 3)
                        dve.wait_ge(sem("silu_ready"), f + 1)
                        dve.wait_ge(sem("ff_psum"), 2 * f + 2)
                        dve.tensor_tensor(gT[:, f, :], silu_t[:, f % 2, :], ps[:, 2 * (f % 2) + 1, :], ALU.mult)\
                           .then_inc(sem("gT_ready"), 1)
                        if 2 * f + 4 < 2 * FT:
                            weights_lo(2 * f + 4)
                        if f % 2:
                            for part, k in ada_ffn(f // 2):
                                if k == KD - 1:
                                    ada(1, part, 6)
                    for h in range(2):
                        dve.wait_ge(sem("dn_psum"), h + 1)
                        for t in range(NT):
                            then(dve.tensor_tensor(add_t[:, :], gate_row[:, t // 2, h * 512:h * 512 + 512],
                                                   ps[:, (4 if h == 0 else 0) + t, :], ALU.mult))
                            ins = dve.tensor_tensor(x_res[:, t, h * 512:h * 512 + 512], x_res[:, t, h * 512:h * 512 + 512],
                                                    add_t[:, :], ALU.add)
                            if t < NT - 1:
                                then(ins)
                        ins.then_inc(sem("dn_added"), 1)
                        dve.wait_ge(sem("dn_added"), h + 1)

            dve.wait_ge(sem("lg_psum"), 1)
            then(dve.tensor_copy(lg[:, :, :], ps[:, 0, 0:2 * NE].rearrange("p (t e) -> p t e", t=2)))
            then(dve.tensor_reduce(v1[:, :], lg[:, :, :], AX.X, ALU.max))
            dve.tensor_tensor(ex[:, :, :], lg[:, :, :], bc(v1[:, :].unsqueeze(2), [P, 2, NE]), ALU.subtract)\
               .then_inc(sem("lgm_ready"), 1)
            for t in range(2):
                a3 = cmp_a[:, t, :].rearrange("p (e j) -> p e j", e=NE)
                b3 = cmp_b[:, t, :].rearrange("p (e j) -> p e j", e=NE)
                other = bc(lg[:, t, :].unsqueeze(1), [P, NE, NE])
                own = bc(lg[:, t, :].unsqueeze(2), [P, NE, NE])
                dve.tensor_tensor(a3, other, own, ALU.is_gt)
                then(dve.tensor_tensor(b3, other, own, ALU.is_equal))
                then(dve.tensor_tensor(b3, b3, lower[:, :, :], ALU.mult))
                then(dve.tensor_tensor(a3, a3, b3, ALU.add))
                then(dve.tensor_reduce(rank[:, t, :], a3, AX.X, ALU.add))
            dve.tensor_scalar(sel[:, :, 0:NE], rank[:, :, :], 1.5, None, ALU.is_lt).then_inc(sem("sel_ready"), 1)
            dve.wait_ge(sem("sel_ready"), 1)
            dve.wait_ge(sem("ex_ready"), 1)
            then(dve.tensor_tensor(ex[:, :, :], ex[:, :, :], sel[:, :, 0:NE], ALU.mult))
            then(dve.tensor_reduce(den[:, :], ex[:, :, :], AX.X, ALU.add))
            then(dve.reciprocal(dinv[:, :], den[:, :]))
            then(dve.tensor_tensor(wgt[:, :, 0:NE], ex[:, :, :], bc(dinv[:, :].unsqueeze(2), [P, 2, NE]), ALU.mult))
            dve.wait_ge(sem("pos_psum"), 1)
            dve.tensor_copy(cnt[:, 0:NE], ps[:, 3, 2 * NE:3 * NE])
            dve.tensor_copy(cntf[:, :], ps[:, 3, 2 * NE:3 * NE])
            dve.memset(acc[:, :, :], 0.0)
            then(dve.tensor_copy(pos[:, :, :], ps[:, 3, 0:2 * NE].rearrange("p (t e) -> p t e", t=2)))
            for g in range(MAXG):
                dve.tensor_scalar(pos_g[:, g, :, :], pos[:, :, :], float(-g * G), None, ALU.add)
            a3 = cmp_a[:, 0, :].rearrange("p (e j) -> p e j", e=NE)
            then(dve.tensor_tensor(a3, bc(cntf[:, :].unsqueeze(1), [P, NE, NE]), lower[:, :, :], ALU.mult))
            then(dve.tensor_reduce(offf[:, :], a3, AX.X, ALU.add))
            dve.tensor_copy(first[:, 0:NE], offf[:, :]).then_inc(sem("first_ready"), 1)
            for t in range(2):
                then(dve.tensor_tensor(ex[:, t, :], pos[:, t, :], offf[:, :], ALU.add))
                for r in range(2):
                    then(dve.scalar_tensor_tensor(cmp_b[:, t, 8 * r:8 * r + NE], rank[:, t, :], float(r), ex[:, t, :],
                                                  ALU.is_equal, ALU.mult))
                    then(dve.tensor_reduce(slot12[:, t, r:r + 1], cmp_b[:, t, 8 * r:8 * r + NE], AX.X, ALU.add))
                then(dve.tensor_scalar(S_all[:, t, :], iota[:, :], slot12[:, t, 0:1], None, ALU.is_equal))
                ins = dve.scalar_tensor_tensor(S_all[:, t, :], iota[:, :], slot12[:, t, 1:2], S_all[:, t, :],
                                               ALU.is_equal, ALU.add)
                if t == 0:
                    then(ins)
            ins.then_inc(sem("S_ready"), 1)
            for k in range(1, KD, 2):
                dve.wait_ge(sem("hAll_psum"), k + 1)
                dve.tensor_scalar(hAll[:, k, 0:2 * LAT], ps[:, 4 + k % 4, :], A2[:, 1, k, 1:2], mod[:, 1, 24 + k, 1:2],
                                  ALU.mult, ALU.add).then_inc(sem("hAll_v"), 1)

            def hidden(e, halves):
                widths = group_widths(halves)
                ng = len(widths)
                inc = COUNT // ng
                for t in range(2):
                    w = wgt[:, t, bass.ds(e, 1)]
                    if halves > 1:
                        full = halves // 2 * P
                        ins = dve.tensor_scalar(C_oh[:, t, 0:full], iota_g[:, 0:full], pos_g[:, 0, t, bass.ds(e, 1)], w,
                                                ALU.is_equal, ALU.mult)
                    if halves % 2:
                        g = ng - 1
                        ins = dve.tensor_scalar(C_oh[:, t, tk(g)], iota_h[:, :], pos_g[:, g, t, bass.ds(e, 1)], w,
                                                ALU.is_equal, ALU.mult)
                ins.then_inc(sem("C_ready"), 1)
                with dve.Fori(0, STEPS) as s:
                    it = dve.snap(e * STEPS + s)
                    for g in range(ng):
                        dve.wait_ge(sem("silu_e_ready"), it * COUNT + inc * (g + 1))
                        n = widths[g] * STEP_F // P
                        dve.tensor_tensor(h_e[:, g % 2, 0:n], silu_e[:, g % 2, 0:n], ps[:, g % 2, n:2 * n], ALU.mult)\
                           .then_inc(sem("he_ready"), inc)

            then(dve.memset(C_oh[:, :, :], 0.0))
            with dve.Fori(0, NE) as e:
                count = dve.value_load(cnt[0:1, bass.ds(e, 1)], min_val=0, max_val=LAT)
                by_halves(dve, count, lambda halves: hidden(e, halves))
                dve.wait_ge(sem("y_psum"), e + 1)
                for g in (2, 3):
                    dve.tensor_copy(y[:, g, :], ps[:, 2 + g, :]).then_inc(sem("y_ready_v"), 1)
                dve.wait_ge(sem("CT_psum"), e * 2 + 2)
                dve.tensor_copy(CT[:, 2:4, :], ps[:, 1, :].rearrange("p (g t) -> p g t", g=2)).then_inc(sem("y_ready_v"), 1)
                for t in range(2):
                    dve.wait_ge(sem("sc_psum"), e * 2 + t + 1)
                    for half in range(2):
                        part = acc[:, t, half * 512:half * 512 + 512]
                        dve.tensor_tensor(part, part, ps[:, (6, 0)[t] + half, :], ALU.add).then_inc(sem("acc_added"), 1)
                dve.wait_ge(sem("acc_added"), e * 4 + 4)
            dve.wait_ge(sem("acc_added"), 4 * NE)
            then(dve.tensor_tensor(acc[:, :, :], acc[:, :, :], bc(gate_row[:, 1, :].unsqueeze(1), [P, 2, D]), ALU.mult))
            for t in range(2):
                dve.tensor_tensor(x_res[:, 2 + t, :], x_res[:, 2 + t, :], acc[:, t, :], ALU.add).then_inc(sem("xf_ready"), 1)
            dve.wait_ge(sem("ssf_ready"), 2)
            dve.tensor_scalar(ss[:, 0:2], ss[:, 0:2], 1.0 / D, EPS, ALU.mult, ALU.add).then_inc(sem("msf_ready"), 1)
            dve.wait_ge(sem("rmsf_ready"), 1)
            then(dve.reciprocal(rs[:, 0:2], rs[:, 0:2]))
            dve.wait_ge(sem("fin_ready"), 2)
            dve.wait_ge(sem("xf_ready"), 2)
            for t in range(2):
                dve.scalar_tensor_tensor(out_t[:, t, :], x_res[:, 2 + t, :], rs[:, t:t + 1], fin_row[:, :],
                                         ALU.mult, ALU.mult).then_inc(sem("out_ready"), 1)


_WEIGHTS = ["w_ada", "w_in", "mla_w_qb", "mla_w_kvb", "w_o_mla", "w_o_gqa", "w_out", "dense_w1", "dense_w3", "dense_w2",
            "moe_router", "moe_w1", "moe_w3", "moe_w2"]


def rope_rows():
    t = np.arange(LAT)
    out = []
    for dim in (HD, ROPE):
        half = dim // 2
        inv = (np.float32(THETA) ** (-(np.arange(half // 2, dtype=np.float32) * np.float32(2.0)) / np.float32(half))).astype(np.float32)
        ang = [(p.astype(np.float32)[:, None] * inv).astype(np.float32) for p in (t // GRID_W, t % GRID_W)]
        out += [np.concatenate([np.cos(g) for a in ang for g in (a, a)], axis=1),
                np.concatenate([s * np.sin(a) for a in ang for s in (-1.0, 1.0)], axis=1)]
    return np.concatenate(out, axis=1).astype(np.float32)


def pack_vectors(i):
    wide = lambda v: np.reshape(v, (-1, P))
    half = lambda v: np.concatenate([np.reshape(v, (1, HD)), np.zeros((1, P - HD), np.float32)], axis=1)
    rows = [wide(i[n][l]) for l in range(DEPTH) for n in ("b_ada", "norm1_g", "norm2_g")]
    rows += [wide(i["c_ctx"]), wide(i["c"]), wide(i["final_norm_g"])]
    rows += [wide(i["mla_q_norm_g"]), wide(i["mla_kv_norm_g"])]
    rows += [half(i[n][l]) for n in ("gqa_q_norm_g", "gqa_k_norm_g") for l in range(DEPTH)]
    return np.ascontiguousarray(np.concatenate(rows, axis=0))


def kernel(**inputs):
    import concourse.bacc as _bacc
    from concourse.bass_utils import run_bass_kernel_spmd as _run

    nc = _bacc.Bacc("TRN2", target_bir_lowering=False, num_devices=1)
    host = {n: np.ascontiguousarray(v) for n, v in inputs.items()}
    given = {n: host[n] for n in ["x", "ctx"] + _WEIGHTS}
    given["vecs"] = pack_vectors(host)
    given["rope"] = rope_rows()
    aps, arrays = {}, {}
    for n, v in given.items():
        arrays[f"in_{n}"] = v
        aps[n] = nc.dram_tensor(f"in_{n}", v.shape, mybir.dt.from_np(v.dtype), kind="ExternalInput").ap()
    out = nc.dram_tensor("out", (1, LAT, D), F32, kind="ExternalOutput").ap()
    build(nc, aps, out)
    r = _run(nc, [arrays], core_ids=[0])
    return r.results[0]["out"]
```

```python
from contextlib import ExitStack

import numpy as np

import concourse.bass as bass
from concourse import mybir

F32 = mybir.dt.float32
F32R = mybir.dt.float32r
I32 = mybir.dt.int32
ALU = mybir.AluOpType
ACT = mybir.ActivationFunctionType
AX = mybir.AxisListType

P = 128
D = 1024
KD = D // P
LAT = 256
CTX = 256
TOK = CTX + LAT
NT = TOK // P
DEPTH = 2
EPS = 1e-6
QL, KVL, ROPE, NOPE, VD = 384, 256, 32, 64, 64
HM, HG, HKV, HD = 8, 8, 2, 64
DK = NOPE + ROPE
MLA_SCALE = DK ** -0.5
GQA_SCALE = HD ** -0.5
FFN = 2816
FT = FFN // P
NE = 8
FE = 3584
FET = FE // P
GRID_W = 64
THETA = 10000.0
C_Q, C_KV, C_PE, C_QG, C_KG, C_VG = 0, QL, QL + KVL, QL + KVL + ROPE, QL + KVL + ROPE + HG * HD, QL + KVL + ROPE + HG * HD + HKV * HD
C_GA = C_VG + HKV * HD
C_GB = C_GA + D
IN_SLABS = [(0, 192, True), (192, 192, True), (C_KV, KVL + ROPE, False), (C_KG, 2 * HKV * HD, False),
            (C_QG, 256, True), (C_QG + 256, 256, True)]
SLAB_KG = 3
ADA_PARTS, ADA_COLS = 3, 2048
RING = 6
SLOT = 2304
STEP_F = 512
STEPS = FE // STEP_F
G = 64
H = G // 2
GROUPS = [(H,), (G,), (P,), (P, H), (P, G), (P, G, G)]
MAXG = LAT // G
COUNT = 12
V_L = 64
V_CC, V_C, V_FIN, V_QN, V_KVN, V_GQ, V_GK = 128, 136, 144, 152, 158, 162, 164
V_ROWS = 166


def tiles_q(l):
    return [0, 1, 2, 3] if l < DEPTH - 1 else [2, 3]


def in_tiles(l):
    return [(s, t) for s, (_, _, q) in enumerate(IN_SLABS) for t in (tiles_q(l) if q else range(NT))]


_UNITS = NT * (HM + HG)
LAYER_COUNTS = dict(
    in_psum=len(in_tiles(0)), z_ready=len(in_tiles(0)), ssc_ready=2 * NT, msc_ready=1, rmsc_ready=1, msg_ready=1,
    rmsg_ready=1, c_ready=1, cT_psum=5, cT_ready=5, up_psum=4 * NT, up_taken=4 * NT, g_ready=1, gT_psum=HG + HKV,
    gT_taken=HG + HKV, qk_ready=1, qkT_psum=2 * HM, qT_taken=HM, kT_taken=HM, s_psum=_UNITS, max_ready=_UNITS,
    p_ready=_UNITS, pT_psum=_UNITS, pT_ready=_UNITS, rinv_ready=_UNITS, o_psum=_UNITS, o_ready=_UNITS, oT_psum=2 * NT,
    gh_hi_ready=KD, gh_split=KD, gw_hi_ready=2 * KD, gw_split=2 * KD,
    oT_ready=2 * NT, mg_psum=KD, sig_ready=KD, mT_ready=KD, out_psum=4 * NT, x1_added=4 * NT,
    **{f"{n}{w}": c for w in (1, 2) for n, c in (("xn_ready", NT), ("ss_ready", NT), ("ms_ready", 1), ("rms_ready", 1),
                                                 ("ht_psum", KD))},
    **{f"ht_taken{w}_{par}": KD // 2 for w in (1, 2) for par in (0, 1)},
    **{f"g{w}_{n}": 4 for w in (1, 2) for n in ("psum", "ready")})


def ada_in(s):
    done = [(part, k) for part in (1, 2) for k in range(KD)]
    per = -(-len(done) // len(IN_SLABS))
    return done[s * per:(s + 1) * per]


def ada_ffn(s):
    done = [(part, k) for part in range(ADA_PARTS) for k in range(KD)]
    return done[0 if s == 0 else 2 * s + 2:2 * s + 4]


def slab_list(a):
    out = []
    cols = lambda w, c, n: w.rearrange("(k p) n -> p k n", p=P)[:, :, c:c + n]

    def add(name, *parts):
        out.append((name, parts))

    def ada(l, part, k):
        c = part * ADA_COLS
        add("ada", a["w_ada"][l][k * P:(k + 1) * P, c:c + ADA_COLS].rearrange("p (k n) -> p k n", k=1))

    for k in range(KD):
        ada(0, 0, k)
    for l in range(DEPTH):
        for s, (c, n, _) in enumerate(IN_SLABS):
            add("in", cols(a["w_in"][l], c, n))
            if l == 0:
                for part, k in ada_in(s):
                    ada(0, part, k)
        add("qb", cols(a["mla_w_qb"][l], 0, HM * DK))
        add("kvb", cols(a["mla_w_kvb"][l], 0, HM * (NOPE + VD)))
        for jj in range(KD // 2):
            add("wo", cols(a["w_o_mla"][l], jj * 256, 256), cols(a["w_o_gqa"][l], jj * 256, 256))
            add("ga", cols(a["w_in"][l], C_GA + jj * 256, 256))
            add("gb", cols(a["w_in"][l], C_GB + jj * 256, 256))
        for s in range(4):
            add("out", cols(a["w_out"][l], s * 256, 256))
        if l == 0:
            for s in range(FT // 2):
                add("w1", cols(a["dense_w1"][0], s * 256, 256))
                add("w3", cols(a["dense_w3"][0], s * 256, 256))
                for part, k in ada_ffn(s):
                    ada(1, part, k)
            for f in range(0, FT, 2):
                add("w2", a["dense_w2"][0].rearrange("(f p) n -> p f n", p=P)[:, f:f + 2, :])
    return out


def build(nc, a, out_dram):
    slabs = slab_list(a)
    n_slabs = len(slabs)

    with ExitStack() as ctx:
        def sb(name, shape, dt=F32):
            return ctx.enter_context(nc.sbuf_tensor(name, shape, dt))

        sems = {}

        def sem(name):
            if name not in sems:
                sems[name] = ctx.enter_context(nc.semaphore(name))
            return sems[name]

        def before_layer(name, l):
            return LAYER_COUNTS[name] if l else 0

        ring = [sb(f"ring{i}", [P, SLOT]) for i in range(RING)]
        x_res = sb("x_res", [P, NT, D])
        v_gqa = sb("v_gqa", [P, NT, HKV * HD])
        S_AT = 10240
        sizes = dict(R_mem=13312, hT_mem=KD * TOK, z_mem=NT * C_VG, q_mem=NT * HM * DK, v_mem=NT * HM * VD,
                     k_mem=NT * HM * DK)

        def layout(stack, tensors):
            return [stack.enter_context(nc.sbuf_tensor(name, shape, dt)) for name, shape, dt in tensors]

        with ExitStack() as stack:
            R_mem, hT_mem, z_mem, q_mem, v_mem, k_mem = layout(stack, [(n, [P, size], F32) for n, size in sizes.items()])
        with ExitStack() as stack:
            _, gh_hi, gw_a, gw_b_hi, _, gw_b_lo, _, gh_lo = layout(stack, [
                ("under_gates", [P, KD * TOK], F32), ("gh_hi", [P, KD, TOK], F32R),
                ("gw_a", [P, 2, KD, P], F32R), ("gw_b_hi", [P, KD, P], F32R),
                ("under_gates_2", [P, sizes["R_mem"] - 2 * KD * TOK - 3 * D + sizes["hT_mem"] + KD * TOK], F32),
                ("gw_b_lo", [P, KD, P], F32R),
                ("under_gates_3", [P, sizes["z_mem"] - KD * TOK - D + sizes["q_mem"]], F32),
                ("gh_lo", [P, KD, TOK], F32R)])
        with ExitStack() as stack:
            _, w_parts_12, hT_hi, hT_lo, w_parts_0 = layout(stack, [
                ("under_ffn", [P, sizes["R_mem"]], F32), ("w_parts_12", [P, 2, 2, KD, P], F32R),
                ("hT_hi", [P, KD, TOK], F32R), ("hT_lo", [P, KD, TOK], F32R),
                ("w_parts_0", [P, 1, 2, KD, P], F32R)])
        with ExitStack() as stack:
            _, dn_w, _, dn_g = layout(stack, [
                ("under_down", [P, sizes["R_mem"]], F32), ("dn_w", [P, 2, 2, D], F32R),
                ("under_down_2", [P, NT * D], F32), ("dn_g", [P, 2, 2, TOK], F32R)])
        with ExitStack() as stack:
            _, S_all, _, xn_parts = layout(stack, [
                ("under_gather", [P, S_AT], F32), ("S_all", [P, 2, 2 * LAT], F32R),
                ("under_gather_2", [P, sizes["R_mem"] - S_AT - 4 * LAT + sizes["hT_mem"] + sizes["z_mem"]], F32),
                ("xn_parts", [P, 2, 2, D], F32R)])
        _, he_parts, _, e_parts, gTe_parts, _ = layout(ctx, [
            ("under_experts", [P, S_AT], F32), ("he_parts", [P, 2, KD, P], F32R),
            ("under_experts_2", [P, sizes["R_mem"] - S_AT - 2 * KD * P + sizes["hT_mem"]], F32),
            ("e_parts", [P, 3, 2, 2048], F32R),
            ("gTe_parts", [P, 2, 4, P], F32R),
            ("under_experts_3", [P, sum(sizes[n] for n in ("z_mem", "q_mem", "v_mem", "k_mem")) - 6 * 2048 - 8 * P], F32)])
        view = lambda mem, off, **dims: mem[:, off:off + int(np.prod(list(dims.values())))].rearrange(
            "p (" + " ".join(dims) + ") -> p " + " ".join(dims), **dims)

        v_mla = view(v_mem, 0, t=NT, c=HM * VD)
        hT = view(hT_mem, 0, k=KD, t=TOK)
        z = view(z_mem, 0, t=NT, c=C_VG)
        xn = view(z_mem, 0, t=NT, c=D)
        oT = view(z_mem, 0, j=KD, t=TOK)
        q_tm = view(q_mem, 0, t=NT, c=HM * DK)
        o_tm = view(q_mem, 0, b=2, c=2 * HM * VD)
        sig = view(q_mem, 0, b=4, c=TOK)
        mg_t = view(q_mem, 4 * TOK, b=2, c=TOK)
        k_tm = view(k_mem, 0, t=NT, c=HM * DK)
        probs = view(k_mem, 0, b=2, c=TOK)
        probsT = view(k_mem, 2 * TOK, b=2, c=TOK)
        add_t = view(k_mem, 0, c=512)
        silu_t = view(k_mem, 512, b=2, c=TOK)
        qT = view(R_mem, 0, h=HM, t=TOK)
        kT = view(R_mem, 4096, h=HM, t=TOK)
        qgT = view(R_mem, 8192, h=HG, t=TOK)
        kgT = view(R_mem, 12288, h=HKV, t=TOK)
        cT = view(R_mem, 8192, j=5, t=TOK)
        junk_act = view(R_mem, 4096, c=QL)
        rope_a = view(R_mem, 0, c=(HG + HKV) * HD)
        rope_b = view(R_mem, 1024, c=(HG + HKV) * HD)
        mT = view(R_mem, 0, j=KD, t=TOK)
        gT = view(R_mem, 0, f=FT, t=TOK)
        gate_row = view(R_mem, 11264, b=2, c=D)
        SPAN = 2 * LAT + LAT
        hAll = view(R_mem, 0, k=KD, s=SPAN)
        hTe = view(R_mem, 6144, k=KD, s=LAT)
        acc = view(R_mem, 8192, t=2, c=D)
        CT = view(hT_mem, 0, g=MAXG, t=LAT)
        C_oh = view(hT_mem, 1024, t=2, c=2 * LAT)
        y = view(hT_mem, 2048, g=MAXG, c=512)
        cmp_a = view(k_mem, 1536, t=2, c=NE * NE)
        cmp_b = view(k_mem, 1664, t=2, c=NE * NE)
        silu_e = lambda g: ring[g % 2][:, 2048:SLOT]
        h_e = lambda g: ring[2 + g % 2][:, 2048:SLOT]
        gTe = lambda g: ring[4 + g % 2][:, 2048:SLOT].rearrange("p (i s) -> p i s", i=4)
        fin_row = view(hT_mem, 0, c=D)
        out_t = view(hT_mem, 2048, t=2, c=D)

        silu_junk = sb("silu_junk", [P, 2])
        h_w = sb("h_w", [P, 512])
        ident = sb("ident", [P, P])
        ones = sb("ones", [P, P])
        before = sb("before", [P, P])
        iota = sb("iota", [P, 2 * LAT])
        iota_g = sb("iota_g", [P, P])
        zero_b = sb("zero_b", [P, 512], mybir.dt.bfloat16)
        lower = sb("lower", [P, NE, NE])
        vec_rows = view(z_mem, 4096, i=2, c=P)
        iota_h = sb("iota_h", [P, P])
        vec = sb("vec", [P, 256])
        sc32 = sb("sc32", [P, KD, 32])
        ada_rows = view(k_mem, 2048, c=512)
        mod = sb("mod", [P, DEPTH, 48, 2])
        A1 = sb("A1", [P, DEPTH, KD, 2])
        A2 = sb("A2", [P, DEPTH, KD, 2])
        rope = sb("rope", [P, 2, 192])
        gq_row = sb("gq_row", [P, DEPTH, 2, HD])
        ss = sb("ss", [P, 8])
        rs = sb("rs", [P, 8])
        ssg = sb("ssg", [P, NT, HG + HKV])
        nmax = sb("nmax", [P, 4])
        rsum = sb("rsum", [P, 4])
        rinv = sb("rinv", [P, 4])
        router = sb("router", [P, KD, NE])
        lg = sb("lg", [P, 2, NE])
        v1 = sb("v1", [P, 2])
        rank = sb("rank", [P, 2, NE])
        ex = sb("ex", [P, 2, NE])
        den = sb("den", [P, 2])
        dinv = sb("dinv", [P, 2])
        sel = sb("sel", [P, 2, NE])
        wgt = sb("wgt", [P, 2, NE])
        pos = sb("pos", [P, 2, NE])
        pos_g = sb("pos_g", [P, MAXG, 2, NE])
        cnt = sb("cnt", [P, NE], I32)
        first = sb("first", [P, NE], I32)
        cntf = sb("cntf", [P, NE])
        offf = sb("offf", [P, NE])
        slot12 = sb("slot12", [P, 2, 2])
        ps = ctx.enter_context(nc.psum_tensor("ps", [P, 8, 512], F32))

        colv = lambda c, n=1: vec[:, c:c + n]
        tk = lambda t: slice(t * P, (t + 1) * P)
        loaded = [sem(f"slab_loaded_{i}") for i in range(RING)]
        slab_used = sem("slab_used")
        load_count = []
        tally = [0] * RING
        for i, (_, parts) in enumerate(slabs):
            tally[i % RING] += 16 * len(parts)
            load_count.append(tally[i % RING])

        def by_count(eng, count, body, lo=0, hi=len(GROUPS) - 1):
            if lo == hi:
                body(Groups(GROUPS[lo]))
                return
            mid = (lo + hi) // 2
            with eng.If(count < sum(GROUPS[mid]) + 1):
                by_count(eng, count, body, lo, mid)
            with eng.Else():
                by_count(eng, count, body, mid + 1, hi)

        class Groups:
            def __init__(self, widths):
                self.widths = widths
                self.n = len(widths)
                self.split = widths[0] == P
                self.inc = COUNT // self.n
                self.starts = [sum(widths[:g]) for g in range(self.n)]
                banks = [1 if w == G else 2 for w in widths]
                self.bank = [sum(banks[:g]) for g in range(self.n)]
                self.banks = sum(banks)

        HI_STEP, LO_STEP = RING, RING + 1
        HI_EXPERT, LO_EXPERT = 1 + STEPS * HI_STEP, 1 + STEPS * LO_STEP
        UP_BANK, TURN_BANK = (0, 7, 0), (6, 7, 6)

        ff_slab = {n: [i for i, (name, _) in enumerate(slabs) if name == n] for n in ("w1", "w3")}

        def ff_weights(n):
            f, m = divmod(n, 2)
            i = ff_slab[("w1", "w3")[m]][f // 2]
            w = ring[i % RING][:, 0:KD * 256].rearrange("p (k n) -> p k n", k=KD)[:, :, tk(f % 2)]
            parts = w_parts_0[:, 0] if n % 3 == 0 else w_parts_12[:, n % 3 - 1]
            return i, w, parts[:, 0], parts[:, 1]

        def gate_weights(l, j, m):
            i = [i for i, (name, _) in enumerate(slabs) if name == ("ga", "gb")[m]][l * KD // 2 + j // 2]
            w = ring[i % RING][:, 0:KD * 256].rearrange("p (k n) -> p k n", k=KD)[:, :, tk(j % 2)]
            return i, w, *((gw_a[:, 0], gw_a[:, 1]) if m == 0 else (gw_b_hi[:, :, :], gw_b_lo[:, :, :]))

        def dn_weights(f):
            i = [i for i, (name, _) in enumerate(slabs) if name == "w2"][f // 2]
            return i, ring[i % RING][:, f % 2 * D:f % 2 * D + D]

        block = ctx.enter_context(nc.Block())

        @block.sync
        def _(sp):
            for i, (name, parts) in enumerate(slabs):
                if i >= RING:
                    sp.wait_ge(slab_used, i - RING + 1)
                off = 0
                for src in parts:
                    _, k, n = src.shape
                    dst = ring[i % RING][:, off:off + k * n].rearrange("p (k n) -> p k n", k=k)
                    sp.dma_start(dst, src).then_inc(loaded[i % RING], 16)
                    off += k * n
            w1 = a["moe_w1"][0].rearrange("e (k p) n -> p (e k) n", p=P)
            w3 = a["moe_w3"][0].rearrange("e (k p) n -> p (e k) n", p=P)
            w2 = a["moe_w2"][0].rearrange("e (f p) n -> p (e f) n", p=P)
            with sp.Fori(0, NE) as e:
                with sp.Fori(0, STEPS) as s:
                    for j in range(RING):
                        slot = (n_slabs + j) % RING
                        sp.wait_ge(slab_used, (e * STEPS + s) * RING + (n_slabs + j - RING + 1))
                        if j < 4:
                            src = (w1, w3)[j // 2][:, bass.ds(e * KD + 4 * (j % 2), 4), bass.ds(s * STEP_F, STEP_F)]
                        else:
                            src = w2[:, bass.ds(e * FET + s * 4 + 2 * (j - 4), 2), :]
                        k = src.shape[1]
                        dst = ring[slot][:, 0:2048].rearrange("p (k n) -> p k n", k=k)
                        sp.dma_start(dst, src).then_inc(loaded[slot], 16)
            for t in range(2):
                sp.wait_ge(sem("out_ready"), t + 1)
                sp.dma_start(out_dram[0, t * P:(t + 1) * P, :], out_t[:, t, :]).then_inc(sem("out_stored"), 16)
            sp.wait_ge(sem("out_stored"), 32)

        @block.gpsimd
        def _(pool):
            pool.memset(ident[:, :], 0.0).then_inc(sem("const_step"), 1)
            pool.memset(ones[:, :], 1.0).then_inc(sem("const_step"), 1)
            pool.memset(before[:, :], 0.0).then_inc(sem("const_step"), 1)
            pool.memset(lower[:, :, :], 0.0).then_inc(sem("const_step"), 1)
            pool.memset(zero_b[:, :], 0.0).then_inc(sem("const_ready"), 1)
            pool.memset(sc32[:, :, :], 0.0).then_inc(sem("const_ready"), 1)
            pool.wait_ge(sem("const_step"), 4)
            pool.affine_select(out=ident[:, :], in_=ident[:, :], compare_op=ALU.not_equal, fill=1.0, base=0,
                               pattern=[[-1, P]], channel_multiplier=1).then_inc(sem("const_ready"), 1)
            pool.affine_select(out=before[:, :], in_=before[:, :], compare_op=ALU.is_ge, fill=1.0, base=0,
                               pattern=[[-1, P]], channel_multiplier=1).then_inc(sem("const_ready"), 1)
            pool.affine_select(out=lower[:, :, :], in_=lower[:, :, :], compare_op=ALU.is_ge, fill=1.0, base=0,
                               pattern=[[-1, NE], [1, NE]], channel_multiplier=0).then_inc(sem("const_ready"), 1)
            pool.iota(iota[:, :], pattern=[[1, 2 * LAT]], base=0, channel_multiplier=0,
                      allow_small_or_imprecise_dtypes=True).then_inc(sem("const_ready"), 1)
            pool.iota(iota_g[:, :], pattern=[[0, P // G], [1, G]], base=0, channel_multiplier=0,
                      allow_small_or_imprecise_dtypes=True).then_inc(sem("const_ready"), 1)
            pool.iota(iota_h[:, :], pattern=[[0, P // H], [1, H]], base=0, channel_multiplier=0,
                      allow_small_or_imprecise_dtypes=True).then_inc(sem("const_ready"), 1)
            pool.wait_ge(sem("x1_added"), LAYER_COUNTS["x1_added"] + 4 * len(tiles_q(DEPTH - 1)))
            pool.memset(hAll[:, :, 2 * LAT:SPAN], 0.0).then_inc(sem("hTe_ready"), 1)
            pool.wait_ge(sem("hTe_ready"), 1)
            pool.wait_ge(sem("hAll_a"), KD // 2)
            pool.wait_ge(sem("hAll_v"), KD // 2)
            pool.wait_ge(sem("first_ready"), 1)
            with pool.Fori(1, NE) as e:
                at = pool.value_load(first[0:1, bass.ds(e, 1)], min_val=0, max_val=2 * LAT)
                pool.wait_ge(sem("y_psum"), e)
                pool.tensor_copy(hTe[:, :, :], hAll[:, :, bass.ds(at, LAT)]).then_inc(sem("hTe_ready"), 1)
        CONSTS = 8

        @block.tensor
        def _(pe):
            at = [0]

            spent = [0]

            def release(mm):
                if spent[0]:
                    mm.then_inc(slab_used, spent[0])
                    spent[0] = 0

            def slab():
                i = at[0]
                at[0] += 1
                pe.wait_ge(loaded[i % RING], load_count[i])
                views, o = [], 0
                for src in slabs[i][1]:
                    _, k, n = src.shape
                    views.append(ring[i % RING][:, o:o + k * n].rearrange("p (k n) -> p k n", k=k))
                    o += k * n
                return views if len(views) > 1 else views[0]

            def ada(l, part, k, bank):
                n = ADA_PARTS * l + part
                w = slab()
                if k == 0 and n:
                    pe.wait_ge(sem("rows_ready"), n)
                for j in range(4):
                    mm = pe.matmul(ps[32 * j:32 * j + 32, 7, :], sc32[:, k, :], w[:, 0, j * 512:j * 512 + 512],
                                   start=(k == 0), stop=(k == KD - 1))
                    if j == 0:
                        release(mm)
                spent[0] += 1
                if k == KD - 1:
                    mm.then_inc(sem("ada_psum"), 1)
                    pe.wait_ge(sem("rows_ready"), n + 1)
                    for i in range(4):
                        mm = pe.transpose(ps[:, bank, tk(i)], ada_rows[:, tk(i)], ident[:, :])
                        if i == 0:
                            release(mm)
                    mm.then_inc(sem("adaT_psum"), 1)

            def h_transpose(l, which, tiles):
                pe.wait_ge(sem(f"xn_ready{which}"), before_layer(f"xn_ready{which}", l) + len(tiles))
                for k in range(KD):
                    if k >= 4:
                        pe.wait_ge(sem(f"ht_taken{which}_{k % 2}"), before_layer(f"ht_taken{which}_{k % 2}", l) + (k - 4) // 2 + 1)
                    for t in tiles:
                        mm = pe.transpose(ps[:, k % 4, tk(t)], xn[:, t, tk(k)], ident[:, :])
                        if t != tiles[-1]:
                            release(mm)
                    mm.then_inc(sem(f"ht_psum{which}"), 1)
                for par in range(2):
                    pe.wait_ge(sem(f"ht_taken{which}_{par}"), before_layer(f"ht_taken{which}_{par}", l) + KD // 2)

            def rows(l, col, banks, name):
                for b, (c, kk) in zip(banks, [(c, kk) for c in col for kk in range(2)]):
                    for k in range(4):
                        mm = pe.matmul(ps[:, b, tk(k)], c(4 * kk + k).to_broadcast([P, P]), ident[:, :],
                                       start=True, stop=True)
                        if k == 0:
                            release(mm)
                    mm.then_inc(sem(f"{name}_psum"), 1)

            pe.wait_ge(sem("const_ready"), CONSTS)
            pe.wait_ge(sem("vec_loaded_a"), 16)
            pe.wait_ge(sem("vec_loaded_b"), 16)
            pe.transpose(ps[:, 0, 0:P], vec_rows[:, 0, :], ident[:, :])
            pe.transpose(ps[:, 0, P:V_ROWS], vec_rows[0:V_ROWS - P, 1, :], ident[0:V_ROWS - P, 0:V_ROWS - P])\
              .then_inc(sem("vec_psum"), 1)
            pe.wait_ge(sem("vec_ready"), 1)
            for l in range(DEPTH):
                for m, c in enumerate((V_GQ + l, V_GK + l)):
                    mm = pe.matmul(ps[:, 1, (2 * l + m) * HD:(2 * l + m + 1) * HD], colv(c).to_broadcast([P, P])[0:HD, :],
                                   ident[0:HD, 0:HD], start=True, stop=True)
            mm.then_inc(sem("gq_psum"), 1)
            pe.wait_ge(sem("gq_ready"), 1)

            for k in range(KD):
                ada(0, 0, k, 3)
            pe.wait_ge(sem("mod_ready"), 1)
            for l in range(DEPTH):
                tq = tiles_q(l)
                q0 = tq[0] * P
                nq = len(tq) * P
                h_transpose(l, 1, range(NT))

                n = -1
                for s, (c, cols, q) in enumerate(IN_SLABS):
                    w = slab()
                    for t in (tq if q else range(NT)):
                        n += 1
                        if n >= 3:
                            pe.wait_ge(sem("z_ready"), before_layer("z_ready", l) + n - 2)
                        for k in range(KD):
                            mm = pe.matmul(ps[:, 4 + n % 3, 0:cols], hT[:, k, tk(t)], w[:, k, :],
                                           start=(k == 0), stop=(k == KD - 1))
                            if k == 0:
                                release(mm)
                        mm.then_inc(sem("in_psum"), 1)
                    spent[0] += 1
                    if l == 0:
                        for part, k in ada_in(s):
                            ada(0, part, k, 3)
                if l == 0:
                    pe.wait_ge(sem("mod_ready"), ADA_PARTS)

                pe.wait_ge(sem("c_ready"), before_layer("c_ready", l) + 1)
                for j in range(5):
                    if j == 4:
                        pe.wait_ge(sem("cT_ready"), before_layer("cT_ready", l) + 1)
                    for t in (tq if j < 3 else range(NT)):
                        mm = pe.transpose(ps[:, j % 4, tk(t)], z[:, t, tk(j)], ident[:, :])
                        if t != NT - 1:
                            release(mm)
                    mm.then_inc(sem("cT_psum"), 1)
                pe.wait_ge(sem("cT_ready"), before_layer("cT_ready", l) + 5)
                pe.wait_ge(sem("z_ready"), before_layer("z_ready", l) + len(in_tiles(l)))
                n = -1
                w = slab()
                for t in tq:
                    for h in range(2):
                        n += 1
                        if n >= 4:
                            pe.wait_ge(sem("up_taken"), before_layer("up_taken", l) + n - 3)
                        for k in range(3):
                            mm = pe.matmul(ps[:, 4 + n % 4, 0:384], cT[:, k, tk(t)], w[:, k, h * 384:h * 384 + 384],
                                           start=(k == 0), stop=(k == 2))
                        mm.then_inc(sem("up_psum"), 1)
                spent[0] += 1
                w = slab()
                for t in range(NT):
                    for h in range(2):
                        n += 1
                        pe.wait_ge(sem("up_taken"), before_layer("up_taken", l) + n - 3)
                        for k in range(2):
                            mm = pe.matmul(ps[:, 4 + n % 4, :], cT[:, 3 + k, tk(t)], w[:, k, h * 512:h * 512 + 512],
                                           start=(k == 0), stop=(k == 1))
                            if k == 0:
                                release(mm)
                        mm.then_inc(sem("up_psum"), 1)
                spent[0] += 1

                pe.wait_ge(sem("g_ready"), before_layer("g_ready", l) + 1)
                for m in range(HG + HKV):
                    if m >= 4:
                        pe.wait_ge(sem("gT_taken"), before_layer("gT_taken", l) + m - 3)
                    for t in (tq if m < HG else range(NT)):
                        mm = pe.transpose(ps[0:HD, m % 4, tk(t)], z[:, t, C_QG + m * HD:C_QG + (m + 1) * HD], ident[:, :])
                        if t != NT - 1:
                            release(mm)
                    mm.then_inc(sem("gT_psum"), 1)
                pe.wait_ge(sem("gT_taken"), before_layer("gT_taken", l) + HG + HKV)
                pe.wait_ge(sem("qk_ready"), before_layer("qk_ready", l) + 1)
                pe.wait_ge(sem("up_taken"), before_layer("up_taken", l) + 2 * (len(tq) + NT))
                for m in range(2 * HM):
                    if m >= 4:
                        pe.wait_ge(sem(("qT_taken", "kT_taken")[m % 2]), before_layer(("qT_taken", "kT_taken")[m % 2], l) + (m - 4) // 2 + 1)
                    src = (q_tm, k_tm)[m % 2]
                    for t in (tq if m % 2 == 0 else range(NT)):
                        mm = pe.transpose(ps[0:DK, m % 4, tk(t)], src[:, t, (m // 2) * DK:(m // 2 + 1) * DK], ident[:, :])
                    mm.then_inc(sem("qkT_psum"), 1)
                pe.wait_ge(sem("qT_taken"), before_layer("qT_taken", l) + HM)
                pe.wait_ge(sem("kT_taken"), before_layer("kT_taken", l) + HM)

                units = [(qi, h) for qi in range(len(tq)) for h in range(HM + HG)]
                keys = lambda qi: CTX if tq[qi] < CTX // P else TOK
                for i in range(len(units) + 4):
                    if i < len(units):
                        qi, h = units[i]
                        nk = keys(qi)
                        if i >= 3:
                            pe.wait_ge(sem("p_ready"), before_layer("p_ready", l) + i - 2)
                        if h < HM:
                            pe.matmul(ps[:, i % 3, 0:nk], qT[0:DK, h, tk(tq[qi])], kT[0:DK, h, 0:nk],
                                      start=True, stop=True).then_inc(sem("s_psum"), 1)
                        else:
                            pe.matmul(ps[:, i % 3, 0:nk], qgT[0:HD, h - HM, tk(tq[qi])],
                                      kgT[0:HD, (h - HM) // (HG // HKV), 0:nk],
                                      start=True, stop=True).then_inc(sem("s_psum"), 1)
                    j = i - 2
                    if 0 <= j < len(units):
                        pe.wait_ge(sem("p_ready"), before_layer("p_ready", l) + j + 1)
                        if j >= 2:
                            pe.wait_ge(sem("pT_ready"), before_layer("pT_ready", l) + j - 1)
                        for kt in range(keys(units[j][0]) // P):
                            mm = pe.transpose(ps[:, 3 + j % 2, tk(kt)], probs[:, j % 2, tk(kt)], ident[:, :])
                        mm.then_inc(sem("pT_psum"), 1)
                    j = i - 3
                    if 0 <= j < len(units):
                        qi, h = units[j]
                        pe.wait_ge(sem("pT_ready"), before_layer("pT_ready", l) + j + 1)
                        if j >= 2:
                            pe.wait_ge(sem("o_ready"), before_layer("o_ready", l) + j - 1)
                        nkt = keys(qi) // P
                        for kt in range(nkt):
                            v = (v_mla[:, kt, h * VD:(h + 1) * VD] if h < HM else
                                 v_gqa[:, kt, (h - HM) // (HG // HKV) * HD:((h - HM) // (HG // HKV) + 1) * HD])
                            mm = pe.matmul(ps[:, 5 + j % 2, 0:VD], probsT[:, j % 2, tk(kt)], v,
                                           start=(kt == 0), stop=(kt == nkt - 1))
                        mm.then_inc(sem("o_psum"), 1)
                    j = i - 4
                    if 0 <= j < len(units) and units[j][1] == HM + HG - 1:
                        qi = units[j][0]
                        pe.wait_ge(sem("o_ready"), before_layer("o_ready", l) + j + 1)
                        for half in range(2):
                            r = 2 * qi + half
                            if r >= 1:
                                pe.wait_ge(sem("oT_ready"), before_layer("oT_ready", l) + r)
                            for k in range(4):
                                mm = pe.transpose(ps[:, 7, tk(k)], o_tm[:, qi % 2, tk(4 * half + k)], ident[:, :])
                            mm.then_inc(sem("oT_psum"), 1)
                pe.wait_ge(sem("oT_ready"), before_layer("oT_ready", l) + 2 * len(tq))

                for jj in range(KD // 2):
                    wa, wb = slab()
                    slab(), slab()
                    for j in (2 * jj, 2 * jj + 1):
                        b = 4 * (j % 2)
                        c = (j % 2) * P
                        if j >= 2:
                            pe.wait_ge(sem("mT_ready"), before_layer("mT_ready", l) + j - 1)
                        for m, w in enumerate((wa, wb)):
                            for k in range(4):
                                mm = pe.matmul(ps[:, b + m, 0:nq], w[:, k, c:c + P], oT[:, 4 * m + k, q0:TOK],
                                               start=(k == 0), stop=(k == 3))
                                if k == 0:
                                    release(mm)
                        for m in range(2):
                            _, _, w_hi, w_lo = gate_weights(l, j, m)
                            pe.wait_ge(sem("gw_split"), before_layer("gw_split", l) + 2 * j + m + 1)
                            for k in range(KD):
                                if j == 0 and m == 0:
                                    pe.wait_ge(sem("gh_split"), before_layer("gh_split", l) + k + 1)
                                out = ps[:, b + 2 + m, 0:nq]
                                pe.matmul(out, w_hi[:, k, :], gh_hi[:, k, q0:TOK], start=(k == 0), stop=False)
                                pe.matmul(out, w_hi[:, k, :], gh_lo[:, k, q0:TOK], start=False, stop=False)
                                mm = pe.matmul(out, w_lo[:, k, :], gh_hi[:, k, q0:TOK], start=False, stop=(k == KD - 1))
                        mm.then_inc(sem("mg_psum"), 1)
                    spent[0] += 3
                pe.wait_ge(sem("mT_ready"), before_layer("mT_ready", l) + KD - 1)
                rows(l, [lambda k, c=c: mod[:, l, 16 + k, c:c + 1] for c in range(2)], range(4), "g1")
                pe.wait_ge(sem("mT_ready"), before_layer("mT_ready", l) + KD)
                n = -1
                for s in range(4):
                    w = slab()
                    for t in tq:
                        n += 1
                        if n >= 4:
                            pe.wait_ge(sem("x1_added"), before_layer("x1_added", l) + n - 3)
                        for k in range(KD):
                            mm = pe.matmul(ps[:, 4 + n % 4, 0:256], mT[:, k, tk(t)], w[:, k, :],
                                           start=(k == 0), stop=(k == KD - 1))
                            if k == 0:
                                release(mm)
                        mm.then_inc(sem("out_psum"), 1)
                    spent[0] += 1
                pe.wait_ge(sem("x1_added"), before_layer("x1_added", l) + n + 1)
                h_transpose(l, 2, tq)
                if l == 0:
                    rows(l, [lambda k, c=c: mod[:, 0, 40 + k, c:c + 1] for c in range(2)], range(4, 8), "g2")
                    for s in range(FT // 2):
                        slab(), slab()
                        for j in range(2):
                            f = 2 * s + j
                            b = 2 * (f % 2)
                            if f >= 2:
                                pe.wait_ge(sem("gT_ready"), f - 1)
                            for m in range(2):
                                _, _, w_hi, w_lo = ff_weights(2 * f + m)
                                pe.wait_ge(sem("w_split"), 2 * f + m + 1)
                                for k in range(KD):
                                    if f == 0 and m == 0:
                                        pe.wait_ge(sem("h_split"), k + 1)
                                    mm = pe.matmul(ps[:, b + m, :], w_hi[:, k, :], hT_hi[:, k, :], start=(k == 0), stop=False)
                                    if k == 0:
                                        release(mm)
                                    pe.matmul(ps[:, b + m, :], w_hi[:, k, :], hT_lo[:, k, :], start=False, stop=False)
                                    mm = pe.matmul(ps[:, b + m, :], w_lo[:, k, :], hT_hi[:, k, :],
                                                   start=False, stop=(k == KD - 1))
                                mm.then_inc(sem("ff_psum"), 1)
                        spent[0] += 2
                        if s == 0:
                            pe.wait_ge(sem("g2_ready"), 4)
                        for part, k in ada_ffn(s):
                            ada(1, part, k, 6)
                    pe.wait_ge(sem("gT_ready"), FT)
                    pe.wait_ge(sem("mod_ready"), 2 * ADA_PARTS)
                    for f in range(FT):
                        if f % 2 == 0:
                            slab()
                        pe.wait_ge(sem("dn_split"), 2 * f + 2)
                        for t in range(NT):
                            for h in range(2):
                                n = 0
                                for g, w in ((0, 0), (0, 1), (1, 0)):
                                    mm = pe.matmul(ps[:, 2 * t + h, :], dn_g[:, f % 2, g, tk(t)],
                                                   dn_w[:, f % 2, w, h * 512:h * 512 + 512],
                                                   start=(f == 0 and n == 0), stop=(f == FT - 1 and n == 2))
                                    n += 1
                                    if t == 0 and h == 0 and n == 1:
                                        release(mm)
                                if f == FT - 1:
                                    mm.then_inc(sem("dn_psum"), 1)
                        if f < FT - 1:
                            mm.then_inc(sem("dn_used"), 1)
                        if f % 2 == 1:
                            spent[0] += 1

            pe.wait_ge(sem("router_loaded"), 16)
            for t in range(2):
                for k in range(KD):
                    mm = pe.matmul(ps[:, 0, t * NE:(t + 1) * NE], hT[:, k, tk(2 + t)], router[:, k, :],
                                   start=(k == 0), stop=(k == KD - 1))
                    release(mm) if k == 0 else None
            mm.then_inc(sem("lg_psum"), 1)
            rows(1, [lambda k, c=c: mod[:, 1, 40 + k, c:c + 1] for c in range(2)], range(4, 8), "g2")
            pe.wait_ge(sem("sel_ready"), 1)
            pe.matmul(ps[:, 3, 0:NE], before[:, :], sel[:, 0, 0:NE], start=True, stop=True)
            pe.matmul(ps[:, 3, NE:2 * NE], ones[:, :], sel[:, 0, 0:NE], start=True, stop=False)
            pe.matmul(ps[:, 3, NE:2 * NE], before[:, :], sel[:, 1, 0:NE], start=False, stop=True)
            pe.matmul(ps[:, 3, 2 * NE:3 * NE], ones[:, :], sel[:, 0, 0:NE], start=True, stop=False)
            pe.matmul(ps[:, 3, 2 * NE:3 * NE], ones[:, :], sel[:, 1, 0:NE], start=False, stop=True)\
              .then_inc(sem("pos_psum"), 1)
            pe.wait_ge(sem("g2_ready"), 8)
            pe.wait_ge(sem("xn_split"), 1)
            pe.wait_ge(sem("S_ready"), 1)
            for k in range(KD):
                if k >= 4:
                    pe.wait_ge(sem(("hAll_a", "hAll_v")[k % 2]), (k - 4) // 2 + 1)
                for part in range(2):
                    for t in range(2):
                        mm = pe.matmul(ps[:, 4 + k % 4, :], xn_parts[:, part, t, tk(k)], S_all[:, t, :],
                                       start=(part == 0 and t == 0), stop=(part == 1 and t == 1))
                mm.then_inc(sem("hAll_psum"), 1)
            pe.wait_ge(sem("hAll_a"), KD // 2)
            pe.wait_ge(sem("hAll_v"), KD // 2)
            for b in range(2, 6):
                mm = pe.matmul(ps[:, b, :], zero_b[:, 0:P], zero_b[:, :], start=True, stop=True)
            mm.then_inc(sem("e_parts_used"), 3)

            def expert(e, gr):
                ng, inc = gr.n, gr.inc
                if gr.split:
                    pe.wait_ge(sem("e_split"), e * LO_EXPERT + 1)
                for b in range(gr.banks):
                    mm = pe.matmul(ps[:, 2 + b, :], zero_b[:, 0:P], zero_b[:, :], start=True, stop=True)
                if not gr.split:
                    mm.then_inc(sem("e_parts_used"), STEPS * RING)
                with pe.Fori(0, STEPS) as s:
                    it = pe.snap(e * STEPS + s)
                    lo_base = pe.snap(e * LO_EXPERT + s * LO_STEP)

                    def arrived(j):
                        slot = (n_slabs + j) % RING
                        pe.wait_ge(loaded[slot], it * 16 + (tally[slot] + 16))

                    def split_products(j, outs):
                        pe.wait_ge(sem("e_split"), lo_base + (1 + j + (1 if j < 4 else 2)))
                        n = 0
                        for out, hi, lo, c, start, stop in outs:
                            for a, part in ((hi, 0), (lo, 0), (hi, 1)):
                                mm = pe.matmul(out, a, e_parts[:, j % 3, part, c:c + 512], start=start and n == 0,
                                               stop=stop and n == 3 * len(outs) - 1, skip_group_check=True)
                                if n == 0 and ng == 1:
                                    mm.then_inc(slab_used, 1)
                                n += 1
                        mm.then_inc(sem("e_parts_used"), 1)

                    def up(g):
                        width = gr.widths[g]
                        if width == P:
                            for j in range(4):
                                m = j // 2
                                split_products(j, [(ps[:, m, :], he_parts[:, 0, 4 * (j % 2) + k, :], he_parts[:, 1, 4 * (j % 2) + k, :],
                                                    k * 512, j % 2 == 0, j % 2 == 1) for k in range(4)])
                            mm = pe.matmul(ps[:, TURN_BANK[0], 0:64], zero_b[:, 0:P], zero_b[:, 0:64], start=True, stop=True)
                            mm.then_inc(sem("upe_psum"), inc)
                            return
                        n = width * STEP_F // P
                        at = gr.starts[g]
                        for m in range(2):
                            for k in range(KD):
                                if g == 0 and k % 4 == 0:
                                    arrived(2 * m + k // 4)
                                w = ring[(n_slabs + 2 * m + k // 4) % RING][:, 0:2048].rearrange("p (k n) -> p k n", k=4)
                                for c in range(P // width):
                                    mm = pe.matmul(ps[width * c:width * c + width, UP_BANK[g], m * n:m * n + n],
                                                   hTe[:, k, at:at + width], w[:, k % 4, c * n:c * n + n],
                                                   start=(k == 0), stop=(k == KD - 1))
                                    if m == 1 and k == 0 and c == 0 and g == ng - 1:
                                        mm.then_inc(slab_used, 2)
                        mm.then_inc(sem("upe_psum"), inc)

                    def turn(g):
                        pe.wait_ge(sem("he_ready"), it * COUNT + inc * (g + 1))
                        width = gr.widths[g]
                        for i in range(width // H):
                            src = h_w[:, tk(i)] if width == P else h_e(g)[:, tk(i)]
                            mm = pe.transpose(ps[:, TURN_BANK[g], tk(i)], src, ident[:, :])
                            if i == 0 and g == ng - 1 and width == G:
                                mm.then_inc(slab_used, 2)
                        mm.then_inc(sem("gTe_psum"), inc)

                    def down(g):
                        width = gr.widths[g]
                        bank = 2 + gr.bank[g]
                        pe.wait_ge(sem("gTe_ready"), it * COUNT + inc * (g + 1))
                        if width == P:
                            for j in (4, 5):
                                split_products(j, [(ps[:, bank + half, :], gTe_parts[:, 0, 2 * (j - 4) + f, :],
                                                    gTe_parts[:, 1, 2 * (j - 4) + f, :], f * D + half * 512, False, False)
                                                   for f in range(2) for half in range(2)])
                            return
                        wf = [ring[(n_slabs + 4 + f // 2) % RING][:, f % 2 * D:f % 2 * D + D] for f in range(4)]
                        if width == G:
                            for f in range(4):
                                if g == 0 and f % 2 == 0:
                                    arrived(4 + f // 2)
                                for half in range(2):
                                    mm = pe.matmul(ps[G * half:G * half + G, bank, :], gTe(g)[:, 2 * (f % 2) + f // 2, :],
                                                   wf[f][:, half * 512:half * 512 + 512], start=False, stop=False,
                                                   skip_group_check=True)
                        else:
                            if g == 0:
                                arrived(4)
                                arrived(5)
                            for half in range(2):
                                for f in range(4):
                                    mm = pe.matmul(ps[H * f:H * f + H, bank + half, :], gTe(g)[:, f, 0:H],
                                                   wf[f][:, half * 512:half * 512 + 512], start=False, stop=False,
                                                   skip_group_check=True)
                                    if f == 0 and half == 0:
                                        mm.then_inc(slab_used, 2)
                        if g == ng - 1:
                            mm.then_inc(slab_used, 2)

                    up(0)
                    for g in range(ng):
                        if g + 1 < ng:
                            up(g + 1)
                        turn(g)
                        down(g)
                pe.wait_ge(sem("C_ready"), e + 1)
                for g in range(MAXG):
                    for t in range(2):
                        mm = pe.transpose(ps[:, g // 2, (g % 2) * LAT + t * P:(g % 2) * LAT + (t + 1) * P],
                                          C_oh[:, t, tk(g)], ident[:, :])
                        if g == 0 and t == 0:
                            mm.then_inc(sem("y_psum"), 1)
                    if g % 2 == 1:
                        mm.then_inc(sem("CT_psum"), 1)
                pe.wait_ge(sem("y_ready_a"), e * 3 + 3)
                pe.wait_ge(sem("y_ready_v"), e * 3 + 3)
                for t in range(2):
                    for half in range(2):
                        out = ps[:, (6, 0)[t] + half, :]
                        for g, width in enumerate(gr.widths):
                            rows_g = slice(G * half, G * half + G) if width == G else slice(0, P)
                            b = gr.bank[g] + (0 if width == G else half)
                            mm = pe.matmul(out, CT[rows_g, g, tk(t)], y[rows_g, b, :], start=(g == 0), stop=(g == ng - 1))
                    mm.then_inc(sem("sc_psum"), 1)
                pe.wait_ge(sem("acc_added"), e * 4 + 4)

            with pe.Fori(0, NE) as e:
                count = pe.value_load(cnt[0:1, bass.ds(e, 1)], min_val=0, max_val=LAT)
                pe.wait_ge(sem("hTe_ready"), e + 1)
                by_count(pe, count, lambda gr: expert(e, gr))
            rows(0, [lambda k: colv(V_FIN + k)], range(1, 3), "fin")

        @block.scalar
        def _(act):
            act.dma_start(vec_rows[:, 0, :], a["vecs"][0:P, :]).then_inc(sem("vec_loaded_a"), 16)
            act.dma_start(vec_rows[0:V_ROWS - P, 1, :], a["vecs"][P:V_ROWS, :]).then_inc(sem("vec_loaded_b"), 16)
            act.dma_start(x_res[:, 0:2, :], a["ctx"][0].rearrange("(t p) d -> p t d", p=P)).then_inc(sem("ctx_loaded"), 16)
            act.dma_start(x_res[:, 2:4, :], a["x"][0].rearrange("(t p) d -> p t d", p=P)).then_inc(sem("x_loaded"), 16)
            act.dma_start(rope[:, :, :], a["rope"].rearrange("(t p) d -> p t d", p=P)).then_inc(sem("rope_loaded"), 16)
            act.dma_start(router[:, :, :], a["moe_router"][0].rearrange("(k p) n -> p k n", p=P))\
               .then_inc(sem("router_loaded"), 16)

            def squares(l, which, tiles, added=None):
                for i, t in enumerate(tiles):
                    if added:
                        act.wait_ge(sem(added), 2 * (i + 1))
                    act.activation(xn[:, t, :], x_res[:, t, :], ACT.Square, accum_out=ss[:, i:i + 1])\
                       .then_inc(sem(f"ss_ready{which}"), 1)
                act.wait_ge(sem(f"ms_ready{which}"), before_layer(f"ms_ready{which}", l) + 1)
                act.activation(rs[:, 0:len(tiles)], ss[:, 0:len(tiles)], ACT.Sqrt).then_inc(sem(f"rms_ready{which}"), 1)

            def modulate(l, which, tiles, A, sh):
                for k in range(0, KD, 2):
                    act.wait_ge(sem(f"ht_psum{which}"), before_layer(f"ht_psum{which}", l) + k + 1)
                    for c in ((0, 1) if 0 in tiles else (1,)):
                        ins = act.activation(hT[:, k, c * CTX:(c + 1) * CTX], ps[:, k % 4, c * CTX:(c + 1) * CTX],
                                             ACT.Identity, scale=A[:, l, k, c:c + 1], bias=mod[:, l, sh + k, c:c + 1])
                    ins.then_inc(sem(f"ht_taken{which}_0"), 1)

            def rows(l, n, bank0, name, dst):
                for b in range(n):
                    act.wait_ge(sem(f"{name}_psum"), 4 * l + b + 1)
                    act.activation(dst(b), ps[:, bank0 + b, :], ACT.Copy).then_inc(sem(f"{name}_ready"), 1)

            n_sq = [0]
            act.wait_ge(sem("vec_done"), 1)
            act.wait_ge(sem("const_ready"), CONSTS)
            act.activation(sc32[:, :, 0:2], vec[:, V_CC:V_CC + 16].rearrange("p (c k) -> p k c", c=2), ACT.Silu)\
               .then_inc(sem("vec_ready"), 1)
            act.wait_ge(sem("ctx_loaded"), 16)
            act.wait_ge(sem("x_loaded"), 16)
            for l in range(DEPTH):
                tq = tiles_q(l)
                nq = len(tq) * P
                squares(l, 1, range(NT), added="dn_added" if l else None)
                act.wait_ge(sem("mod_ready"), ADA_PARTS * l + 1)
                modulate(l, 1, range(NT), A1, 0)
                n = -1
                for s, (c, cols, q) in enumerate(IN_SLABS):
                    for t in (tq if q else range(NT)):
                        n += 1
                        act.wait_ge(sem("in_psum"), before_layer("in_psum", l) + n + 1)
                        if s == SLAB_KG:
                            act.activation(v_gqa[:, t, :], ps[:, 4 + n % 3, P:2 * P], ACT.Copy)
                            cols = P
                        act.activation(z[:, t, c:c + cols], ps[:, 4 + n % 3, 0:cols], ACT.Copy)\
                           .then_inc(sem("z_ready"), 1)
                    if s == 2:
                        act.wait_ge(sem("z_ready"), before_layer("z_ready", l) + n + 1)
                        for t in tq:
                            act.activation(junk_act[:, 0:QL], z[:, t, C_Q:C_Q + QL], ACT.Square,
                                           accum_out=ss[:, t:t + 1]).then_inc(sem("ssc_ready"), 1)
                            n_sq[0] += 1
                            act.wait_ge(sem("ssc_ready"), n_sq[0])
                        for t in range(NT):
                            act.activation(junk_act[:, 0:KVL], z[:, t, C_KV:C_KV + KVL], ACT.Square,
                                           accum_out=ss[:, 4 + t:5 + t]).then_inc(sem("ssc_ready"), 1)
                            n_sq[0] += 1
                            act.wait_ge(sem("ssc_ready"), n_sq[0])
                    if s == 3:
                        act.wait_ge(sem("msc_ready"), before_layer("msc_ready", l) + 1)
                        act.activation(rs[:, tq[0]:8], ss[:, tq[0]:8], ACT.Sqrt).then_inc(sem("rmsc_ready"), 1)
                n = -1
                for t in tq:
                    for h in range(2):
                        n += 1
                        act.wait_ge(sem("up_psum"), before_layer("up_psum", l) + n + 1)
                        act.activation(q_tm[:, t, h * 384:h * 384 + 384], ps[:, 4 + n % 4, 0:384], ACT.Copy)\
                           .then_inc(sem("up_taken"), 1)
                act.wait_ge(sem("msg_ready"), before_layer("msg_ready", l) + 1)
                act.activation(ssg[:, :, :], ssg[:, :, :], ACT.Sqrt).then_inc(sem("rmsg_ready"), 1)
                for t in range(NT):
                    for h in range(2):
                        n += 1
                        act.wait_ge(sem("up_psum"), before_layer("up_psum", l) + n + 1)
                        src = ps[:, 4 + n % 4, :].rearrange("p (h c) -> p h c", h=4)
                        act.activation(k_tm[:, t, :].rearrange("p (h c) -> p h c", h=HM)[:, 4 * h:4 * h + 4, 0:NOPE],
                                       src[:, :, 0:NOPE], ACT.Copy)
                        act.activation(v_mla[:, t, h * 256:h * 256 + 256].rearrange("p (h c) -> p h c", h=4),
                                       src[:, :, NOPE:NOPE + VD], ACT.Copy).then_inc(sem("up_taken"), 1)
                for m in range(HG + HKV):
                    act.wait_ge(sem("gT_psum"), before_layer("gT_psum", l) + m + 1)
                    if m < HG:
                        act.activation(qgT[0:HD, m, tq[0] * P:TOK], ps[0:HD, m % 4, tq[0] * P:TOK], ACT.Copy,
                                       scale=GQA_SCALE).then_inc(sem("gT_taken"), 1)
                    else:
                        act.activation(kgT[0:HD, m - HG, :], ps[0:HD, m % 4, :], ACT.Copy).then_inc(sem("gT_taken"), 1)
                for h in range(HM):
                    act.wait_ge(sem("qkT_psum"), before_layer("qkT_psum", l) + 2 * h + 1)
                    act.activation(qT[0:DK, h, tq[0] * P:TOK], ps[0:DK, (2 * h) % 4, tq[0] * P:TOK], ACT.Copy,
                                   scale=MLA_SCALE).then_inc(sem("qT_taken"), 1)
                n_units = len(tq) * (HM + HG)
                for i in range(n_units):
                    qi = i // (HM + HG)
                    nk = CTX if tq[qi] < CTX // P else TOK
                    act.wait_ge(sem("max_ready"), before_layer("max_ready", l) + i + 1)
                    if i >= 2:
                        act.wait_ge(sem("pT_psum"), before_layer("pT_psum", l) + i - 1)
                    act.activation(probs[:, i % 2, 0:nk], ps[:, i % 3, 0:nk], ACT.Exp, bias=nmax[:, i % 4:i % 4 + 1],
                                   accum_out=rsum[:, i % 4:i % 4 + 1]).then_inc(sem("p_ready"), 1)
                    for qi in range(len(tq)):
                        if i == min((qi + 1) * (HM + HG) + 3, n_units - 1 if qi == len(tq) - 1 else n_units):
                            for half in range(2):
                                act.wait_ge(sem("oT_psum"), before_layer("oT_psum", l) + 2 * qi + half + 1)
                                act.activation(oT[:, 4 * half:4 * half + 4, tk(tq[qi])],
                                               ps[:, 7, :].rearrange("p (k t) -> p k t", k=4), ACT.Copy)\
                                   .then_inc(sem("oT_ready"), 1)
                def gate_hi(j, m):
                    i, w, w_hi, _ = gate_weights(l, j, m)
                    act.wait_ge(loaded[i % RING], load_count[i])
                    act.activation(w_hi, w, ACT.Copy).then_inc(sem("gw_hi_ready"), 1)

                act.wait_ge(sem("oT_psum"), before_layer("oT_psum", l) + 2 * len(tq))
                gate_hi(0, 0)
                for k in range(KD):
                    act.activation(gh_hi[:, k, tq[0] * P:TOK], hT[:, k, tq[0] * P:TOK], ACT.Copy)\
                       .then_inc(sem("gh_hi_ready"), 1)
                gate_hi(0, 1)
                for j in range(KD):
                    act.wait_ge(sem("mg_psum"), before_layer("mg_psum", l) + j + 1)
                    if j + 1 < KD:
                        gate_hi(j + 1, 0)
                        gate_hi(j + 1, 1)
                    if j >= 2:
                        act.wait_ge(sem("mT_ready"), before_layer("mT_ready", l) + j - 1)
                    for m in range(2):
                        ins = act.activation(sig[:, 2 * (j % 2) + m, 0:nq], ps[:, 4 * (j % 2) + 2 + m, 0:nq], ACT.Sigmoid)
                    ins.then_inc(sem("sig_ready"), 1)
                rows(l, 4, 0, "g1", lambda b: gate_row[:, b // 2, (b % 2) * 512:(b % 2) * 512 + 512])
                act.wait_ge(sem("x1_added"), before_layer("x1_added", l) + 4 * len(tq))
                squares(l, 2, tq)
                act.wait_ge(sem("mod_ready"), ADA_PARTS * l + 3)
                modulate(l, 2, tq, A2, 24)
                if l == DEPTH - 1:
                    act.activation(xn_parts[:, 0, :, :], xn[:, 2:4, :], ACT.Copy).then_inc(sem("xn_hi_ready"), 1)
                rows(l, 4, 4, "g2", lambda b: gate_row[:, b // 2, (b % 2) * 512:(b % 2) * 512 + 512])
                if l == 0:
                    def weights_hi(n):
                        i, w, w_hi, _ = ff_weights(n)
                        act.wait_ge(loaded[i % RING], load_count[i])
                        if n in (1, 2):
                            act.wait_ge(sem("h_split"), KD)
                        act.activation(w_hi, w, ACT.Copy).then_inc(sem("w_hi_ready"), 1)

                    act.wait_ge(sem("ht_psum2"), KD)
                    weights_hi(0)
                    for k in range(KD):
                        act.wait_ge(sem(f"ht_taken2_{k % 2}"), k // 2 + 1)
                        act.activation(hT_hi[:, k, :], hT[:, k, :], ACT.Copy).then_inc(sem("h_hi_ready"), 1)
                    weights_hi(1)
                    weights_hi(2)
                    for f in range(FT):
                        act.wait_ge(sem("ff_psum"), 2 * f + 1)
                        if f >= 2:
                            act.wait_ge(sem("gT_ready"), f - 1)
                        act.activation(silu_t[:, f % 2, :], ps[:, 2 * (f % 2), :], ACT.Silu).then_inc(sem("silu_ready"), 1)
                        for m in range(2):
                            if 2 * f + m + 3 < 2 * FT:
                                act.wait_ge(sem("ff_psum"), 2 * f + m + 1)
                                weights_hi(2 * f + m + 3)
                    act.wait_ge(sem("ff_psum"), 2 * FT)
                    for f in range(FT):
                        if f >= 2:
                            act.wait_ge(sem("dn_used"), f - 1)
                        i, w = dn_weights(f)
                        act.wait_ge(loaded[i % RING], load_count[i])
                        act.activation(dn_w[:, f % 2, 0, :], w, ACT.Copy).then_inc(sem("dn_hi_ready"), 1)
                        act.wait_ge(sem("gT_ready"), f + 1)
                        act.activation(dn_g[:, f % 2, 0, :], gT[:, f, :], ACT.Copy).then_inc(sem("dn_hi_ready"), 1)

            act.wait_ge(sem("lgm_ready"), 1)
            act.activation(ex[:, :, :], ex[:, :, :], ACT.Exp).then_inc(sem("ex_ready"), 1)

            act.wait_ge(sem("mod_ready"), 2 * ADA_PARTS)
            for k in range(0, KD, 2):
                act.wait_ge(sem("hAll_psum"), k + 1)
                act.activation(hTe[:, k, :], ps[:, 4 + k % 4, 0:LAT], ACT.Identity, scale=A2[:, 1, k, 1:2],
                               bias=mod[:, 1, 24 + k, 1:2])
                act.activation(hAll[:, k, 0:2 * LAT], ps[:, 4 + k % 4, :], ACT.Identity, scale=A2[:, 1, k, 1:2],
                               bias=mod[:, 1, 24 + k, 1:2]).then_inc(sem("hAll_a"), 1)

            act.wait_ge(sem("hAll_v"), KD // 2)
            act.activation(silu_junk[:, 0:1], nmax[:, 0:1], ACT.Silu).then_inc(sem("silu_table"), 1)
            act.wait_ge(sem("silu_table"), 1)

            def expert_groups(e, gr):
                inc = gr.inc
                if gr.split:
                    act.wait_ge(sem("hTe_ready"), e + 1)
                    act.activation(he_parts[:, 0, :, :], hTe[:, :, 0:P], ACT.Copy).then_inc(sem("e_hi_ready"), 1)
                else:
                    act.activation(nmax[:, 0:1], rsum[:, 0:1], ACT.Copy).then_inc(sem("e_hi_ready"), HI_EXPERT)
                with act.Fori(0, STEPS) as s:
                    it = act.snap(e * STEPS + s)

                    def slab_hi(j):
                        slot = (n_slabs + j) % RING
                        act.wait_ge(loaded[slot], it * 16 + (tally[slot] + 16))
                        act.wait_ge(sem("e_parts_used"), it * RING + (j + 1))
                        act.activation(e_parts[:, j % 3, 0, :], ring[slot][:, 0:2048], ACT.Copy)\
                           .then_inc(sem("e_hi_ready"), 1)

                    def gate(g):
                        act.wait_ge(sem("upe_psum"), it * COUNT + inc * (g + 1))
                        if gr.widths[g] == P:
                            act.activation(h_w[:, :], ps[:, 0, :], ACT.Silu).then_inc(sem("silu_e_ready"), inc)
                        else:
                            n = gr.widths[g] * STEP_F // P
                            act.activation(silu_e(g)[:, 0:n], ps[:, UP_BANK[g], 0:n], ACT.Silu)\
                               .then_inc(sem("silu_e_ready"), inc)

                    if gr.split:
                        act.activation(silu_junk[:, 1:2], silu_junk[:, 0:1], ACT.Silu).then_inc(sem("silu_table"), 1)
                        for j in range(5):
                            slab_hi(j)
                    gate(0)
                    if gr.split:
                        slab_hi(5)
                    for g in range(gr.n):
                        if g + 1 < gr.n:
                            gate(g + 1)
                        act.wait_ge(sem("gTe_psum"), it * COUNT + inc * (g + 1))
                        width = gr.widths[g]
                        into = gTe_parts[:, 0, :, :] if width == P else gTe(g)[:, :, 0:width]
                        act.activation(into, ps[:, TURN_BANK[g], 0:4 * width].rearrange("p (i s) -> p i s", i=4),
                                       ACT.Copy).then_inc(sem("gTe_ready"), inc)

            with act.Fori(0, NE) as e:
                count = act.value_load(cnt[0:1, bass.ds(e, 1)], min_val=0, max_val=LAT)
                by_count(act, count, lambda gr: expert_groups(e, gr))
                act.wait_ge(sem("y_psum"), e + 1)
                for g in (0, 1):
                    act.activation(y[:, g, :], ps[:, 2 + g, :], ACT.Copy).then_inc(sem("y_ready_a"), 1)
                act.wait_ge(sem("CT_psum"), e * 2 + 1)
                act.activation(CT[:, 0:2, :], ps[:, 0, :].rearrange("p (g t) -> p g t", g=2), ACT.Copy)\
                   .then_inc(sem("y_ready_a"), 1)
            rows(0, 2, 1, "fin", lambda b: fin_row[:, b * 512:b * 512 + 512])
            for t in range(2):
                act.wait_ge(sem("xf_ready"), t + 1)
                act.activation(xn[:, t, :].rearrange("p (a b) -> p a b", a=2), x_res[:, 2 + t, :].rearrange("p (a b) -> p a b", a=2),
                               ACT.Square, accum_out=ss[:, t:t + 1]).then_inc(sem("ssf_ready"), 1)
            act.wait_ge(sem("msf_ready"), 1)
            act.activation(rs[:, 0:2], ss[:, 0:2], ACT.Sqrt).then_inc(sem("rmsf_ready"), 1)

        @block.vector
        def _(dve):
            steps = [0]

            def then(ins):
                steps[0] += 1
                ins.then_inc(sem("dve_step"), 1)
                dve.wait_ge(sem("dve_step"), steps[0])

            def bc(ap, shape):
                return ap.to_broadcast(shape)

            def norm(l, which, tiles):
                n = len(tiles)
                dve.wait_ge(sem(f"ss_ready{which}"), before_layer(f"ss_ready{which}", l) + n)
                dve.tensor_scalar(ss[:, 0:n], ss[:, 0:n], 1.0 / D, EPS, ALU.mult, ALU.add)\
                   .then_inc(sem(f"ms_ready{which}"), 1)
                dve.wait_ge(sem(f"rms_ready{which}"), before_layer(f"rms_ready{which}", l) + 1)
                then(dve.reciprocal(rs[:, 0:n], rs[:, 0:n]))
                for i, t in enumerate(tiles):
                    dve.tensor_scalar(xn[:, t, :], x_res[:, t, :], rs[:, i:i + 1], None, ALU.mult)\
                       .then_inc(sem(f"xn_ready{which}"), 1)

            def ada(l, part, bank):
                n = ADA_PARTS * l + part
                dve.wait_ge(sem("ada_psum"), n + 1)
                if n:
                    dve.wait_ge(sem("adaT_psum"), n)
                dve.tensor_copy(ada_rows[:, :], ps[:, 7, :]).then_inc(sem("rows_ready"), 1)
                dve.wait_ge(sem("adaT_psum"), n + 1)
                t0 = 16 * part
                into = mod[:, l, t0:t0 + 16, :].rearrange("p (j i) c -> p i j c", j=4)
                src = ps[:, bank, :].rearrange("p (i j r) -> p i j r", i=4, j=4)[:, :, :, 0:2]
                bias = vec[:, l * V_L + t0:l * V_L + t0 + 16].rearrange("p (j i) -> p i j", j=4)
                last = dve.tensor_tensor(into, src, bc(bias.unsqueeze(3), [P, 4, 4, 2]), ALU.add)
                if part != 1:
                    then(last)
                    A, at, g = (A1, 8, 48) if part == 0 else (A2, 32, 56)
                    last = dve.scalar_tensor_tensor(A[:, l, :, :], mod[:, l, at:at + KD, :], 1.0,
                                                    bc(vec[:, l * V_L + g:l * V_L + g + KD].unsqueeze(2), [P, KD, 2]),
                                                    ALU.add, ALU.mult)
                last.then_inc(sem("mod_ready"), 1)

            def modulate(l, which, tiles, A, sh):
                dve.wait_ge(sem("mod_ready"), ADA_PARTS * l + (1 if which == 1 else 3))
                for k in range(1, KD, 2):
                    dve.wait_ge(sem(f"ht_psum{which}"), before_layer(f"ht_psum{which}", l) + k + 1)
                    for c in ((0, 1) if 0 in tiles else (1,)):
                        ins = dve.tensor_scalar(hT[:, k, c * CTX:(c + 1) * CTX], ps[:, k % 4, c * CTX:(c + 1) * CTX],
                                                A[:, l, k, c:c + 1], mod[:, l, sh + k, c:c + 1], ALU.mult, ALU.add)
                    ins.then_inc(sem(f"ht_taken{which}_1"), 1)

            def rotate(xs, t, heads, dim, stride, tab, ta, tb):
                f = dim // 4
                flat = lambda m: m[:, 0:heads * dim].rearrange("p (h d) -> p h d", h=heads)
                halves = lambda m: m.rearrange("p h (a b f) -> p h a b f", a=2, b=2)
                cos = rope[:, t, tab:tab + dim]
                sin = rope[:, t, tab + dim:tab + 2 * dim].rearrange("p (a b f) -> p a b f", a=2, b=2)
                dve.tensor_tensor(flat(ta), xs, bc(cos.unsqueeze(1), [P, heads, dim]), ALU.mult)
                for b in range(2):
                    for ax in range(2):
                        ins = dve.tensor_tensor(halves(flat(tb))[:, :, ax, b, :], halves(xs)[:, :, ax, 1 - b, :],
                                                bc(sin[:, ax, b, :].unsqueeze(1), [P, heads, f]), ALU.mult)
                then(ins)
                return dve.tensor_tensor(xs, flat(ta), flat(tb), ALU.add)

            dve.wait_ge(sem("vec_psum"), 1)
            dve.tensor_copy(vec[:, 0:V_ROWS], ps[:, 0, 0:V_ROWS]).then_inc(sem("vec_done"), 1)
            dve.wait_ge(sem("gq_psum"), 1)
            dve.tensor_copy(gq_row[:, :, :, :], ps[:, 1, 0:4 * HD].rearrange("p (l m d) -> p l m d", l=DEPTH, m=2))\
               .then_inc(sem("gq_ready"), 1)
            dve.wait_ge(sem("ctx_loaded"), 16)
            dve.wait_ge(sem("x_loaded"), 16)
            dve.wait_ge(sem("rope_loaded"), 16)

            for l in range(DEPTH):
                tq = tiles_q(l)
                nq = len(tq) * P
                qt = slice(tq[0], NT)
                norm(l, 1, range(NT))
                if l == 0:
                    ada(0, 0, 3)
                modulate(l, 1, range(NT), A1, 0)

                if l == 0:
                    ada(0, 1, 3)
                dve.wait_ge(sem("ssc_ready"), before_layer("ssc_ready", l) + len(tq) + NT)
                then(dve.tensor_scalar(ss[:, tq[0]:4], ss[:, tq[0]:4], 1.0 / QL, EPS, ALU.mult, ALU.add))
                dve.tensor_scalar(ss[:, 4:8], ss[:, 4:8], 1.0 / KVL, EPS, ALU.mult, ALU.add).then_inc(sem("msc_ready"), 1)
                dve.wait_ge(sem("rmsc_ready"), before_layer("rmsc_ready", l) + 1)
                then(dve.reciprocal(rs[:, tq[0]:8], rs[:, tq[0]:8]))
                for t in tq:
                    dve.tensor_scalar(z[:, t, C_Q:C_Q + QL], z[:, t, C_Q:C_Q + QL], rs[:, t:t + 1], None, ALU.mult)
                for t in range(NT):
                    ins = dve.tensor_scalar(z[:, t, C_KV:C_KV + KVL], z[:, t, C_KV:C_KV + KVL], rs[:, 4 + t:5 + t], None, ALU.mult)
                ins.then_inc(sem("c_ready"), 1)
                z_g = lambda t, m0, m1: z[:, t, C_QG + m0 * HD:C_QG + m1 * HD]
                if l == 0:
                    ada(0, 2, 3)
                for j in range(5):
                    g = (V_QN + 3 * l + j) if j < 3 else (V_KVN + 2 * l + j - 3)
                    lo = tq[0] * P if j < 3 else 0
                    dve.wait_ge(sem("cT_psum"), before_layer("cT_psum", l) + j + 1)
                    dve.tensor_scalar(cT[:, j, lo:TOK], ps[:, j % 4, lo:TOK], colv(g), None, ALU.mult)\
                       .then_inc(sem("cT_ready"), 1)
                dve.wait_ge(sem("z_ready"), before_layer("z_ready", l) + len(in_tiles(l)))
                heads = lambda t: (0 if t in tq else HG, HG + HKV)
                if l > 0:
                    then(dve.memset(ssg[:, 0:2, 0:HG], HD))
                for t in range(NT):
                    m0, m1 = heads(t)
                    n = (m1 - m0) * HD
                    then(dve.tensor_tensor(rope_a[:, 0:n], z_g(t, m0, m1), z_g(t, m0, m1), ALU.mult))
                    then(dve.tensor_reduce(ssg[:, t, m0:m1], rope_a[:, 0:n].rearrange("p (h d) -> p h d", d=HD), AX.X, ALU.add))
                dve.tensor_scalar(ssg[:, :, :], ssg[:, :, :], 1.0 / HD, EPS, ALU.mult, ALU.add)\
                   .then_inc(sem("msg_ready"), 1)
                dve.wait_ge(sem("rmsg_ready"), before_layer("rmsg_ready", l) + 1)
                then(dve.reciprocal(ssg[:, :, :], ssg[:, :, :]))
                for t in range(NT):
                    m0, m1 = heads(t)
                    xs = z_g(t, m0, m1).rearrange("p (h d) -> p h d", d=HD)
                    then(dve.tensor_tensor(xs, xs, bc(ssg[:, t, m0:m1].unsqueeze(2), [P, m1 - m0, HD]), ALU.mult))
                    if m0 == 0:
                        xq = z_g(t, 0, HG).rearrange("p (h d) -> p h d", d=HD)
                        dve.tensor_tensor(xq, xq, bc(gq_row[:, l, 0, :].unsqueeze(1), [P, HG, HD]), ALU.mult)
                    xk = z_g(t, HG, HG + HKV).rearrange("p (h d) -> p h d", d=HD)
                    ins = dve.tensor_tensor(xk, xk, bc(gq_row[:, l, 1, :].unsqueeze(1), [P, HKV, HD]), ALU.mult)
                    if t >= 2:
                        then(ins)
                        ins = rotate(xs, t - 2, m1 - m0, HD, HD, 0, rope_a, rope_b)
                        if t < NT - 1:
                            then(ins)
                ins.then_inc(sem("g_ready"), 1)
                dve.wait_ge(sem("g_ready"), before_layer("g_ready", l) + 1)
                for t in range(NT):
                    xk = z[:, t, C_PE:C_PE + ROPE].rearrange("p (h d) -> p h d", h=1)
                    if t >= 2:
                        then(rotate(xk, t - 2, 1, ROPE, ROPE, 128, rope_a, rope_b))
                    dve.tensor_copy(k_tm[:, t, :].rearrange("p (h c) -> p h c", h=HM)[:, :, NOPE:DK],
                                    bc(z[:, t, C_PE:C_PE + ROPE].unsqueeze(1), [P, HM, ROPE]))
                for t in (2, 3):
                    dve.wait_ge(sem("up_taken"), before_layer("up_taken", l) + 2 * (t - tq[0] + 1))
                    xq = q_tm[:, t, :].rearrange("p (h c) -> p h c", h=HM)[:, :, NOPE:DK]
                    ins = rotate(xq, t - 2, HM, ROPE, DK, 128, rope_a, rope_b)
                    if t == 2:
                        then(ins)
                ins.then_inc(sem("qk_ready"), 1)
                for h in range(HM):
                    dve.wait_ge(sem("qkT_psum"), before_layer("qkT_psum", l) + 2 * h + 2)
                    dve.tensor_copy(kT[0:DK, h, :], ps[0:DK, (2 * h + 1) % 4, :]).then_inc(sem("kT_taken"), 1)

                n_units = len(tq) * (HM + HG)
                keys = lambda i: CTX if tq[i // (HM + HG)] < CTX // P else TOK
                for i in range(n_units + 3):
                    if i < n_units:
                        dve.wait_ge(sem("s_psum"), before_layer("s_psum", l) + i + 1)
                        dve.tensor_reduce(nmax[:, i % 4:i % 4 + 1], ps[:, i % 3, 0:keys(i)], AX.X, ALU.max, negate=True)\
                           .then_inc(sem("max_ready"), 1)
                    j = i - 2
                    if 0 <= j < n_units:
                        dve.wait_ge(sem("pT_psum"), before_layer("pT_psum", l) + j + 1)
                        if j >= 2:
                            dve.wait_ge(sem("o_psum"), before_layer("o_psum", l) + j - 1)
                        dve.tensor_copy(probsT[:, j % 2, 0:keys(j)], ps[:, 3 + j % 2, 0:keys(j)]).then_inc(sem("pT_ready"), 1)
                        dve.reciprocal(rinv[:, j % 4:j % 4 + 1], rsum[:, j % 4:j % 4 + 1]).then_inc(sem("rinv_ready"), 1)
                    j = i - 3
                    if 0 <= j < n_units:
                        qi, h = divmod(j, HM + HG)
                        dve.wait_ge(sem("o_psum"), before_layer("o_psum", l) + j + 1)
                        dve.wait_ge(sem("rinv_ready"), before_layer("rinv_ready", l) + j + 1)
                        if h == 0 and qi >= 2:
                            dve.wait_ge(sem("oT_psum"), before_layer("oT_psum", l) + 2 * (qi - 1))
                        dve.tensor_scalar(o_tm[:, qi % 2, h * VD:(h + 1) * VD], ps[:, 5 + j % 2, 0:VD],
                                          rinv[:, j % 4:j % 4 + 1], None, ALU.mult).then_inc(sem("o_ready"), 1)
                def gate_lo(j, m):
                    _, w, w_hi, w_lo = gate_weights(l, j, m)
                    dve.wait_ge(sem("gw_hi_ready"), before_layer("gw_hi_ready", l) + 2 * j + m + 1)
                    dve.tensor_tensor(w_lo, w, w_hi, ALU.subtract).then_inc(sem("gw_split"), 1)

                gate_lo(0, 0)
                for k in range(KD):
                    dve.wait_ge(sem("gh_hi_ready"), before_layer("gh_hi_ready", l) + k + 1)
                    dve.tensor_tensor(gh_lo[:, k, tq[0] * P:TOK], hT[:, k, tq[0] * P:TOK], gh_hi[:, k, tq[0] * P:TOK],
                                      ALU.subtract).then_inc(sem("gh_split"), 1)
                gate_lo(0, 1)
                for j in range(KD):
                    if j + 1 < KD:
                        gate_lo(j + 1, 0)
                        gate_lo(j + 1, 1)
                    dve.wait_ge(sem("sig_ready"), before_layer("sig_ready", l) + j + 1)
                    dve.wait_ge(sem("mT_ready"), before_layer("mT_ready", l) + j)
                    for m in range(2):
                        ins = dve.tensor_tensor(mg_t[:, m, 0:nq], sig[:, 2 * (j % 2) + m, 0:nq], ps[:, 4 * (j % 2) + m, 0:nq], ALU.mult)
                    then(ins)
                    dve.tensor_tensor(mT[:, j, tq[0] * P:TOK], mg_t[:, 0, 0:nq], mg_t[:, 1, 0:nq], ALU.add)\
                       .then_inc(sem("mT_ready"), 1)
                dve.wait_ge(sem("g1_ready"), before_layer("g1_ready", l) + 4)
                n = -1
                for s in range(4):
                    for t in tq:
                        n += 1
                        dve.wait_ge(sem("out_psum"), before_layer("out_psum", l) + n + 1)
                        then(dve.tensor_tensor(add_t[:, 0:256], gate_row[:, t // 2, s * 256:s * 256 + 256],
                                               ps[:, 4 + n % 4, 0:256], ALU.mult))
                        dve.tensor_tensor(x_res[:, t, s * 256:s * 256 + 256], x_res[:, t, s * 256:s * 256 + 256],
                                          add_t[:, 0:256], ALU.add).then_inc(sem("x1_added"), 1)
                        dve.wait_ge(sem("x1_added"), before_layer("x1_added", l) + n + 1)
                norm(l, 2, tq)
                modulate(l, 2, tq, A2, 24)
                if l == 0:
                    def weights_lo(n):
                        _, w, w_hi, w_lo = ff_weights(n)
                        dve.wait_ge(sem("w_hi_ready"), n + 1)
                        dve.tensor_tensor(w_lo, w, w_hi, ALU.subtract).then_inc(sem("w_split"), 1)

                    weights_lo(0)
                    for k in range(KD):
                        dve.wait_ge(sem("h_hi_ready"), k + 1)
                        dve.tensor_tensor(hT_lo[:, k, :], hT[:, k, :], hT_hi[:, k, :], ALU.subtract)\
                           .then_inc(sem("h_split"), 1)
                    weights_lo(1)
                    weights_lo(2)
                    for f in range(FT):
                        if 2 * f + 3 < 2 * FT:
                            weights_lo(2 * f + 3)
                        dve.wait_ge(sem("silu_ready"), f + 1)
                        dve.wait_ge(sem("ff_psum"), 2 * f + 2)
                        dve.tensor_tensor(gT[:, f, :], silu_t[:, f % 2, :], ps[:, 2 * (f % 2) + 1, :], ALU.mult)\
                           .then_inc(sem("gT_ready"), 1)
                        if 2 * f + 4 < 2 * FT:
                            weights_lo(2 * f + 4)
                        if f % 2:
                            for part, k in ada_ffn(f // 2):
                                if k == KD - 1:
                                    ada(1, part, 6)
                    for f in range(FT):
                        _, w = dn_weights(f)
                        dve.wait_ge(sem("dn_hi_ready"), 2 * f + 1)
                        dve.tensor_tensor(dn_w[:, f % 2, 1, :], w, dn_w[:, f % 2, 0, :], ALU.subtract)\
                           .then_inc(sem("dn_split"), 1)
                        dve.wait_ge(sem("dn_hi_ready"), 2 * f + 2)
                        dve.tensor_tensor(dn_g[:, f % 2, 1, :], gT[:, f, :], dn_g[:, f % 2, 0, :], ALU.subtract)\
                           .then_inc(sem("dn_split"), 1)
                    for t in range(NT):
                        for h in range(2):
                            dve.wait_ge(sem("dn_psum"), 2 * t + h + 1)
                            then(dve.tensor_tensor(add_t[:, :], gate_row[:, t // 2, h * 512:h * 512 + 512],
                                                   ps[:, 2 * t + h, :], ALU.mult))
                            dve.tensor_tensor(x_res[:, t, h * 512:h * 512 + 512], x_res[:, t, h * 512:h * 512 + 512],
                                              add_t[:, :], ALU.add).then_inc(sem("dn_added"), 1)
                            dve.wait_ge(sem("dn_added"), 2 * t + h + 1)

            dve.wait_ge(sem("xn_hi_ready"), 1)
            dve.tensor_tensor(xn_parts[:, 1, :, :], xn[:, 2:4, :], xn_parts[:, 0, :, :], ALU.subtract)\
               .then_inc(sem("xn_split"), 1)
            dve.wait_ge(sem("lg_psum"), 1)
            then(dve.tensor_copy(lg[:, :, :], ps[:, 0, 0:2 * NE].rearrange("p (t e) -> p t e", t=2)))
            then(dve.tensor_reduce(v1[:, :], lg[:, :, :], AX.X, ALU.max))
            dve.tensor_tensor(ex[:, :, :], lg[:, :, :], bc(v1[:, :].unsqueeze(2), [P, 2, NE]), ALU.subtract)\
               .then_inc(sem("lgm_ready"), 1)
            for t in range(2):
                a3 = cmp_a[:, t, :].rearrange("p (e j) -> p e j", e=NE)
                b3 = cmp_b[:, t, :].rearrange("p (e j) -> p e j", e=NE)
                other = bc(lg[:, t, :].unsqueeze(1), [P, NE, NE])
                own = bc(lg[:, t, :].unsqueeze(2), [P, NE, NE])
                dve.tensor_tensor(a3, other, own, ALU.is_gt)
                then(dve.tensor_tensor(b3, other, own, ALU.is_equal))
                then(dve.tensor_tensor(b3, b3, lower[:, :, :], ALU.mult))
                then(dve.tensor_tensor(a3, a3, b3, ALU.add))
                then(dve.tensor_reduce(rank[:, t, :], a3, AX.X, ALU.add))
            dve.tensor_scalar(sel[:, :, 0:NE], rank[:, :, :], 1.5, None, ALU.is_lt).then_inc(sem("sel_ready"), 1)
            dve.wait_ge(sem("sel_ready"), 1)
            dve.wait_ge(sem("pos_psum"), 1)
            dve.tensor_copy(cnt[:, 0:NE], ps[:, 3, 2 * NE:3 * NE])
            dve.tensor_copy(cntf[:, :], ps[:, 3, 2 * NE:3 * NE])
            then(dve.tensor_copy(pos[:, :, :], ps[:, 3, 0:2 * NE].rearrange("p (t e) -> p t e", t=2)))
            for g in range(MAXG):
                dve.tensor_scalar(pos_g[:, g, :, :], pos[:, :, :], float(-g * G), None, ALU.add)
            a3 = cmp_a[:, 0, :].rearrange("p (e j) -> p e j", e=NE)
            then(dve.tensor_tensor(a3, bc(cntf[:, :].unsqueeze(1), [P, NE, NE]), lower[:, :, :], ALU.mult))
            then(dve.tensor_reduce(offf[:, :], a3, AX.X, ALU.add))
            dve.tensor_copy(first[:, 0:NE], offf[:, :]).then_inc(sem("first_ready"), 1)
            for t in range(2):
                slot = cmp_b[:, t, 32:32 + NE]
                then(dve.tensor_tensor(slot, pos[:, t, :], offf[:, :], ALU.add))
                for r in range(2):
                    then(dve.scalar_tensor_tensor(cmp_b[:, t, 8 * r:8 * r + NE], rank[:, t, :], float(r), slot,
                                                  ALU.is_equal, ALU.mult))
                    then(dve.tensor_reduce(slot12[:, t, r:r + 1], cmp_b[:, t, 8 * r:8 * r + NE], AX.X, ALU.add))
                then(dve.tensor_scalar(S_all[:, t, :], iota[:, :], slot12[:, t, 0:1], None, ALU.is_equal))
                ins = dve.scalar_tensor_tensor(S_all[:, t, :], iota[:, :], slot12[:, t, 1:2], S_all[:, t, :],
                                               ALU.is_equal, ALU.add)
                if t == 0:
                    then(ins)
            ins.then_inc(sem("S_ready"), 1)
            dve.memset(acc[:, :, :], 0.0)
            then(dve.memset(C_oh[:, :, :], 0.0))
            for k in range(1, KD, 2):
                dve.wait_ge(sem("hAll_psum"), k + 1)
                dve.tensor_scalar(hTe[:, k, :], ps[:, 4 + k % 4, 0:LAT], A2[:, 1, k, 1:2], mod[:, 1, 24 + k, 1:2],
                                  ALU.mult, ALU.add)
                dve.tensor_scalar(hAll[:, k, 0:2 * LAT], ps[:, 4 + k % 4, :], A2[:, 1, k, 1:2], mod[:, 1, 24 + k, 1:2],
                                  ALU.mult, ALU.add).then_inc(sem("hAll_v"), 1)

            def hidden(e, gr):
                inc = gr.inc
                for t in range(2):
                    for g, width in enumerate(gr.widths):
                        slots = {P: iota[:, 0:P], G: iota_g[:, :], H: iota_h[:, :]}[width]
                        ins = dve.tensor_scalar(C_oh[:, t, tk(g)], slots, pos_g[:, gr.starts[g] // G, t, bass.ds(e, 1)],
                                                wgt[:, t, bass.ds(e, 1)], ALU.is_equal, ALU.mult)
                    if t == 0 and not gr.split:
                        ins.then_inc(sem("e_split"), LO_EXPERT)
                ins.then_inc(sem("C_ready"), 1)
                if gr.split:
                    dve.wait_ge(sem("e_hi_ready"), e * HI_EXPERT + 1)
                    dve.tensor_tensor(he_parts[:, 1, :, :], hTe[:, :, 0:P], he_parts[:, 0, :, :], ALU.subtract)\
                       .then_inc(sem("e_split"), 1)
                with dve.Fori(0, STEPS) as s:
                    it = dve.snap(e * STEPS + s)
                    hi_base = dve.snap(e * HI_EXPERT + s * HI_STEP)

                    def slab_lo(j):
                        dve.wait_ge(sem("e_hi_ready"), hi_base + (1 + j + 1))
                        dve.tensor_tensor(e_parts[:, j % 3, 1, :], ring[(n_slabs + j) % RING][:, 0:2048],
                                          e_parts[:, j % 3, 0, :], ALU.subtract).then_inc(sem("e_split"), 1)

                    if gr.split:
                        for j in range(5):
                            slab_lo(j)
                    for g in range(gr.n):
                        dve.wait_ge(sem("silu_e_ready"), it * COUNT + inc * (g + 1))
                        if gr.widths[g] == P:
                            dve.tensor_tensor(h_w[:, :], h_w[:, :], ps[:, 1, :], ALU.mult).then_inc(sem("he_ready"), inc)
                            dve.wait_ge(sem("gTe_ready"), it * COUNT + inc)
                            dve.tensor_tensor(gTe_parts[:, 1, :, :], ps[:, TURN_BANK[g], :].rearrange("p (i s) -> p i s", i=4),
                                              gTe_parts[:, 0, :, :], ALU.subtract).then_inc(sem("e_split"), 1)
                            slab_lo(5)
                        else:
                            n = gr.widths[g] * STEP_F // P
                            dve.tensor_tensor(h_e(g)[:, 0:n], silu_e(g)[:, 0:n], ps[:, UP_BANK[g], n:2 * n], ALU.mult)\
                               .then_inc(sem("he_ready"), inc)

            dve.wait_ge(sem("ex_ready"), 1)
            then(dve.tensor_tensor(ex[:, :, :], ex[:, :, :], sel[:, :, 0:NE], ALU.mult))
            then(dve.tensor_reduce(den[:, :], ex[:, :, :], AX.X, ALU.add))
            then(dve.reciprocal(dinv[:, :], den[:, :]))
            then(dve.tensor_tensor(wgt[:, :, 0:NE], ex[:, :, :], bc(dinv[:, :].unsqueeze(2), [P, 2, NE]), ALU.mult))
            dve.wait_ge(sem("hAll_a"), KD // 2)
            with dve.Fori(0, NE) as e:
                count = dve.value_load(cnt[0:1, bass.ds(e, 1)], min_val=0, max_val=LAT)
                by_count(dve, count, lambda gr: hidden(e, gr))
                dve.wait_ge(sem("y_psum"), e + 1)
                for g in (2, 3):
                    dve.tensor_copy(y[:, g, :], ps[:, 2 + g, :]).then_inc(sem("y_ready_v"), 1)
                dve.wait_ge(sem("CT_psum"), e * 2 + 2)
                dve.tensor_copy(CT[:, 2:4, :], ps[:, 1, :].rearrange("p (g t) -> p g t", g=2)).then_inc(sem("y_ready_v"), 1)
                for t in range(2):
                    dve.wait_ge(sem("sc_psum"), e * 2 + t + 1)
                    for half in range(2):
                        part = acc[:, t, half * 512:half * 512 + 512]
                        dve.tensor_tensor(part, part, ps[:, (6, 0)[t] + half, :], ALU.add).then_inc(sem("acc_added"), 1)
                dve.wait_ge(sem("acc_added"), e * 4 + 4)
            dve.wait_ge(sem("acc_added"), 4 * NE)
            then(dve.tensor_tensor(acc[:, :, :], acc[:, :, :], bc(gate_row[:, 1, :].unsqueeze(1), [P, 2, D]), ALU.mult))
            for t in range(2):
                dve.tensor_tensor(x_res[:, 2 + t, :], x_res[:, 2 + t, :], acc[:, t, :], ALU.add).then_inc(sem("xf_ready"), 1)
            dve.wait_ge(sem("ssf_ready"), 2)
            dve.tensor_scalar(ss[:, 0:2], ss[:, 0:2], 1.0 / D, EPS, ALU.mult, ALU.add).then_inc(sem("msf_ready"), 1)
            dve.wait_ge(sem("rmsf_ready"), 1)
            then(dve.reciprocal(rs[:, 0:2], rs[:, 0:2]))
            dve.wait_ge(sem("fin_ready"), 2)
            dve.wait_ge(sem("xf_ready"), 2)
            for t in range(2):
                dve.scalar_tensor_tensor(out_t[:, t, :], x_res[:, 2 + t, :], rs[:, t:t + 1], fin_row[:, :],
                                         ALU.mult, ALU.mult).then_inc(sem("out_ready"), 1)


_WEIGHTS = ["w_ada", "w_in", "mla_w_qb", "mla_w_kvb", "w_o_mla", "w_o_gqa", "w_out", "dense_w1", "dense_w3", "dense_w2",
            "moe_router", "moe_w1", "moe_w3", "moe_w2"]


def rope_rows():
    t = np.arange(LAT)
    out = []
    for dim in (HD, ROPE):
        half = dim // 2
        inv = (np.float32(THETA) ** (-(np.arange(half // 2, dtype=np.float32) * np.float32(2.0)) / np.float32(half))).astype(np.float32)
        ang = [(p.astype(np.float32)[:, None] * inv).astype(np.float32) for p in (t // GRID_W, t % GRID_W)]
        out += [np.concatenate([np.cos(g) for a in ang for g in (a, a)], axis=1),
                np.concatenate([s * np.sin(a) for a in ang for s in (-1.0, 1.0)], axis=1)]
    return np.concatenate(out, axis=1).astype(np.float32)


def pack_vectors(i):
    wide = lambda v: np.reshape(v, (-1, P))
    half = lambda v: np.concatenate([np.reshape(v, (1, HD)), np.zeros((1, P - HD), np.float32)], axis=1)
    rows = [wide(i[n][l]) for l in range(DEPTH) for n in ("b_ada", "norm1_g", "norm2_g")]
    rows += [wide(i["c_ctx"]), wide(i["c"]), wide(i["final_norm_g"])]
    rows += [wide(i["mla_q_norm_g"]), wide(i["mla_kv_norm_g"])]
    rows += [half(i[n][l]) for n in ("gqa_q_norm_g", "gqa_k_norm_g") for l in range(DEPTH)]
    return np.ascontiguousarray(np.concatenate(rows, axis=0))


def kernel(**inputs):
    import concourse.bacc as _bacc
    from concourse.bass_utils import run_bass_kernel_spmd as _run

    nc = _bacc.Bacc("TRN2", target_bir_lowering=False, num_devices=1)
    host = {n: np.ascontiguousarray(v) for n, v in inputs.items()}
    given = {n: host[n] for n in ["x", "ctx"] + _WEIGHTS}
    given["vecs"] = pack_vectors(host)
    given["rope"] = rope_rows()
    aps, arrays = {}, {}
    for n, v in given.items():
        arrays[f"in_{n}"] = v
        aps[n] = nc.dram_tensor(f"in_{n}", v.shape, mybir.dt.from_np(v.dtype), kind="ExternalInput").ap()
    out = nc.dram_tensor("out", (1, LAT, D), F32, kind="ExternalOutput").ap()
    build(nc, aps, out)
    r = _run(nc, [arrays], core_ids=[0])
    return r.results[0]["out"]
```
